# Optimizing a Trainium2 kernel written in Bass

```python
import jax, jax.numpy as jnp
from jax import lax
import numpy as np

D_MODEL = 1024
BATCH = 1
SEQ = 256
DEPTH = 2

HEAD_DIM = 64
SB_HEADS = (3 * D_MODEL) // (8 * HEAD_DIM)
FOX_HEADS = (3 * D_MODEL) // (8 * HEAD_DIM)
SB_DIM = SB_HEADS * HEAD_DIM
FOX_DIM = FOX_HEADS * HEAD_DIM
POOL_WINDOWS = (2, 4, 8, 16)
POOL_DIM = D_MODEL // 4
POOL_GROUP = POOL_DIM // len(POOL_WINDOWS)
MIX_DIM = SB_DIM + FOX_DIM + POOL_DIM
SPLIT_POINTS = [SB_DIM, 2 * SB_DIM, 3 * SB_DIM,
                3 * SB_DIM + FOX_DIM, 3 * SB_DIM + 2 * FOX_DIM, 3 * SB_DIM + 3 * FOX_DIM,
                3 * SB_DIM + 3 * FOX_DIM + FOX_HEADS]
C_IN = 3 * SB_DIM + 3 * FOX_DIM + FOX_HEADS + POOL_DIM
Q_BLOCK = 128
MEM_LEN = 256
XA_HEADS = 4
XA_HEAD_DIM = D_MODEL // XA_HEADS
D_FF = ((8 * D_MODEL // 3 + 255) // 256) * 256
N_EXPERTS = 8
TOP_K = 2
MOE_BLOCK = 256
N_DENSE = (DEPTH + 1) // 2
N_MOE = DEPTH // 2
EPS = 1e-6

kernel_name = 'hymba_sb_fox_pool_moe_trunk'

def rmsnorm(x, g):
    xf = x.astype(jnp.float32)
    y = xf * lax.rsqrt(jnp.mean(xf * xf, axis=-1, keepdims=True) + EPS)
    return (y * g.astype(jnp.float32)).astype(x.dtype)

def _heads(t, n):
    b, s, _ = t.shape
    return t.reshape(b, s, n, HEAD_DIM).transpose(0, 2, 1, 3)

def _merge_blocks(o):
    nb, b, h, q, dh = o.shape
    return o.transpose(1, 0, 3, 2, 4).reshape(b, nb * q, h * dh)

def stick_breaking_attention(q, k, v):
    _, _, s_len, dh = q.shape
    scale = dh ** -0.5
    s_idx = jnp.arange(s_len)

    def block(i):
        t0 = i * Q_BLOCK
        qb = lax.dynamic_slice_in_dim(q, t0, Q_BLOCK, axis=2)
        z = jnp.einsum('bhqd,bhsd->bhqs', qb, k).astype(jnp.float32) * scale
        t_idx = t0 + jnp.arange(Q_BLOCK)
        mask = s_idx[None, :] < t_idx[:, None]
        log_beta = jax.nn.log_sigmoid(z)
        log_keep = jnp.where(mask, log_beta - z, 0.0)
        later = lax.cumsum(log_keep, axis=3, reverse=True) - log_keep
        w = jnp.where(mask, jnp.exp(log_beta + later), 0.0)
        return jnp.einsum('bhqs,bhsd->bhqd', w.astype(v.dtype), v)

    return _merge_blocks(lax.map(block, jnp.arange(s_len // Q_BLOCK)))

def forgetting_attention(q, k, v, log_f_cum):
    _, _, s_len, dh = q.shape
    scale = dh ** -0.5
    s_idx = jnp.arange(s_len)

    def block(i):
        t0 = i * Q_BLOCK
        qb = lax.dynamic_slice_in_dim(q, t0, Q_BLOCK, axis=2)
        cq = lax.dynamic_slice_in_dim(log_f_cum, t0, Q_BLOCK, axis=2)
        logits = (jnp.einsum('bhqd,bhsd->bhqs', qb, k).astype(jnp.float32) * scale
                  + cq[..., :, None] - log_f_cum[..., None, :])
        t_idx = t0 + jnp.arange(Q_BLOCK)
        mask = s_idx[None, :] <= t_idx[:, None]
        p = jax.nn.softmax(jnp.where(mask, logits, -jnp.inf), axis=-1)
        return jnp.einsum('bhqs,bhsd->bhqd', p.astype(v.dtype), v)

    return _merge_blocks(lax.map(block, jnp.arange(s_len // Q_BLOCK)))

def multiscale_pool(u, pool_w, pool_scale):
    _, s_len, _ = u.shape
    pos = jnp.arange(s_len)
    outs = []
    for g, win in enumerate(POOL_WINDOWS):
        ug = u[..., g * POOL_GROUP:(g + 1) * POOL_GROUP].astype(jnp.float32)
        cs = jnp.cumsum(ug, axis=1)
        cs_prev = jnp.pad(cs, ((0, 0), (win, 0), (0, 0)))[:, :s_len]
        count = jnp.minimum(pos + 1, win).astype(jnp.float32)[None, :, None]
        r = ((cs - cs_prev) / count - ug).astype(u.dtype)
        outs.append(r @ pool_w[g])
    return jnp.concatenate(outs, axis=-1) * pool_scale

def hybrid_mixer(hn, w_in, b_forget, pool_w, pool_scale, w_out):
    proj = hn @ w_in
    sq, sk, sv, fq, fk, fv, f_logit, u = jnp.split(proj, SPLIT_POINTS, axis=-1)
    sb = stick_breaking_attention(_heads(sq, SB_HEADS), _heads(sk, SB_HEADS), _heads(sv, SB_HEADS))
    log_f = jax.nn.log_sigmoid((f_logit + b_forget).astype(jnp.float32))
    log_f_cum = jnp.cumsum(log_f, axis=1).transpose(0, 2, 1)
    fox = forgetting_attention(_heads(fq, FOX_HEADS), _heads(fk, FOX_HEADS), _heads(fv, FOX_HEADS), log_f_cum)
    pool = multiscale_pool(u, pool_w, pool_scale)
    return jnp.concatenate([sb, fox, pool], axis=-1) @ w_out

def memory_cross_attention(hn, mn, wq, wkv, wo):
    b, s_len, _ = hn.shape
    m_len = mn.shape[1]
    q = (hn @ wq).reshape(b, s_len, XA_HEADS, XA_HEAD_DIM)
    k, v = jnp.split(mn @ wkv, 2, axis=-1)
    k = k.reshape(b, m_len, XA_HEADS, XA_HEAD_DIM)
    v = v.reshape(b, m_len, XA_HEADS, XA_HEAD_DIM)
    logits = jnp.einsum('bqhd,bmhd->bhqm', q, k).astype(jnp.float32) * (XA_HEAD_DIM ** -0.5)
    p = jax.nn.softmax(logits, axis=-1)
    o = jnp.einsum('bhqm,bmhd->bqhd', p.astype(v.dtype), v).reshape(b, s_len, D_MODEL)
    return o @ wo

def swiglu(h, w_gate, w_up, w_down):
    return (jax.nn.silu(h @ w_gate) * (h @ w_up)) @ w_down

def moe_swiglu(h, router_w, w_gate, w_up, w_down):
    b, s_len, d = h.shape
    xf = h.reshape(-1, d)
    n_tok = xf.shape[0]
    n_pairs = n_tok * TOP_K
    logits = (xf @ router_w).astype(jnp.float32)
    top_val, top_idx = lax.top_k(logits, TOP_K)
    gates = jax.nn.softmax(top_val, axis=-1)
    e_flat = top_idx.reshape(-1)
    tok_flat = jnp.repeat(jnp.arange(n_tok), TOP_K)
    g_flat = gates.reshape(-1)
    order = jnp.argsort(e_flat)
    e_s, tok_s, g_s = e_flat[order], tok_flat[order], g_flat[order]
    counts = jnp.bincount(e_flat, length=N_EXPERTS)
    padded = ((counts + MOE_BLOCK - 1) // MOE_BLOCK) * MOE_BLOCK
    start = jnp.cumsum(counts) - counts
    pend = jnp.cumsum(padded)
    pstart = pend - padded
    dest = pstart[e_s] + (jnp.arange(n_pairs) - start[e_s])
    n_blocks = -(-n_pairs // MOE_BLOCK) + N_EXPERTS
    n_rows = n_blocks * MOE_BLOCK
    buf_tok = jnp.zeros((n_rows,), jnp.int32).at[dest].set(tok_s.astype(jnp.int32))
    buf_g = jnp.zeros((n_rows,), jnp.float32).at[dest].set(g_s)
    blk_e = jnp.clip(jnp.searchsorted(pend, jnp.arange(n_blocks) * MOE_BLOCK, side='right'), 0, N_EXPERTS - 1)
    xs = xf[buf_tok].reshape(n_blocks, MOE_BLOCK, d)

    def expert_block(args):
        xb, e = args
        return swiglu(xb, w_gate[e], w_up[e], w_down[e])

    ys = lax.map(expert_block, (xs, blk_e)).reshape(n_rows, d)
    ys = ys * buf_g[:, None].astype(ys.dtype)
    out = jnp.zeros((n_tok, d), h.dtype).at[buf_tok].add(ys)
    return out.reshape(b, s_len, d)

def setup_inputs(seed: int = 0) -> dict:
    key = jax.random.key(seed)
    ks = jax.random.split(key, 26)
    f32 = jnp.float32

    def nrm(k, shape, fan_in):
        return jax.random.normal(k, shape, f32) * (fan_in ** -0.5)

    def gain(k, shape):
        return 1.0 + 0.05 * jax.random.normal(k, shape, f32)

    return {
        'x': jax.random.normal(ks[0], (BATCH, SEQ, D_MODEL), f32),
        'mem': jax.random.normal(ks[1], (BATCH, MEM_LEN, D_MODEL), f32),
        'mix_norm_pre': gain(ks[2], (DEPTH, D_MODEL)),
        'mix_norm_post': gain(ks[3], (DEPTH, D_MODEL)),
        'w_in': nrm(ks[4], (DEPTH, D_MODEL, C_IN), D_MODEL),
        'b_forget': 2.0 + 0.5 * jax.random.normal(ks[5], (DEPTH, FOX_HEADS), f32),
        'pool_w': nrm(ks[6], (DEPTH, len(POOL_WINDOWS), POOL_GROUP, POOL_GROUP), POOL_GROUP),
        'pool_scale': 1.0 + 0.1 * jax.random.normal(ks[7], (DEPTH, POOL_DIM), f32),
        'w_out': nrm(ks[8], (DEPTH, MIX_DIM, D_MODEL), MIX_DIM),
        'xa_norm_pre': gain(ks[9], (DEPTH, D_MODEL)),
        'xa_norm_post': gain(ks[10], (DEPTH, D_MODEL)),
        'mem_norm': gain(ks[11], (DEPTH, D_MODEL)),
        'xa_wq': nrm(ks[12], (DEPTH, D_MODEL, D_MODEL), D_MODEL),
        'xa_wkv': nrm(ks[13], (DEPTH, D_MODEL, 2 * D_MODEL), D_MODEL),
        'xa_wo': nrm(ks[14], (DEPTH, D_MODEL, D_MODEL), D_MODEL),
        'ffn_norm_pre': gain(ks[15], (DEPTH, D_MODEL)),
        'ffn_norm_post': gain(ks[16], (DEPTH, D_MODEL)),
        'dense_w_gate': nrm(ks[17], (N_DENSE, D_MODEL, D_FF), D_MODEL),
        'dense_w_up': nrm(ks[18], (N_DENSE, D_MODEL, D_FF), D_MODEL),
        'dense_w_down': nrm(ks[19], (N_DENSE, D_FF, D_MODEL), D_FF),
        'router_w': nrm(ks[20], (N_MOE, D_MODEL, N_EXPERTS), D_MODEL),
        'moe_w_gate': nrm(ks[21], (N_MOE, N_EXPERTS, D_MODEL, D_FF), D_MODEL),
        'moe_w_up': nrm(ks[22], (N_MOE, N_EXPERTS, D_MODEL, D_FF), D_MODEL),
        'moe_w_down': nrm(ks[23], (N_MOE, N_EXPERTS, D_FF, D_MODEL), D_FF),
    }

def reference(x, mem, mix_norm_pre, mix_norm_post, w_in, b_forget, pool_w, pool_scale, w_out,
              xa_norm_pre, xa_norm_post, mem_norm, xa_wq, xa_wkv, xa_wo,
              ffn_norm_pre, ffn_norm_post, dense_w_gate, dense_w_up, dense_w_down,
              router_w, moe_w_gate, moe_w_up, moe_w_down):
    h = x
    for i in range(DEPTH):
        a = hybrid_mixer(rmsnorm(h, mix_norm_pre[i]), w_in[i], b_forget[i], pool_w[i], pool_scale[i], w_out[i])
        h = h + rmsnorm(a, mix_norm_post[i])
        c = memory_cross_attention(rmsnorm(h, xa_norm_pre[i]), rmsnorm(mem, mem_norm[i]),
                                   xa_wq[i], xa_wkv[i], xa_wo[i])
        h = h + rmsnorm(c, xa_norm_post[i])
        hn = rmsnorm(h, ffn_norm_pre[i])
        j = i // 2
        if i % 2 == 0:
            f = swiglu(hn, dense_w_gate[j], dense_w_up[j], dense_w_down[j])
        else:
            f = moe_swiglu(hn, router_w[j], moe_w_gate[j], moe_w_up[j], moe_w_down[j])
        h = h + rmsnorm(f, ffn_norm_post[i])
    return h


_drawn_inputs = setup_inputs


def setup_inputs(seed=0):
    import zlib

    import numpy as np

    out = dict(_drawn_inputs(seed))
    spreads = {}
    factors = {}
    for name, (base, spread) in spreads.items():
        noise = np.random.default_rng([zlib.crc32(name.encode()), seed]).standard_normal(out[name].shape)
        drawn = base * np.exp(spread * noise) if base else spread * noise
        out[name] = __import__('jax').numpy.asarray(drawn.astype(out[name].dtype))
    for name, factor in factors.items():
        out[name] = (out[name] * factor).astype(out[name].dtype)
    return out
```

```python
from contextlib import ExitStack

import numpy as np

import concourse.bass as bass
from concourse import mybir

ALU = mybir.AluOpType
ACT = mybir.ActivationFunctionType
AX_X = mybir.AxisListType.X
F32 = mybir.dt.float32
BF16 = mybir.dt.bfloat16
I32 = mybir.dt.int32
U32 = mybir.dt.uint32

P = 128
D = 1024
SEQ = 256
DEPTH = 2
KT = D // P
TT = SEQ // P
HD = 64
HEADS = 6
MIX = HEADS * HD
PAIRS = HEADS // 2
XH = 4
XHD = D // XH
FF = 2816
FFC = 256
STEPS = FF // FFC
FPS = FFC // P
EXPERTS = 8
WINDOWS = (2, 4, 8, 16)
PAD = WINDOWS[-1]
SMALL_DMAS = 2 + DEPTH * len(WINDOWS)
HALF = 512
BANKS = 8
LOW = -1.0e30
TRI = P + SEQ

SLOTS = 4
SLOT = 2 * KT * FFC + FPS * D
UNITS = 14
UNIT_USES = [len(range(s, UNITS, SLOTS)) for s in range(SLOTS)]
STEP_USES = [len(range(s, STEPS, SLOTS)) for s in range(SLOTS)]
HEAD_STEPS = STEPS - 2 * SLOTS
UNIT_DMAS, STEP_DMAS = 2, 3

WIDTHS = (64, 128, 160, 256)

STAGES = [("mixT", 4), ("fu", 3), ("fqk", 6), ("sqk", 6), ("v", 4), ("pool", 2), ("out", 4),
          ("memT", 4), ("xk", 8), ("xv", 4), ("xaT", 4), ("xq", 8), ("xo", 4), ("ffT", 4)]
COUNT = dict(STAGES)
FIRST = {name: sum(c for _, c in STAGES[:i]) for i, (name, _) in enumerate(STAGES)}
UNIT_LAST = [("fu", 2), ("fqk", 5), ("sqk", 5), ("v", 3), ("out", 1), ("out", 3), ("xk", 3), ("xk", 7),
             ("xv", 1), ("xv", 3), ("xq", 3), ("xq", 7), ("xo", 1), ("xo", 3)]
PER_LAYER = sum(c for _, c in STAGES)

C_IDENT, C_TRI, C_NEG, C_ONES = 0, 128, 256, 384
C_STRICT, C_MIN, C_CAUSAL = 640, 1024, 1408
C_IOTA, C_INV, C_EPS, C_END = 1792, 2048, 2560, 2561

G_MIX, G_XA, G_MEM, G_FF, G_POOL, G_ROWS = 0, 16, 32, 48, 64, 68


GAIN_OF = {"mixT": G_MIX, "xaT": G_XA, "memT": G_MEM, "ffT": G_FF}


def constants():
    c = np.zeros((P, C_END), np.float32)
    i, j = np.arange(P)[:, None], np.arange(P)[None, :]
    c[:, C_IDENT:C_IDENT + P] = i == j
    c[:, C_TRI:C_TRI + P] = -1.0 * (i >= j)
    c[:, C_NEG:C_NEG + P] = -1.0
    c[:, C_ONES:C_ONES + SEQ] = 1.0
    c[:, C_STRICT:C_STRICT + TRI] = 1.0
    for b in (0, SEQ):
        c[:, C_STRICT + b:C_STRICT + b + P] = i < j
        c[:, C_MIN + b:C_MIN + b + P] = np.where(i < j, 0.0, LOW)
        c[:, C_CAUSAL + b:C_CAUSAL + b + P] = np.where(j <= i, 0.0, LOW)
    c[:, C_IOTA:C_IOTA + SEQ] = np.arange(SEQ)
    for g, w in enumerate(WINDOWS):
        col = C_INV + SEQ * (g // 2)
        c[64 * (g % 2):64 * (g % 2) + 64, col:col + SEQ] = 1.0 / np.minimum(np.arange(SEQ) + 1, w)
    c[:, C_EPS] = 1e-6
    return c


def build(nc, a, out, consts_dram):
    with ExitStack() as ctx:
        def sb(name, shape, dt=F32):
            return ctx.enter_context(nc.sbuf_tensor(name, shape, dt))

        def sem(name):
            return ctx.enter_context(nc.semaphore(name))

        banks = ctx.enter_context(nc.psum_tensor("banks", [P, BANKS, HALF], F32))

        ring = sb("ring", [P, SLOTS, SLOT])
        h_res = sb("h_res", [P, TT, D])
        mem_n = sb("mem_n", [P, TT, D])
        xn = sb("xn", [P, TT, D])
        xT = sb("xT", [P, KT, SEQ])
        mixT = sb("mixT", [P, KT, SEQ])
        res = sb("res", [P, TT, D])
        gpost = sb("gpost", [P, 2, D])
        cst = sb("cst", [P, C_END])
        phase = sb("phase", [P, 9216])
        gcols = sb("gcols", [P, G_ROWS])
        stats = sb("stats", [P, 3, 2 * (1 + 6 * DEPTH)])
        small = sb("small", [P, 512])
        count_i = sb("count_i", [P, EXPERTS], I32)
        topi = sb("topi", [P, TT, 8], U32)
        poolw = sb("poolw", [P, DEPTH, 2, P])
        grow = sb("grow", [P, P])

        ident = cst[:, C_IDENT:C_IDENT + P]
        neg_tri = cst[:, C_TRI:C_TRI + P]
        neg_ones = cst[:, C_NEG:C_NEG + P]
        ones = cst[:, C_ONES:C_ONES + SEQ]
        strict = cst[:, C_STRICT:C_STRICT + TRI]
        low_min = cst[:, C_MIN:C_MIN + TRI]
        causal = cst[:, C_CAUSAL:C_CAUSAL + TRI]
        iota = cst[:, C_IOTA:C_IOTA + SEQ]
        inv_count = cst[:, C_INV:C_INV + 2 * SEQ].rearrange("p (c t) -> p c t", c=2)
        eps = cst[:, C_EPS:C_EPS + 1]

        def view(t, at, *dims):
            n = int(np.prod(dims))
            flat = t[:, at:at + n]
            if len(dims) == 1:
                return flat
            if len(dims) == 2:
                return flat.rearrange("p (a b) -> p a b", a=dims[0])
            return flat.rearrange("p (a b c) -> p a b c", a=dims[0], b=dims[1])

        qkT = view(phase, 0, 12, SEQ)
        vals = view(phase, 3072, TT, 2 * MIX)
        fox_p = view(phase, 4608, 2, TRI)
        fox_pT = view(phase, 5376, 2, TRI)
        sb_l = view(phase, 6144, 2, TRI)
        sb_keep = view(phase, 6912, 2, TRI)
        sb_w = view(phase, 7680, 2, TRI)
        forget = view(phase, 8448, 3, SEQ)
        xkT = view(phase, 0, KT, SEQ)
        xval = view(phase, 2048, TT, D)
        xqT = view(phase, 4096, KT, SEQ)
        x_p = view(phase, 6144, 2, TT * SEQ)
        x_pT = view(phase, 7168, 2, TT * SEQ)
        xg = view(phase, 0, KT, SEQ)
        y_sb = view(phase, 2048, 2, D)
        hT = view(phase, 4096, FPS, SEQ)
        silu_g = view(phase, 4608, FPS, SEQ)
        place = view(phase, 5120, TT, SEQ)
        place_g = view(phase, 5632, TT, SEQ)
        spread = view(phase, 6144, 2, SEQ)
        flat_xn = xn[:, :, :].rearrange("p t d -> p (t d)")
        decay_q = view(flat_xn, 0, HEADS, SEQ)
        decay_k = flat_xn[:, HEADS * SEQ:(HEADS + 1) * SEQ]
        flat_res = res[:, :, :].rearrange("p t d -> p (t d)")
        u_pad = view(flat_res, 0, 2, PAD + SEQ)
        run_a = flat_res[:, 544:816]
        run_b = flat_res[:, 816:1088]
        pool_r = view(flat_res, 1088, 2, SEQ)

        fox_nmax = view(small, 0, 2, 2)
        fox_sum = view(small, 4, 2, 2)
        fox_inv = view(small, 8, 2, 2)
        x_nmax = view(small, 12, 2, 2)
        x_sum = view(small, 16, 2, 2)
        x_inv = view(small, 20, 2, 2)
        x_max = view(small, 24, 2, 2)
        bias_f = view(small, 28, DEPTH)
        logits = view(small, 32, TT, 8)
        top = view(small, 48, TT, 8)
        topf = view(small, 64, TT, 8)
        first = view(small, 80, TT, 8)
        second = view(small, 96, TT, 8)
        chosen = view(small, 112, TT, 8)
        gate = view(small, 128, TT, 8)
        rank = view(small, 144, TT, 8)
        gap = view(small, 160, TT)
        egap = view(small, 162, TT)
        gate1 = view(small, 164, TT)
        gate2 = view(small, 166, TT)
        router = view(small, 192, KT, 8)
        fox_max = view(small, 168, 2, 2)

        consts_in = sem("consts_in")
        x_in = sem("x_in")
        mem_in = sem("mem_in")
        vectors_in = sem("vectors_in")
        small_in = sem("small_in")
        gpost_in = [sem(f"gpost_in{i}") for i in range(2)]
        slot_in = [sem(f"slot_in{s}") for s in range(SLOTS)]
        steps_done = sem("steps_done")
        pads_set = sem("pads_set")
        act_step = sem("act_step")
        dve_step = sem("dve_step")
        pool_step = sem("pool_step")
        tile_full = sem("tile_full")
        tile_act = sem("tile_act")
        tile_dve = sem("tile_dve")
        rms_ready = sem("rms_ready")
        mem_ready = sem("mem_ready")
        xn_ready = sem("xn_ready")
        h_ready = sem("h_ready")
        forget_log = sem("forget_log")
        decay_set = sem("decay_set")
        decay_ready = sem("decay_ready")
        pool_ready = sem("pool_ready")
        fox_scored, fox_masked, fox_exp, fox_prob, fox_turned, fox_pt, fox_out, fox_mix = (
            sem(f"fox_{n}") for n in ("scored", "masked", "exp", "prob", "turned", "pt", "out", "mix"))
        sb_scored, sb_soft, sb_kept, sb_summed, sb_logw, sb_wt, sb_out, sb_mix = (
            sem(f"sb_{n}") for n in ("scored", "soft", "kept", "summed", "logw", "wt", "out", "mix"))
        xa_scored, xa_max, xa_exp, xa_prob, xa_turned, xa_pt, xa_out, xa_mix = (
            sem(f"xa_{n}") for n in ("scored", "max", "exp", "prob", "turned", "pt", "out", "mix"))
        hidden_full = sem("hidden_full")
        silu_ready = sem("silu_ready")
        hidden_ready = sem("hidden_ready")
        y_act, y_dve = sem("y_act"), sem("y_dve")
        logits_full, logits_ready = sem("logits_full"), sem("logits_ready")
        gap_ready, gap_exp = sem("gap_ready"), sem("gap_exp")
        chosen_ready = sem("chosen_ready")
        rank_full, rank_ready = sem("rank_full"), sem("rank_ready")
        place_ready, place_g_ready = sem("place_ready"), sem("place_g_ready")
        gathered, gather_act, gather_dve = sem("gathered"), sem("gather_act"), sem("gather_dve")
        spread_full, spread_ready = sem("spread_full"), sem("spread_ready")
        sum_full, sum_added = sem("sum_full"), sem("sum_added")
        out_done = sem("out_done")

        def tile(layer, stage, i=0):
            return 1 + PER_LAYER * layer + FIRST[stage] + i

        def wait_moved(eng, n):
            eng.wait_ge(tile_act, (n + 1) // 2)
            if n // 2:
                eng.wait_ge(tile_dve, n // 2)

        def after(layer, stage):
            return tile(layer, stage) + COUNT[stage]

        def steps_before(layer):
            return 1 + layer * STEPS

        def unit_read(eng, layer, u):
            stage, i = UNIT_LAST[u]
            eng.wait_ge(tile_full, tile(layer, stage, i) + 1)

        def slot_dmas(layer, s):
            return 16 * layer * (UNIT_DMAS * UNIT_USES[s] + STEP_DMAS * STEP_USES[s])

        def wait_unit(eng, layer, u):
            s = u % SLOTS
            eng.wait_ge(slot_in[s], slot_dmas(layer, s) + 16 * UNIT_DMAS * (u // SLOTS + 1))

        def wait_step(eng, layer, s, n):
            base = slot_dmas(layer, s) + 16 * UNIT_DMAS * UNIT_USES[s]
            eng.wait_ge(slot_in[s], (n + 1) * (16 * STEP_DMAS) + base)

        def hidden_before(layer):
            return layer * STEPS * FPS

        def slot(s, at, *dims):
            return view(ring[:, s, :], at, *dims)

        def rms_number(layer, j):
            return 1 if layer == 0 and j == 0 else 6 * layer + j + 2

        def move_gains(eng, move):
            eng.wait_ge(tile_full, 1)
            move(gcols[:, :], banks[:, 0, 0:G_ROWS]).then_inc(tile_act, 1)

        def mover(eng, move, parity):
            def move_stage(layer, stage):
                for i in range(COUNT[stage]):
                    n = tile(layer, stage, i)
                    if n % 2 != parity:
                        continue
                    src = banks[:, n % BANKS, :]
                    eng.wait_ge(tile_full, n + 1)
                    if stage in GAIN_OF:
                        for j in range(2):
                            d = 2 * i + j
                            g = GAIN_OF[stage] + KT * layer + d
                            ins = move(xT[:, d, :], src[:, j * SEQ:(j + 1) * SEQ], gcols[:, g:g + 1])
                    elif stage == "fu" and i == 0:
                        ins = move(forget[0:HEADS, 0, :], src[0:HEADS, 0:SEQ])
                    elif stage == "fu":
                        ins = move(u_pad[:, i - 1, PAD:], src[:, 0:SEQ])
                    elif stage == "fqk":
                        ins = move(qkT[:, i, :], src[:, 0:SEQ], HD ** -0.5 if i < PAIRS else 1.0)
                    elif stage == "sqk":
                        ins = move(qkT[:, 2 * PAIRS + i, :], src[:, 0:SEQ], HD ** -0.5 if i < PAIRS else 1.0)
                    elif stage == "v":
                        ins = move(vals[:, i // 2, (i % 2) * MIX:(i % 2 + 1) * MIX], src[:, 0:MIX])
                    elif stage == "pool":
                        g = G_POOL + 2 * layer + i
                        ins = move(mixT[:, 2 * PAIRS + i, :], src[:, 0:SEQ], gcols[:, g:g + 1])
                    elif stage in ("out", "xo"):
                        ins = move(res[:, i % 2, (i // 2) * HALF:(i // 2 + 1) * HALF], src)
                    elif stage == "xk":
                        ins = move(xkT[:, i, :], src[:, 0:SEQ])
                    elif stage == "xq":
                        ins = move(xqT[:, i, :], src[:, 0:SEQ], XHD ** -0.5)
                    elif stage == "xv":
                        ins = move(xval[:, i % 2, (i // 2) * HALF:(i // 2 + 1) * HALF], src)
                    ins.then_inc(tile_dve if parity else tile_act, 1)
            return move_stage

        def w(name, layer):
            return a[name][layer].rearrange("(k p) n -> p k n", p=P)

        block = ctx.enter_context(nc.Block())

        @block.sync
        def _(sp):
            sp.dma_start(cst[:, :], consts_dram).then_inc(consts_in, 16)
            sp.dma_start(h_res[:, :, :], a["x"][0].rearrange("(t p) d -> p t d", p=P)).then_inc(x_in, 16)
            for i, name in enumerate(("mix_norm_pre", "xa_norm_pre", "mem_norm", "ffn_norm_pre")):
                sp.dma_start(grow[16 * i:16 * i + 16, :],
                             a[name].rearrange("l (k p) -> (l k) p", p=P)).then_inc(vectors_in, 16)
            sp.dma_start(grow[G_POOL:G_ROWS, :],
                         a["pool_scale"].rearrange("l (k p) -> (l k) p", p=P)).then_inc(vectors_in, 16)

            def load_gpost(layer, q):
                n = 3 * layer + q
                if n >= 2:
                    sp.wait_ge(h_ready, TT * (n - 1))
                name = ("mix_norm_post", "xa_norm_post", "ffn_norm_post")[q]
                sp.dma_start(gpost[:, n % 2, :],
                             a[name][layer:layer + 1, :].to_broadcast([P, D])).then_inc(gpost_in[n % 2], 16)

            def load_unit(layer, u):
                s = u % SLOTS
                if u >= SLOTS:
                    unit_read(sp, layer, u - SLOTS)
                elif layer:
                    sp.wait_ge(steps_done, 1 + STEPS)
                f0 = 6 * MIX
                whole = {0: ("w_in", f0, HEADS + D // 4), 1: ("w_in", 3 * MIX, 2 * MIX), 2: ("w_in", 0, 2 * MIX),
                         4: ("w_out", 0, HALF), 5: ("w_out", HALF, HALF),
                         6: ("xa_wkv", 0, HALF), 7: ("xa_wkv", HALF, HALF),
                         8: ("xa_wkv", D, HALF), 9: ("xa_wkv", D + HALF, HALF),
                         10: ("xa_wq", 0, HALF), 11: ("xa_wq", HALF, HALF),
                         12: ("xa_wo", 0, HALF), 13: ("xa_wo", HALF, HALF)}
                if u in whole:
                    name, c0, n = whole[u]
                    dst = slot(s, 0, KT, n)
                    for k in (0, KT // 2):
                        sp.dma_start(dst[:, k:k + KT // 2, :],
                                     w(name, layer)[:, k:k + KT // 2, c0:c0 + n]).then_inc(slot_in[s], 16)
                else:
                    for j, c0 in enumerate((2 * MIX, 5 * MIX)):
                        sp.dma_start(slot(s, j * KT * MIX, KT, MIX),
                                     w("w_in", layer)[:, :, c0:c0 + MIX]).then_inc(slot_in[s], 16)

            def load_step(layer, gate_w, up_w, down_w, s, done, c0, first_round, head=False):
                if first_round:
                    unit_read(sp, layer, s + SLOTS * (UNIT_USES[s] - 1))
                if layer or not head:
                    sp.wait_ge(steps_done, done + steps_before(layer))
                sp.dma_start(slot(s, 0, KT, FFC),
                             gate_w.rearrange("(k p) n -> p k n", p=P)[:, :, bass.ds(c0, FFC)]).then_inc(slot_in[s], 16)
                sp.dma_start(slot(s, KT * FFC, KT, FFC),
                             up_w.rearrange("(k p) n -> p k n", p=P)[:, :, bass.ds(c0, FFC)]).then_inc(slot_in[s], 16)
                sp.dma_start(slot(s, 2 * KT * FFC, FPS, D),
                             down_w[bass.ds(c0, FFC), :].rearrange("(k p) n -> p k n", p=P)).then_inc(slot_in[s], 16)

            def load_steps(layer, gate_w, up_w, down_w, before):
                for i in range(HEAD_STEPS):
                    load_step(layer, gate_w, up_w, down_w, i, before - (HEAD_STEPS - 1 - i), FFC * i, True, True)
                with sp.Fori(0, 2) as r:
                    for j in range(SLOTS):
                        i = HEAD_STEPS + j
                        load_step(layer, gate_w, up_w, down_w, i % SLOTS, before + r * SLOTS + (i + 1 - SLOTS),
                                  r * (FFC * SLOTS) + FFC * i, i < SLOTS)

            for layer in range(DEPTH):
                for u in range(UNITS):
                    if layer == 0 and u == 1:
                        sp.dma_start(mem_n[:, :, :],
                                     a["mem"][0].rearrange("(t p) d -> p t d", p=P)).then_inc(mem_in, 16)
                    if u == 4 and layer == 0:
                        load_gpost(0, 0)
                        load_gpost(0, 1)
                    if u == 6 and layer:
                        load_gpost(layer, 1)
                    if u == 10:
                        load_gpost(layer, 2)
                    load_unit(layer, u)
                if layer == 0:
                    load_steps(0, a["dense_w_gate"][0], a["dense_w_up"][0], a["dense_w_down"][0], 0)
                    load_gpost(1, 0)
                else:
                    with sp.Fori(0, EXPERTS) as e:
                        one = bass.ds(e, 1)
                        load_steps(layer, a["moe_w_gate"][0][one].rearrange("a d f -> (a d) f"),
                                   a["moe_w_up"][0][one].rearrange("a d f -> (a d) f"),
                                   a["moe_w_down"][0][one].rearrange("a d f -> (a d) f"),
                                   e * STEPS)
            sp.wait_ge(out_done, 16)

        @block.gpsimd
        def _(pool):
            steps = [0]

            def chain(ins):
                steps[0] += 1
                ins.then_inc(pool_step, 1)
                pool.wait_ge(pool_step, steps[0])

            with nc.allow_non_contiguous_dma(reason="two small vectors"):
                pool.dma_start(bias_f[0:HEADS, :], a["b_forget"].rearrange("l h -> h l")).then_inc(small_in, 16)
                pool.dma_start(router[:, :, :], a["router_w"][0].rearrange("(k p) e -> p k e", p=P)).then_inc(small_in, 16)
            chain(pool.memset(poolw[:, :, :, :], 0.0))
            for layer in range(DEPTH):
                for g in range(len(WINDOWS)):
                    r0 = 64 * (g % 2)
                    pool.dma_start(poolw[r0:r0 + 64, layer, g // 2, r0:r0 + 64],
                                   a["pool_w"][layer, g]).then_inc(small_in, 16)
            pool.wait_ge(consts_in, 16)
            for layer in range(DEPTH):
                wait_moved(pool, after(layer, "mixT"))
                chain(pool.memset(flat_xn[:, 0:(HEADS + 1) * SEQ], 0.0))
                for h in range(HEADS):
                    chain(pool.tensor_scalar(decay_q[32:32 + HEADS, h, :], ones[32:32 + HEADS, :],
                                             ident[32:32 + HEADS, 32 + h:33 + h], None, ALU.mult))
                pool.memset(decay_k[0:HEADS, :], 1.0).then_inc(decay_set, 1)
                pool.wait_ge(decay_set, layer + 1)
                chain(pool.memset(u_pad[:, :, 0:PAD], 0.0))
                wait_moved(pool, after(layer, "fu"))
                for c in range(2):
                    u = u_pad[:, c, :]
                    end = PAD + SEQ

                    def wider(dst, src, shift):
                        lo = 2 * shift - 1
                        chain(pool.tensor_tensor(dst[:, lo:end], src[:, lo:end], src[:, lo - shift:end - shift], ALU.add))

                    wider(run_a, u, 1)
                    wider(run_b, run_a, 2)
                    if c == 1:
                        wider(run_a, run_b, 4)
                        wider(run_b, run_a, 8)
                    for half, src in enumerate((run_a, run_b)):
                        rows = slice(64 * half, 64 * half + 64)
                        chain(pool.tensor_tensor(pool_r[rows, c, :], src[rows, PAD:end], inv_count[rows, c, :], ALU.mult))
                        ins = pool.tensor_tensor(pool_r[rows, c, :], pool_r[rows, c, :], u[rows, PAD:end], ALU.subtract)
                        chain(ins)
                pool.engine_nop().then_inc(pool_ready, 1)

        @block.scalar
        def _(act):
            steps = [0]

            def chain(ins):
                steps[0] += 1
                ins.then_inc(act_step, 1)
                act.wait_ge(act_step, steps[0])

            def rms(n, src, arrived, unused=xn):
                for t in range(TT):
                    arrived(t)
                    chain(act.activation(unused[:, t, :], src[:, t, :], ACT.Square, accum_out=stats[:, 0, 2 * n + t:2 * n + t + 1]))
                pair = slice(2 * n, 2 * n + 2)
                chain(act.activation(stats[:, 1, pair], stats[:, 0, pair], ACT.Ln, bias=eps, scale=1.0 / D))
                act.activation(stats[:, 2, pair], stats[:, 1, pair], ACT.Exp, scale=-0.5).then_inc(rms_ready, 1)

            def pre(layer, q):
                def arrived(t):
                    if layer == 0 and q == 0:
                        act.wait_ge(x_in, 16)
                    else:
                        act.wait_ge(h_ready, TT * (3 * layer + q - 1) + t + 1)
                rms(1 + 6 * layer + 2 * q, h_res, arrived)

            def post(layer, q):
                def arrived(t):
                    if q < 2:
                        wait_moved(act, after(layer, ("out", "xo")[q]))
                    elif layer == 0:
                        act.wait_ge(y_act, 1)
                        act.wait_ge(y_dve, 1)
                    else:
                        act.wait_ge(sum_added, 4 * EXPERTS)
                rms(2 + 6 * layer + 2 * q, res, arrived)

            def move(out_, in_, scale=1.0):
                return act.activation(out_, in_, ACT.Copy, scale=scale)

            move_stage = mover(act, move, 0)

            def fox_heads(layer):
                for i in range(HEADS + 2):
                    if i < HEADS:
                        n = HEADS * layer + i
                        act.wait_ge(sb_scored, n + 1)
                        z = banks[:, 2 + i % 3, 0:TRI]
                        chain(act.activation(sb_l[:, i % 2, :], z, ACT.Abs))
                        chain(act.activation(sb_l[:, i % 2, :], sb_l[:, i % 2, :], ACT.Exp, scale=-1.0))
                        act.activation(sb_l[:, i % 2, :], sb_l[:, i % 2, :], ACT.Ln, bias=1.0).then_inc(sb_soft, 1)
                        act.wait_ge(fox_masked, n + 1)
                        for t, cols in enumerate((slice(0, P), slice(P, TRI))):
                            ins = act.activation(fox_p[:, i % 2, cols], fox_p[:, i % 2, cols], ACT.Exp,
                                                 bias=fox_nmax[:, i % 2, t:t + 1], accum_out=fox_sum[:, i % 2, t:t + 1])
                        ins.then_inc(fox_exp, 1)
                    if 1 <= i <= HEADS:
                        j, n = i - 1, HEADS * layer + i - 1
                        act.wait_ge(sb_logw, n + 1)
                        act.activation(sb_w[:, j % 2, :], sb_w[:, j % 2, :], ACT.Exp).then_inc(sb_wt, 1)
                        act.wait_ge(fox_turned, n + 1)
                        move(fox_pT[:, j % 2, :], banks[:, 5, 0:TRI]).then_inc(fox_pt, 1)
                    if i >= 2 and i % 2 == 1:
                        pair = (i - 3) // 2
                        act.wait_ge(sb_out, HEADS * layer + 2 * pair + 2)
                        move(mixT[:, pair, :], banks[:, 7, 0:SEQ]).then_inc(sb_mix, 1)

            def xa_heads(layer):
                for i in range(XH + 2):
                    if i < XH:
                        n = XH * layer + i
                        act.wait_ge(xa_max, n + 1)
                        if i >= 2:
                            act.wait_ge(xa_turned, n - 1)
                        for t in range(TT):
                            cols = slice(t * SEQ, t * SEQ + SEQ)
                            ins = act.activation(x_p[:, i % 2, cols], banks[:, i % 2, cols], ACT.Exp,
                                                 bias=x_nmax[:, i % 2, t:t + 1], accum_out=x_sum[:, i % 2, t:t + 1])
                        ins.then_inc(xa_exp, 1)
                    if 1 <= i <= XH:
                        j, n = i - 1, XH * layer + i - 1
                        act.wait_ge(xa_turned, n + 1)
                        move(x_pT[:, j % 2, :], banks[:, 2 + j % 2, :]).then_inc(xa_pt, 1)

            def hidden_tiles(n):
                for j in range(FPS):
                    act.wait_ge(hidden_full, n + (j + 1))
                    act.activation(silu_g[:, j, :], banks[:, 4 + j, 0:SEQ], ACT.Silu).then_inc(silu_ready, 1)

            def y_done(layer, e):
                act.wait_ge(steps_done, e * STEPS + (steps_before(layer) + STEPS))

            act.wait_ge(consts_in, 16)
            for layer in range(DEPTH):
                pre(layer, 0)
                if layer == 0:
                    rms(0, mem_n, lambda t: act.wait_ge(mem_in, 16), unused=res)
                    move_gains(act, move)
                    act.wait_ge(tile_act, 1)
                move_stage(layer, "mixT")
                move_stage(layer, "fu")
                wait_moved(act, after(layer, "fu"))
                act.wait_ge(small_in, SMALL_DMAS * 16)
                fl = forget[0:HEADS, 0, :]
                fa = forget[0:HEADS, 1, :]
                chain(act.activation(fa, fl, ACT.Abs, bias=bias_f[0:HEADS, layer:layer + 1]))
                chain(act.activation(fa, fa, ACT.Exp, scale=-1.0))
                act.activation(fa, fa, ACT.Ln, bias=1.0).then_inc(forget_log, 1)
                move_stage(layer, "fqk")
                move_stage(layer, "sqk")
                move_stage(layer, "v")
                fox_heads(layer)
                move_stage(layer, "pool")
                move_stage(layer, "out")
                post(layer, 0)
                pre(layer, 1)
                move_stage(layer, "memT")
                move_stage(layer, "xk")
                move_stage(layer, "xv")
                move_stage(layer, "xaT")
                move_stage(layer, "xq")
                xa_heads(layer)
                move_stage(layer, "xo")
                post(layer, 1)
                pre(layer, 2)
                move_stage(layer, "ffT")
                if layer == 0:
                    with act.Fori(0, STEPS) as i:
                        hidden_tiles(i * FPS)
                    y_done(0, 0)
                    for hh in range(2):
                        ins = move(res[:, 0, hh * HALF:(hh + 1) * HALF], banks[:, hh, :])
                    ins.then_inc(y_act, 1)
                else:
                    act.wait_ge(gap_ready, 1)
                    act.activation(egap[:, :], gap[:, :], ACT.Exp).then_inc(gap_exp, 1)
                    with act.Fori(0, EXPERTS) as e:
                        for d in range(0, KT, 2):
                            act.wait_ge(gathered, e * KT + (d + 1))
                            move(xg[:, d, :], banks[:, 6, 0:SEQ],
                                 gcols[:, G_FF + KT * layer + d:G_FF + KT * layer + d + 1]).then_inc(gather_act, 1)
                        with act.Fori(0, STEPS) as i:
                            hidden_tiles(e * (STEPS * FPS) + i * FPS + hidden_before(layer))
                        act.wait_ge(spread_full, e + 1)
                        move(spread[:, :, :].rearrange("p a b -> p (a b)"), banks[:, 6, :]).then_inc(spread_ready, 1)
                        y_done(layer, e)
                        for hh in range(2):
                            ins = move(y_sb[:, 0, hh * HALF:(hh + 1) * HALF], banks[:, hh, :])
                        ins.then_inc(y_act, 1)
                post(layer, 2)
            act.wait_ge(h_ready, TT * 3 * DEPTH)
            act.dma_start(out[0].rearrange("(t p) d -> p t d", p=P), h_res[:, :, :]).then_inc(out_done, 16)
            act.wait_ge(out_done, 16)

        @block.vector
        def _(dve):
            steps = [0]

            def chain(ins):
                steps[0] += 1
                ins.then_inc(dve_step, 1)
                dve.wait_ge(dve_step, steps[0])

            def inv_rms(n, t):
                return stats[:, 2, 2 * n + t:2 * n + t + 1]

            def pre(layer, q):
                n = 1 + 6 * layer + 2 * q
                dve.wait_ge(rms_ready, rms_number(layer, 2 * q))
                for t in range(TT):
                    dve.tensor_scalar(xn[:, t, :], h_res[:, t, :], inv_rms(n, t), None, ALU.mult).then_inc(xn_ready, 1)

            def post(layer, q):
                n, p = 2 + 6 * layer + 2 * q, 3 * layer + q
                dve.wait_ge(rms_ready, rms_number(layer, 2 * q + 1))
                dve.wait_ge(gpost_in[p % 2], 16 * (p // 2 + 1))
                for t in range(TT):
                    chain(dve.scalar_tensor_tensor(out=res[:, t, :], in0=res[:, t, :], scalar=inv_rms(n, t),
                                                   in1=gpost[:, p % 2, :], op0=ALU.mult, op1=ALU.mult))
                    dve.tensor_tensor(h_res[:, t, :], h_res[:, t, :], res[:, t, :], ALU.add).then_inc(h_ready, 1)

            def move(out_, in_, scale=1.0):
                return dve.tensor_scalar(out_, in_, scale, None, ALU.mult)

            move_stage = mover(dve, move, 1)

            def decay(layer):
                fl, fa, fc = (forget[0:HEADS, r, :] for r in range(3))
                wait_moved(dve, after(layer, "fu"))
                dve.wait_ge(small_in, SMALL_DMAS * 16)
                chain(dve.tensor_scalar(fc, fl, bias_f[0:HEADS, layer:layer + 1], 0.0, ALU.add, ALU.min))
                dve.wait_ge(forget_log, layer + 1)
                chain(dve.tensor_tensor(fl, fc, fa, ALU.subtract))
                chain(dve.tensor_tensor_scan(fc, ones[0:HEADS, :], fl, 0.0, ALU.mult, ALU.add))
                dve.wait_ge(decay_set, layer + 1)
                for h in range(HEADS):
                    dve.tensor_scalar(decay_q[0:HEADS, h, :], fc, ident[0:HEADS, h:h + 1], None, ALU.mult)
                dve.tensor_scalar(decay_k[32:32 + HEADS, :], fc, -1.0, None, ALU.mult).then_inc(decay_ready, 1)

            def heads(layer):
                for i in range(HEADS + 2):
                    if i < HEADS:
                        n = HEADS * layer + i
                        dve.wait_ge(fox_scored, n + 1)
                        if i >= 2:
                            dve.wait_ge(fox_turned, n - 1)
                        for t, cols in enumerate((slice(0, P), slice(P, TRI))):
                            chain(dve.tensor_tensor_reduce(out=fox_p[:, i % 2, cols], in0=banks[:, i % 2, cols],
                                                           in1=causal[:, cols], scale=1.0, scalar=3.0 * LOW, op0=ALU.add,
                                                           op1=ALU.max, accum_out=fox_max[:, i % 2, t:t + 1]))
                        dve.tensor_scalar(fox_nmax[:, i % 2, :], fox_max[:, i % 2, :], -1.0, None,
                                          ALU.mult).then_inc(fox_masked, 1)
                        dve.wait_ge(sb_soft, n + 1)
                        chain(dve.scalar_tensor_tensor(out=sb_keep[:, i % 2, :], in0=banks[:, 2 + i % 3, 0:TRI], scalar=0.0,
                                                       in1=sb_l[:, i % 2, :], op0=ALU.max, op1=ALU.add))
                        dve.tensor_tensor(sb_keep[:, i % 2, :], sb_keep[:, i % 2, :], strict, ALU.mult).then_inc(sb_kept, 1)
                        dve.wait_ge(fox_exp, n + 1)
                        chain(dve.reciprocal(fox_inv[:, i % 2, :], fox_sum[:, i % 2, :]))
                        for t, cols in enumerate((slice(0, P), slice(P, TRI))):
                            ins = dve.tensor_scalar(fox_p[:, i % 2, cols], fox_p[:, i % 2, cols],
                                                    fox_inv[:, i % 2, t:t + 1], None, ALU.mult)
                        ins.then_inc(fox_prob, 1)
                    if 1 <= i <= HEADS:
                        j, n = i - 1, HEADS * layer + i - 1
                        dve.wait_ge(sb_summed, n + 1)
                        if j >= 2:
                            dve.wait_ge(sb_out, n - 1)
                        dve.tensor_tensor(sb_w[:, j % 2, :], banks[:, 2 + j % 3, 0:TRI], low_min, ALU.min).then_inc(sb_logw, 1)
                    if i >= 2 and i % 2 == 1:
                        pair = (i - 3) // 2
                        dve.wait_ge(fox_out, HEADS * layer + 2 * pair + 2)
                        move(mixT[:, PAIRS + pair, :], banks[:, 6, 0:SEQ]).then_inc(fox_mix, 1)

            def xa_heads(layer):
                for i in range(XH + 2):
                    if i < XH:
                        n = XH * layer + i
                        dve.wait_ge(xa_scored, n + 1)
                        chain(dve.tensor_reduce(x_max[:, i % 2, :], banks[:, i % 2, :].rearrange("p (t m) -> p t m", t=TT),
                                                AX_X, ALU.max))
                        dve.tensor_scalar(x_nmax[:, i % 2, :], x_max[:, i % 2, :], -1.0, None, ALU.mult).then_inc(xa_max, 1)
                        dve.wait_ge(xa_exp, n + 1)
                        chain(dve.reciprocal(x_inv[:, i % 2, :], x_sum[:, i % 2, :]))
                        for t in range(TT):
                            cols = slice(t * SEQ, t * SEQ + SEQ)
                            ins = dve.tensor_scalar(x_p[:, i % 2, cols], x_p[:, i % 2, cols], x_inv[:, i % 2, t:t + 1],
                                                    None, ALU.mult)
                        ins.then_inc(xa_prob, 1)
                    if i >= 2:
                        j, n = i - 2, XH * layer + i - 2
                        dve.wait_ge(xa_out, n + 1)
                        move(mixT[:, 2 * j:2 * j + 2, :].rearrange("p a b -> p (a b)"), banks[:, 4 + j % 2, :]).then_inc(xa_mix, 1)

            def hidden_tiles(n):
                for j in range(FPS):
                    dve.wait_ge(silu_ready, n + (j + 1))
                    dve.tensor_tensor(hT[:, j, :], silu_g[:, j, :], banks[:, 4 + j, SEQ:2 * SEQ], ALU.mult).then_inc(hidden_ready, 1)

            def y_done(layer, e):
                dve.wait_ge(steps_done, e * STEPS + (steps_before(layer) + STEPS))

            def route():
                dve.wait_ge(logits_full, 1)
                chain(dve.tensor_copy(logits.rearrange("p a b -> p (a b)"), banks[:, 7, 0:TT * 8]))
                for t in range(TT):
                    chain(dve.max(top[:, t, :], logits[:, t, :]))
                    chain(dve.max_index(topi[:, t, :], top[:, t, :], logits[:, t, :]))
                    chain(dve.tensor_copy(topf[:, t, :], topi[:, t, :]))
                    chain(dve.tensor_scalar(first[:, t, :], iota[:, 0:8], topf[:, t, 0:1], None, ALU.is_equal))
                    chain(dve.tensor_scalar(second[:, t, :], iota[:, 0:8], topf[:, t, 1:2], None, ALU.is_equal))
                    dve.tensor_tensor(chosen[:, t, :], first[:, t, :], second[:, t, :], ALU.add).then_inc(chosen_ready, 1)
                dve.tensor_tensor(gap[:, :], top[:, :, 1], top[:, :, 0], ALU.subtract).then_inc(gap_ready, 1)
                dve.wait_ge(gap_exp, 1)
                chain(dve.tensor_scalar(gate2[:, :], egap[:, :], 1.0, None, ALU.add))
                chain(dve.reciprocal(gate1[:, :], gate2[:, :]))
                chain(dve.tensor_tensor(gate2[:, :], egap[:, :], gate1[:, :], ALU.mult))
                for t in range(TT):
                    chain(dve.tensor_scalar(gate[:, t, :], first[:, t, :], gate1[:, t:t + 1], None, ALU.mult))
                    chain(dve.scalar_tensor_tensor(out=gate[:, t, :], in0=second[:, t, :], scalar=gate2[:, t:t + 1],
                                                   in1=gate[:, t, :], op0=ALU.mult, op1=ALU.add))
                dve.wait_ge(rank_full, 1)
                chain(dve.tensor_copy(rank.rearrange("p a b -> p (a b)"), banks[:, 6, 0:TT * 8]))
                dve.tensor_copy(count_i[:, :], banks[:, 6, TT * 8:TT * 8 + 8]).then_inc(rank_ready, 1)

            dve.wait_ge(consts_in, 16)
            for layer in range(DEPTH):
                pre(layer, 0)
                if layer == 0:
                    dve.wait_ge(rms_ready, 2)
                    for t in range(TT):
                        dve.tensor_scalar(mem_n[:, t, :], mem_n[:, t, :], inv_rms(0, t), None, ALU.mult).then_inc(mem_ready, 1)
                if layer == 0:
                    dve.wait_ge(tile_act, 1)
                move_stage(layer, "mixT")
                move_stage(layer, "fu")
                move_stage(layer, "fqk")
                decay(layer)
                move_stage(layer, "sqk")
                move_stage(layer, "v")
                heads(layer)
                move_stage(layer, "pool")
                move_stage(layer, "out")
                post(layer, 0)
                pre(layer, 1)
                move_stage(layer, "memT")
                move_stage(layer, "xk")
                move_stage(layer, "xv")
                move_stage(layer, "xaT")
                move_stage(layer, "xq")
                xa_heads(layer)
                move_stage(layer, "xo")
                post(layer, 1)
                pre(layer, 2)
                move_stage(layer, "ffT")
                if layer == 0:
                    with dve.Fori(0, STEPS) as i:
                        hidden_tiles(i * FPS)
                    y_done(0, 0)
                    for hh in range(2):
                        ins = move(res[:, 1, hh * HALF:(hh + 1) * HALF], banks[:, 2 + hh, :])
                    ins.then_inc(y_dve, 1)
                else:
                    route()
                    chain(dve.memset(res[:, :, :], 0.0))
                    with dve.Fori(0, EXPERTS) as e:
                        for t in range(TT):
                            dve.tensor_scalar(place[:, t, :], iota, rank[:, t, bass.ds(e, 1)], chosen[:, t, bass.ds(e, 1)],
                                              ALU.is_equal, ALU.mult).then_inc(place_ready, 1)
                        for d in range(1, KT, 2):
                            dve.wait_ge(gathered, e * KT + (d + 1))
                            move(xg[:, d, :], banks[:, 7, 0:SEQ],
                                 gcols[:, G_FF + KT * layer + d:G_FF + KT * layer + d + 1]).then_inc(gather_dve, 1)
                        for t in range(TT):
                            dve.wait_ge(place_ready, e * TT + (t + 1))
                            dve.tensor_scalar(place_g[:, t, :], place[:, t, :], gate[:, t, bass.ds(e, 1)], None,
                                              ALU.mult).then_inc(place_g_ready, 1)
                        with dve.Fori(0, STEPS) as i:
                            hidden_tiles(e * (STEPS * FPS) + i * FPS + hidden_before(layer))
                        y_done(layer, e)
                        for hh in range(2):
                            ins = move(y_sb[:, 1, hh * HALF:(hh + 1) * HALF], banks[:, 2 + hh, :])
                        ins.then_inc(y_dve, 1)
                        for j in range(4):
                            t, hh = j // 2, j % 2
                            dve.wait_ge(sum_full, e * 4 + (j + 1))
                            dst = res[:, t, hh * HALF:(hh + 1) * HALF]
                            dve.tensor_tensor(dst, banks[:, 4 + j, :], dst, ALU.add).then_inc(sum_added, 1)
                post(layer, 2)

        @block.tensor
        def _(pe):
            def bank(n):
                if n >= BANKS:
                    m = n - BANKS
                    pe.wait_ge(tile_act if m % 2 == 0 else tile_dve, m // 2 + 1)
                return banks[:, n % BANKS, :]

            def turn_stage(layer, stage, src, ready, count):
                pe.wait_ge(ready, count)
                for i in range(COUNT[stage]):
                    dst = bank(tile(layer, stage, i))
                    for j in range(2):
                        for t in range(TT):
                            ins = pe.transpose(dst[:, j * SEQ + t * P:j * SEQ + (t + 1) * P],
                                               src[:, t, (2 * i + j) * P:(2 * i + j + 1) * P], ident)
                    ins.then_inc(tile_full, 1)

            def turned_out(n, c0, cols, weights):
                dst = bank(n)
                for k in range(KT):
                    ins = pe.matmul(dst[0:cols, 0:SEQ], weights[:, k, c0:c0 + cols], xT[:, k, :],
                                    start=(k == 0), stop=(k == KT - 1))
                return ins.then_inc(tile_full, 1)

            def rows_out(n, lhsT, t, weights, cols):
                dst = bank(n)
                for k in range(KT):
                    ins = pe.matmul(dst[:, 0:cols], lhsT[:, k, t * P:(t + 1) * P], weights[:, k, :],
                                    start=(k == 0), stop=(k == KT - 1))
                return ins.then_inc(tile_full, 1)

            def unit(layer, u, n):
                wait_unit(pe, layer, u)
                return slot(u % SLOTS, 0, KT, n)

            def turned_units(layer, stage, units, width):
                i = 0
                for u in units:
                    wt = unit(layer, u, width)
                    for c in range(width // P):
                        turned_out(tile(layer, stage, i), c * P, P, wt)
                        i += 1

            def rows_units(layer, stage, units, lhsT):
                i = 0
                for u in units:
                    wt = unit(layer, u, HALF)
                    for t in range(TT):
                        rows_out(tile(layer, stage, i), lhsT, t, wt, HALF)
                        i += 1

            def heads(layer):
                wait_moved(pe, after(layer, "v"))
                pe.wait_ge(decay_ready, layer + 1)
                for i in range(HEADS + 2):
                    if i < HEADS:
                        rows, c, n = slice(HD * (i % 2), HD * (i % 2) + HD), i // 2, HEADS * layer + i
                        fq, fk, sq, sk = (qkT[rows, PAIRS * m + c, :] for m in range(4))
                        b = banks[:, i % 2, :]
                        if i >= 2:
                            pe.wait_ge(fox_masked, n - 1)
                        for t, cols, keys in ((0, slice(0, P), P), (1, slice(P, TRI), SEQ)):
                            pe.matmul(b[:, cols], fq[:, t * P:(t + 1) * P], fk[:, 0:keys], start=(t == 0), stop=False,
                                      skip_group_check=True)
                        for t, cols, keys in ((0, slice(0, P), P), (1, slice(P, TRI), SEQ)):
                            ins = pe.matmul(b[:, cols], decay_q[:, i, t * P:(t + 1) * P], decay_k[:, 0:keys],
                                            start=False, stop=True, skip_group_check=True)
                        ins.then_inc(fox_scored, 1)
                        b = banks[:, 2 + i % 3, :]
                        pe.matmul(b[:, 0:SEQ], sk[:, 0:P], sq, start=True, stop=False, skip_group_check=True)
                        pe.matmul(b[:, SEQ:TRI], sk[:, P:SEQ], sq[:, P:SEQ], start=False, stop=False,
                                  skip_group_check=True).then_inc(sb_scored, 1)
                    if 1 <= i <= HEADS:
                        j, n = i - 1, HEADS * layer + i - 1
                        b = banks[:, 2 + j % 3, :]
                        pe.wait_ge(sb_kept, n + 1)
                        keep = sb_keep[:, j % 2, :]
                        pe.matmul(b[:, 0:SEQ], neg_tri, keep[:, 0:SEQ], start=False, stop=False, skip_group_check=True)
                        pe.matmul(b[:, P:SEQ], neg_ones, keep[:, SEQ:TRI], start=False, stop=False, skip_group_check=True)
                        pe.matmul(b[:, SEQ:TRI], neg_tri, keep[:, SEQ:TRI], start=False, stop=True,
                                  skip_group_check=True).then_inc(sb_summed, 1)
                        pe.wait_ge(fox_prob, n + 1)
                        if j >= 1:
                            pe.wait_ge(fox_pt, n)
                        for m in range(3):
                            ins = pe.transpose(banks[:, 5, m * P:(m + 1) * P], fox_p[:, j % 2, m * P:(m + 1) * P], ident)
                        ins.then_inc(fox_turned, 1)
                    if i >= 2:
                        j, n = i - 2, HEADS * layer + i - 2
                        out_rows, pairs = slice(HD * (j % 2), HD * (j % 2) + HD), PAIRS * layer + j // 2
                        for kind, b, wt, ready, moved, done in ((0, 7, sb_w, sb_wt, sb_mix, sb_out),
                                                                (1, 6, fox_pT, fox_pt, fox_mix, fox_out)):
                            pe.wait_ge(ready, n + 1)
                            if j >= 2 and j % 2 == 0:
                                pe.wait_ge(moved, pairs)
                            o = banks[out_rows, b, :]
                            v0, v1 = (vals[:, t, kind * MIX + j * HD:kind * MIX + (j + 1) * HD] for t in range(TT))
                            pe.matmul(o[:, 0:SEQ], v0, wt[:, j % 2, 0:SEQ], start=True, stop=False, skip_group_check=True)
                            pe.matmul(o[:, P:SEQ], v1, wt[:, j % 2, SEQ:TRI], start=False, stop=True,
                                      skip_group_check=True).then_inc(done, 1)
                pe.wait_ge(sb_mix, PAIRS * (layer + 1))
                pe.wait_ge(fox_mix, PAIRS * (layer + 1))

            def xa_heads(layer):
                wait_moved(pe, after(layer, "xq"))
                for i in range(XH + 2):
                    if i < XH:
                        n = XH * layer + i
                        if i >= 2:
                            pe.wait_ge(xa_exp, n - 1)
                        for t in range(TT):
                            for k in range(2):
                                ins = pe.matmul(banks[:, i % 2, t * SEQ:(t + 1) * SEQ], xqT[:, 2 * i + k, t * P:(t + 1) * P],
                                                xkT[:, 2 * i + k, :], start=(t == 0 and k == 0), stop=(k == 1),
                                                skip_group_check=True)
                        ins.then_inc(xa_scored, 1)
                    if 1 <= i <= XH:
                        j, n = i - 1, XH * layer + i - 1
                        pe.wait_ge(xa_prob, n + 1)
                        if j >= 2:
                            pe.wait_ge(xa_pt, n - 1)
                        for m in range(TT):
                            for t in range(TT):
                                ins = pe.transpose(banks[:, 2 + j % 2, m * SEQ + t * P:m * SEQ + (t + 1) * P],
                                                   x_p[:, j % 2, t * SEQ + m * P:t * SEQ + (m + 1) * P], ident)
                        ins.then_inc(xa_turned, 1)
                    if i >= 2:
                        j, n = i - 2, XH * layer + i - 2
                        pe.wait_ge(xa_pt, n + 1)
                        if j >= 2:
                            pe.wait_ge(xa_mix, n - 1)
                        for d in range(2):
                            for m in range(TT):
                                ins = pe.matmul(banks[:, 4 + j % 2, d * SEQ:(d + 1) * SEQ],
                                                xval[:, m, (2 * j + d) * P:(2 * j + d + 1) * P],
                                                x_pT[:, j % 2, m * SEQ:(m + 1) * SEQ],
                                                start=(m == 0), stop=(m == TT - 1))
                        ins.then_inc(xa_out, 1)
                pe.wait_ge(xa_mix, XH * (layer + 1))

            def step(layer, s, n, hidden, tokens, width, begin):
                wait_step(pe, layer, s, n)
                for j in range(FPS):
                    b = banks[:, 4 + j, :]
                    for half in range(2):
                        wt = slot(s, half * KT * FFC, KT, FFC)
                        for k in range(KT):
                            ins = pe.matmul(b[:, half * SEQ:half * SEQ + width], wt[:, k, j * P:(j + 1) * P],
                                            tokens[:, k, 0:width], start=(k == 0), stop=(k == KT - 1))
                    ins.then_inc(hidden_full, 1)
                down = slot(s, 2 * KT * FFC, FPS, D)
                for j in range(FPS):
                    pe.wait_ge(hidden_ready, hidden + (j + 1))
                    for m in range(-(-width // P)):
                        cols = min(P, width)
                        for hh in range(2):
                            ins = pe.matmul(banks[0:cols, 2 * m + hh, :], hT[:, j, m * P:m * P + cols],
                                            down[:, j, hh * HALF:(hh + 1) * HALF], start=(begin and j == 0), stop=True,
                                            skip_group_check=True)
                ins.then_inc(steps_done, 1)

            def mixer(layer, done, hidden, tokens, width):
                for i in range(HEAD_STEPS):
                    step(layer, i, done(i), hidden + i * FPS, tokens, width, i == 0)
                with pe.Fori(0, 2) as r:
                    for j in range(SLOTS):
                        i = HEAD_STEPS + j
                        step(layer, i % SLOTS, done(i % SLOTS) + r + i // SLOTS,
                             hidden + r * (SLOTS * FPS) + i * FPS, tokens, width, False)

            def expert(layer, e, width):
                pe.wait_ge(place_ready, e * TT + TT)
                for d in range(KT):
                    if d >= 2:
                        pe.wait_ge(gather_dve if d % 2 else gather_act, e * (KT // 2) + d // 2)
                    for t in range(TT):
                        ins = pe.matmul(banks[:, 6 + d % 2, 0:width], xn[:, t, d * P:(d + 1) * P], place[:, t, 0:width],
                                        start=(t == 0), stop=(t == TT - 1))
                    ins.then_inc(gathered, 1)
                pe.wait_ge(gather_act, e * (KT // 2) + KT // 2)
                pe.wait_ge(gather_dve, e * (KT // 2) + KT // 2)
                pe.wait_ge(place_g_ready, e * TT + TT)
                for m in range(2):
                    for t in range(TT):
                        ins = pe.transpose(banks[:, 6, m * SEQ + t * P:m * SEQ + (t + 1) * P],
                                           place_g[:, t, m * P:(m + 1) * P], ident)
                ins.then_inc(spread_full, 1)
                mixer(layer, lambda s: e * STEP_USES[s], e * (STEPS * FPS) + hidden_before(layer), xg, width)
                pe.wait_ge(spread_ready, e + 1)
                pe.wait_ge(y_act, e + 2)
                pe.wait_ge(y_dve, e + 2)
                parts = -(-width // P)
                for j in range(4):
                    t, hh = j // 2, j % 2
                    for m in range(parts):
                        rows = min(P, width - m * P)
                        ins = pe.matmul(banks[:, 4 + j, :], spread[0:rows, m, t * P:(t + 1) * P],
                                        y_sb[0:rows, m, hh * HALF:(hh + 1) * HALF],
                                        start=(m == 0), stop=(m == parts - 1))
                    ins.then_inc(sum_full, 1)
                pe.wait_ge(sum_added, e * 4 + 4)

            def by_width(layer, e, tokens_here, widths):
                if len(widths) == 1:
                    expert(layer, e, widths[0])
                    return
                with pe.If(tokens_here < widths[0] + 1):
                    expert(layer, e, widths[0])
                with pe.Else():
                    by_width(layer, e, tokens_here, widths[1:])

            pe.nop().then_inc(steps_done, 1)
            pe.wait_ge(consts_in, 16)
            pe.wait_ge(vectors_in, 5 * 16)
            pe.transpose(bank(0)[:, 0:G_ROWS], grow[0:G_ROWS, :], ident[0:G_ROWS, 0:G_ROWS]).then_inc(tile_full, 1)
            pe.wait_ge(small_in, SMALL_DMAS * 16)
            for layer in range(DEPTH):
                turn_stage(layer, "mixT", xn, xn_ready, TT * (3 * layer + 1))
                wait_moved(pe, after(layer, "mixT"))
                wt = unit(layer, 0, HEADS + D // 4)
                turned_out(tile(layer, "fu", 0), 0, HEADS, wt)
                turned_out(tile(layer, "fu", 1), HEADS, P, wt)
                turned_out(tile(layer, "fu", 2), HEADS + P, P, wt)
                turned_units(layer, "fqk", (1,), 2 * MIX)
                turned_units(layer, "sqk", (2,), 2 * MIX)
                wait_unit(pe, layer, 3)
                for i in range(COUNT["v"]):
                    wt = slot(3, (i % 2) * KT * MIX, KT, MIX)
                    rows_out(tile(layer, "v", i), xT, i // 2, wt, MIX)
                heads(layer)
                pe.wait_ge(pool_ready, layer + 1)
                for c in range(COUNT["pool"]):
                    pe.matmul(bank(tile(layer, "pool", c))[:, 0:SEQ], poolw[:, layer, c, :], pool_r[:, c, :],
                              start=True, stop=True).then_inc(tile_full, 1)
                wait_moved(pe, after(layer, "pool"))
                rows_units(layer, "out", (4, 5), mixT)
                turn_stage(layer, "memT", mem_n, mem_ready, TT)
                wait_moved(pe, after(layer, "memT"))
                turned_units(layer, "xk", (6, 7), HALF)
                rows_units(layer, "xv", (8, 9), xT)
                turn_stage(layer, "xaT", xn, xn_ready, TT * (3 * layer + 2))
                wait_moved(pe, after(layer, "xaT"))
                turned_units(layer, "xq", (10, 11), HALF)
                xa_heads(layer)
                rows_units(layer, "xo", (12, 13), mixT)
                turn_stage(layer, "ffT", xn, xn_ready, TT * (3 * layer + 3))
                wait_moved(pe, after(layer, "ffT"))
                if layer == 0:
                    mixer(0, lambda s: 0, 0, xT, SEQ)
                else:
                    for t in range(TT):
                        for k in range(KT):
                            ins = pe.matmul(banks[:, 7, t * 8:t * 8 + 8], xT[:, k, t * P:(t + 1) * P], router[:, k, :],
                                            start=(k == 0), stop=(k == KT - 1))
                    ins.then_inc(logits_full, 1)
                    pe.wait_ge(chosen_ready, TT)
                    before, all_rows = strict[:, 0:P], ones[:, 0:P]
                    for at, parts in ((0, ((before, 0),)), (8, ((all_rows, 0), (before, 1))),
                                      (16, ((all_rows, 0), (all_rows, 1)))):
                        for m, (mask, t) in enumerate(parts):
                            ins = pe.matmul(banks[:, 6, at:at + 8], mask, chosen[:, t, :],
                                            start=(m == 0), stop=(m == len(parts) - 1))
                    ins.then_inc(rank_full, 1)
                    pe.wait_ge(rank_ready, 1)
                    with pe.Fori(0, EXPERTS) as e:
                        tokens_here = pe.value_load(count_i[0:1, bass.ds(e, 1)], min_val=0, max_val=SEQ)
                        by_width(layer, e, tokens_here, WIDTHS)


_INS = ["x", "mem", "mix_norm_pre", "mix_norm_post", "w_in", "b_forget", "pool_w", "pool_scale", "w_out",
        "xa_norm_pre", "xa_norm_post", "mem_norm", "xa_wq", "xa_wkv", "xa_wo", "ffn_norm_pre", "ffn_norm_post",
        "dense_w_gate", "dense_w_up", "dense_w_down", "router_w", "moe_w_gate", "moe_w_up", "moe_w_down"]


def kernel(**inputs):
    import concourse.bacc as bacc
    from concourse.bass_utils import run_bass_kernel_spmd

    nc = bacc.Bacc("TRN2", target_bir_lowering=False, num_devices=1)
    arrays, aps = {}, {}
    for name in _INS:
        arr = np.ascontiguousarray(inputs[name])
        arrays[f"in_{name}_dram"] = arr
        aps[name] = nc.dram_tensor(f"in_{name}_dram", arr.shape, mybir.dt.from_np(arr.dtype), kind="ExternalInput").ap()
    table = constants()
    arrays["in_constants_dram"] = table
    consts = nc.dram_tensor("in_constants_dram", table.shape, F32, kind="ExternalInput").ap()
    out = nc.dram_tensor("out_0_dram", (1, SEQ, D), F32, kind="ExternalOutput").ap()
    build(nc, aps, out, consts)
    r = run_bass_kernel_spmd(nc, [arrays], core_ids=[0])
    return r.results[0]["out_0_dram"]
```

```python
from contextlib import ExitStack, nullcontext

import numpy as np

import concourse.bass as bass
from concourse import mybir

ALU = mybir.AluOpType
ACT = mybir.ActivationFunctionType
AX_X = mybir.AxisListType.X
F32 = mybir.dt.float32
F32R = mybir.dt.float32r
I32 = mybir.dt.int32
U32 = mybir.dt.uint32

P = 128
D = 1024
SEQ = 256
DEPTH = 2
KT = D // P
TT = SEQ // P
HD = 64
HEADS = 6
MIX = HEADS * HD
PAIRS = HEADS // 2
XH = 4
XHD = D // XH
FF = 2816
FFC = 256
STEPS = FF // FFC
FPS = FFC // P
EXPERTS = 8
WINDOWS = (2, 4, 8, 16)
PAD = WINDOWS[-1]
SMALL_DMAS = 3 + DEPTH * len(WINDOWS)
HALF = 512
BANKS = 8
LOW = -1.0e30
TRI = P + SEQ

RAW = 6
SPLIT = 3
PIECE = KT * FFC
PIECE_DMAS = 2
NORMS = 7
PIECES = 30
MIXER = 3 * STEPS

STAGES = [("mixT", 4), ("f", 1), ("u", 2), ("fqk", 6), ("sqk", 6), ("v", 6), ("pool", 2), ("out", 8),
          ("memT", 4), ("xk", 8), ("xv", 8), ("xaT", 4), ("xq", 8), ("xo", 8), ("ffT", 4)]
COUNT = dict(STAGES)
FIRST = {name: sum(c for _, c in STAGES[:i]) for i, (name, _) in enumerate(STAGES)}
SPLIT_STAGES = ("mixT", "pool", "memT", "xaT", "ffT")
PIECE_STAGES = ("u", "fqk", "sqk", "v", "out", "xk", "xv", "xq", "xo")
PIECE_TILES = [(name, i) for name in PIECE_STAGES for i in range(0, COUNT[name], 2)]
assert len(PIECE_TILES) == PIECES
PER_LAYER = sum(c for _, c in STAGES)


def movers():
    who = [0]
    for _ in range(DEPTH):
        for name, count in STAGES:
            who += [1] * count if name in SPLIT_STAGES else [(j + 1) % 2 for j in range(count)]
    return who


MOVER = movers()

C_IDENT, C_TRI, C_NEG, C_ONES = 0, 128, 256, 384
C_STRICT, C_MIN, C_CAUSAL = 640, 1024, 1408
C_IOTA, C_INV, C_EPS, C_END = 1792, 2048, 2560, 2561

G_MIX, G_XA, G_MEM, G_FF, G_POOL, G_ROWS = 0, 16, 32, 48, 64, 68


GAIN_OF = {"mixT": G_MIX, "xaT": G_XA, "memT": G_MEM, "ffT": G_FF}


def constants():
    c = np.zeros((P, C_END), np.float32)
    i, j = np.arange(P)[:, None], np.arange(P)[None, :]
    c[:, C_IDENT:C_IDENT + P] = i == j
    c[:, C_TRI:C_TRI + P] = -1.0 * (i >= j)
    c[:, C_NEG:C_NEG + P] = -1.0
    c[:, C_ONES:C_ONES + SEQ] = 1.0
    c[:, C_STRICT:C_STRICT + TRI] = 1.0
    for b in (0, SEQ):
        c[:, C_STRICT + b:C_STRICT + b + P] = i < j
        c[:, C_MIN + b:C_MIN + b + P] = np.where(i < j, 0.0, LOW)
        c[:, C_CAUSAL + b:C_CAUSAL + b + P] = np.where(j <= i, 0.0, LOW)
    c[:, C_IOTA:C_IOTA + SEQ] = np.arange(SEQ)
    for g, w in enumerate(WINDOWS):
        col = C_INV + SEQ * (g // 2)
        c[64 * (g % 2):64 * (g % 2) + 64, col:col + SEQ] = 1.0 / np.minimum(np.arange(SEQ) + 1, w)
    c[:, C_EPS] = 1e-6
    return c


def build(nc, a, out, consts_dram):
    with ExitStack() as ctx:
        def sb(name, shape, dt=F32):
            return ctx.enter_context(nc.sbuf_tensor(name, shape, dt))

        def sem(name):
            return ctx.enter_context(nc.semaphore(name))

        banks = ctx.enter_context(nc.psum_tensor("banks", [P, BANKS, HALF], F32))

        raw = sb("raw", [P, RAW, PIECE])
        w_high = sb("w_high", [P, SPLIT, PIECE], F32R)
        w_low = sb("w_low", [P, SPLIT, PIECE], F32R)
        h_res = sb("h_res", [P, TT, D])
        xn = sb("xn", [P, TT, D])
        x_high = sb("x_high", [P, KT, SEQ], F32R)
        x_low = sb("x_low", [P, KT, SEQ], F32R)
        mix_high = sb("mix_high", [P, KT, SEQ], F32R)
        mix_low = sb("mix_low", [P, KT, SEQ], F32R)
        res = sb("res", [P, TT, D])
        cst = sb("cst", [P, C_END])
        phase = sb("phase", [P, 9216])
        hT_high = sb("hT_high", [P, FPS, SEQ], F32R)
        hT_low = sb("hT_low", [P, FPS, SEQ], F32R)
        gcols = sb("gcols", [P, G_ROWS])
        stats = sb("stats", [P, 3, 2 * NORMS * DEPTH])
        small = sb("small", [P, 272])
        count_i = sb("count_i", [P, EXPERTS], I32)
        topi = sb("topi", [P, TT, 8], U32)
        poolw = sb("poolw", [P, DEPTH, 2, P])
        w_forget = sb("w_forget", [P, DEPTH, KT, HEADS])

        ident = cst[:, C_IDENT:C_IDENT + P]
        neg_tri = cst[:, C_TRI:C_TRI + P]
        neg_ones = cst[:, C_NEG:C_NEG + P]
        ones = cst[:, C_ONES:C_ONES + SEQ]
        strict = cst[:, C_STRICT:C_STRICT + TRI]
        low_min = cst[:, C_MIN:C_MIN + TRI]
        causal = cst[:, C_CAUSAL:C_CAUSAL + TRI]
        iota = cst[:, C_IOTA:C_IOTA + SEQ]
        inv_count = cst[:, C_INV:C_INV + 2 * SEQ].rearrange("p (c t) -> p c t", c=2)
        eps = cst[:, C_EPS:C_EPS + 1]

        def view(t, at, *dims):
            n = int(np.prod(dims))
            flat = t[:, at:at + n]
            if len(dims) == 1:
                return flat
            if len(dims) == 2:
                return flat.rearrange("p (a b) -> p a b", a=dims[0])
            return flat.rearrange("p (a b c) -> p a b c", a=dims[0], b=dims[1])

        def plain(t):
            return t.bitcast(F32)

        x_high_f, x_low_f = plain(x_high[:, :, :]), plain(x_low[:, :, :])

        qkT = view(phase, 0, 12, SEQ)
        vals = view(phase, 3072, TT, 2 * MIX)
        fox_p = view(phase, 4608, 2, TRI)
        fox_pT = view(phase, 5376, 2, TRI)
        sb_l = view(phase, 6144, 2, TRI)
        sb_keep = view(phase, 6912, 2, TRI)
        sb_w = view(phase, 7680, 2, TRI)
        forget = view(phase, 8448, 3, SEQ)
        mem_n = view(phase, 0, TT, D)
        xkT = view(phase, 0, KT, SEQ)
        xval = view(phase, 2048, TT, D)
        xqT = view(phase, 4096, KT, SEQ)
        x_p = view(phase, 6144, 2, TT * SEQ)
        x_pT = view(phase, 7168, 2, TT * SEQ)
        y_sb = view(phase, 0, 2, D)
        silu_g = view(phase, 2048, 2, FFC)
        hidden = view(phase, 2560, 2, FFC)
        place = view(phase, 3072, TT, SEQ)
        place_g = view(phase, 3584, TT, SEQ)
        spread = view(phase, 4096, 2, SEQ)
        gpost = phase[:, 8192:9216]
        grow = phase[:, 0:P]
        flat_xn = xn[:, :, :].rearrange("p t d -> p (t d)")
        decay_q = view(flat_xn, 0, HEADS, SEQ)
        decay_k = flat_xn[:, HEADS * SEQ:(HEADS + 1) * SEQ]
        flat_res = res[:, :, :].rearrange("p t d -> p (t d)")
        u_pad = view(flat_res, 0, 2, PAD + SEQ)
        run_a = flat_res[:, 544:816]
        run_b = flat_res[:, 816:1088]
        pool_r = view(flat_res, 1088, 2, SEQ)

        fox_nmax = view(small, 0, 2, 2)
        fox_sum = view(small, 4, 2, 2)
        fox_inv = view(small, 8, 2, 2)
        x_nmax = view(small, 12, 2, 2)
        x_sum = view(small, 16, 2, 2)
        x_inv = view(small, 20, 2, 2)
        x_max = view(small, 24, 2, 2)
        bias_f = view(small, 28, DEPTH)
        logits = view(small, 32, TT, 8)
        top = view(small, 48, TT, 8)
        topf = view(small, 64, TT, 8)
        first = view(small, 80, TT, 8)
        second = view(small, 96, TT, 8)
        chosen_wide = view(small, 112, TT, 16)
        chosen = chosen_wide[:, :, 0:8]
        gate = view(small, 144, TT, 8)
        rank_wide = view(small, 160, TT, 16)
        rank = rank_wide[:, :, 0:8]
        gap = view(small, 192, TT)
        egap = view(small, 194, TT)
        gate1 = view(small, 196, TT)
        gate2 = view(small, 198, TT)
        router = view(small, 208, KT, 8)
        fox_max = view(small, 200, 2, 2)

        consts_in = sem("consts_in")
        x_in = sem("x_in")
        mem_in = sem("mem_in")
        vectors_in = sem("vectors_in")
        small_in = sem("small_in")
        gpost_in = sem("gpost_in")
        raw_in = [sem(f"raw_in{s}") for s in range(RAW)]
        high_ready = sem("high_ready")
        low_ready = sem("low_ready")
        act_step = sem("act_step")
        dve_step = sem("dve_step")
        pool_step = sem("pool_step")
        tile_full = sem("tile_full")
        tile_high = sem("tile_high")
        tile_act = sem("tile_act")
        tile_dve = sem("tile_dve")
        rms_ready = sem("rms_ready")
        mem_ready = sem("mem_ready")
        xn_ready = sem("xn_ready")
        h_ready = sem("h_ready")
        forget_log = sem("forget_log")
        decay_set = sem("decay_set")
        decay_ready = sem("decay_ready")
        pool_ready = sem("pool_ready")
        fox_scored, fox_masked, fox_exp, fox_prob, fox_turned, fox_pt, fox_out, fox_high, fox_mix = (
            sem(f"fox_{n}") for n in ("scored", "masked", "exp", "prob", "turned", "pt", "out", "high", "mix"))
        sb_scored, sb_soft, sb_kept, sb_summed, sb_logw, sb_wt, sb_out, sb_high, sb_mix = (
            sem(f"sb_{n}") for n in ("scored", "soft", "kept", "summed", "logw", "wt", "out", "high", "mix"))
        xa_scored, xa_max, xa_exp, xa_prob, xa_turned, xa_pt, xa_out, xa_high, xa_mix = (
            sem(f"xa_{n}") for n in ("scored", "max", "exp", "prob", "turned", "pt", "out", "high", "mix"))
        mixed = sem("mixed")
        silu_ready = sem("silu_ready")
        hidden_ready = sem("hidden_ready")
        hidden_turned = sem("hidden_turned")
        hT_half, hT_ready = sem("hT_half"), sem("hT_ready")
        y_act, y_dve = sem("y_act"), sem("y_dve")
        logits_full = sem("logits_full")
        gap_ready, gap_exp = sem("gap_ready"), sem("gap_exp")
        chosen_ready = sem("chosen_ready")
        rank_full, rank_ready = sem("rank_full"), sem("rank_ready")
        place_ready, place_g_ready = sem("place_ready"), sem("place_g_ready")
        gathered, gather_high, gather_low = sem("gathered"), sem("gather_high"), sem("gather_low")
        spread_full, spread_ready = sem("spread_full"), sem("spread_ready")
        sum_full, sum_added = sem("sum_full"), sem("sum_added")
        out_done = sem("out_done")

        SUM_BANKS = (6, 7, 0, 1)

        def tile(layer, stage, i=0):
            return 1 + PER_LAYER * layer + FIRST[stage] + i

        def after(layer, stage):
            return tile(layer, stage) + COUNT[stage]

        def wait_moved(eng, n):
            for who, moved in enumerate((tile_act, tile_dve)):
                count = MOVER[:n].count(who)
                if count:
                    eng.wait_ge(moved, count)

        def highs_before(n):
            names = [None] + DEPTH * [name for name, count in STAGES for _ in range(count)]
            return sum(name in SPLIT_STAGES for name in names[:n])

        def first_piece(layer):
            return layer * (PIECES + MIXER)

        def before_mixer(layer):
            return PIECES * (layer + 1)

        def wait_used(eng, layer, c, r):
            start = first_piece(layer)
            p = c - start - SPLIT
            if p < 0:
                if layer:
                    eng.wait_ge(mixed, layer * MIXER + p + 1)
                return
            if p < PIECES:
                stage, i = PIECE_TILES[p]
                eng.wait_ge(tile_full, tile(layer, stage, i) + 2)
            if p >= PIECES or not isinstance(r, int):
                eng.wait_ge(mixed, r * RAW + (c - SPLIT - before_mixer(layer) + 1))

        def weights(at, *dims):
            return view(w_high[:, at, :], 0, *dims), view(w_low[:, at, :], 0, *dims)

        def norm(layer, j):
            return NORMS * layer + (j + 1 if j else 0)

        def split_tile(layer, stage, i):
            src = banks[:, tile(layer, stage, i) % BANKS, :]
            if stage == "pool":
                g, d = G_POOL + 2 * layer + i, 2 * PAIRS + i
                return [(mix_high[:, d, :], src[:, 0:SEQ], gcols[:, g:g + 1], mix_low[:, d, :])]
            parts = []
            for j in range(2):
                d = 2 * i + j
                g = GAIN_OF[stage] + KT * layer + d
                parts.append((x_high[:, d, :], src[:, j * SEQ:(j + 1) * SEQ], gcols[:, g:g + 1], x_low[:, d, :]))
            return parts

        def plain_tile(move, layer, stage, i):
            src = banks[:, tile(layer, stage, i) % BANKS, 0:SEQ]
            cols = slice(i // 2 * FFC, (i // 2 + 1) * FFC)
            if stage == "f":
                return move(forget[0:HEADS, 0, :], src[0:HEADS, :])
            if stage == "u":
                return move(u_pad[:, i, PAD:], src)
            if stage in ("fqk", "sqk"):
                return move(qkT[:, (0 if stage == "fqk" else 2 * PAIRS) + i, :], src, HD ** -0.5 if i < PAIRS else 1.0)
            if stage == "xk":
                return move(xkT[:, i, :], src)
            if stage == "xq":
                return move(xqT[:, i, :], src, XHD ** -0.5)
            dst = {"v": vals, "xv": xval, "out": res, "xo": res}[stage]
            return move(dst[:, i % 2, cols], src)

        def always(eng):
            return nullcontext()

        def w(name, layer):
            return a[name][layer].rearrange("(k p) n -> p k n", p=P)

        block = ctx.enter_context(nc.Block())

        @block.sync
        def _(sp):
            sp.dma_start(h_res[:, :, :], a["x"][0].rearrange("(t p) d -> p t d", p=P)).then_inc(x_in, 16)
            sp.dma_start(cst[:, :], consts_dram).then_inc(consts_in, 16)
            for i, name in enumerate(("mix_norm_pre", "xa_norm_pre", "mem_norm", "ffn_norm_pre")):
                sp.dma_start(grow[16 * i:16 * i + 16, :],
                             a[name].rearrange("l (k p) -> (l k) p", p=P)).then_inc(vectors_in, 16)
            sp.dma_start(grow[G_POOL:G_ROWS, :],
                         a["pool_scale"].rearrange("l (k p) -> (l k) p", p=P)).then_inc(vectors_in, 16)

            def load_gpost(layer, q):
                if q == 0:
                    sp.wait_ge(sb_mix, PAIRS * (layer + 1))
                    sp.wait_ge(fox_mix, PAIRS * (layer + 1))
                else:
                    sp.wait_ge(h_ready, TT * (3 * layer + q))
                name = ("mix_norm_post", "xa_norm_post", "ffn_norm_post")[q]
                sp.dma_start(gpost, a[name][layer:layer + 1, :].to_broadcast([P, D])).then_inc(gpost_in, 16)

            def load(c, r, parts):
                if c >= RAW:
                    sp.wait_ge(low_ready, r * RAW + (c - RAW + 1))
                for dst, src in parts:
                    sp.dma_start(dst, src).then_inc(raw_in[c % RAW], 16)

            def columns(c, src):
                dst = view(raw[:, c % RAW, :], 0, KT, FFC)
                half = KT // 2
                return [(dst[:, k:k + half, :], src[:, k:k + half, :]) for k in (0, half)]

            def unit(layer, p):
                c = first_piece(layer) + p
                stage, i = PIECE_TILES[p]
                at = i // 2 * FFC
                name, at = {"u": ("w_in", 6 * MIX + HEADS), "fqk": ("w_in", 3 * MIX + at), "sqk": ("w_in", at),
                            "v": ("w_in", 2 * MIX + at), "out": ("w_out", at), "xk": ("xa_wkv", at),
                            "xv": ("xa_wkv", D + at), "xq": ("xa_wq", at), "xo": ("xa_wo", at)}[stage]
                if stage != "v" or i == 0:
                    return load(c, 0, columns(c, w(name, layer)[:, :, at:at + FFC]))
                if i == 4:
                    return load(c, 0, columns(c, w(name, layer)[:, :, 5 * MIX + P:6 * MIX]))
                dst = view(raw[:, c % RAW, :], 0, KT, FFC)
                load(c, 0, [(dst[:, :, 0:P], w(name, layer)[:, :, at:at + P]),
                            (dst[:, :, P:FFC], w(name, layer)[:, :, 5 * MIX:5 * MIX + P])])

            def mixer(gate_w, up_w, down_w, c, r):
                gate_w, up_w = (m.rearrange("(k p) n -> p k n", p=P) for m in (gate_w, up_w))

                def pair(c, r, at):
                    for j, m in enumerate((gate_w, up_w)):
                        load(c + j, r, columns(c + j, m[:, :, bass.ds(at, FFC)]))

                def down(c, r, at):
                    dst = view(raw[:, c % RAW, :], 0, FPS, D)
                    src = down_w[bass.ds(at, FFC), :].rearrange("(t p) n -> p t n", p=P)
                    load(c, r, [(dst[:, t, :], src[:, t, :]) for t in range(FPS)])

                pair(c, r, 0)
                with sp.Fori(0, (STEPS - 1) // 2) as n:
                    for j in range(2):
                        pair(c + 2 + 3 * j, r + n, n * (2 * FFC) + (j + 1) * FFC)
                        down(c + 4 + 3 * j, r + n, n * (2 * FFC) + j * FFC)
                down(c + MIXER - 1, r, (STEPS - 1) * FFC)

            for layer in range(DEPTH):
                for p in range(PIECES):
                    if p == 14:
                        load_gpost(layer, 0)
                        sp.dma_start(mem_n[:, :, :], a["mem"][0].rearrange("(t p) d -> p t d", p=P)).then_inc(mem_in, 16)
                    if p == 26:
                        load_gpost(layer, 1)
                    unit(layer, p)
                c = first_piece(layer) + PIECES
                if layer == 0:
                    mixer(a["dense_w_gate"][0], a["dense_w_up"][0], a["dense_w_down"][0], c, 0)
                else:
                    with sp.Fori(0, EXPERTS // 2) as q:
                        for j in range(2):
                            one = bass.ds(q * 2 + j, 1)
                            mixer(*(a[m][0][one].rearrange("a d f -> (a d) f")
                                           for m in ("moe_w_gate", "moe_w_up", "moe_w_down")),
                                  c + MIXER * j, q * (2 * MIXER // RAW))
                load_gpost(layer, 2)
            sp.wait_ge(out_done, 16)

        @block.gpsimd
        def _(pool):
            steps = [0]

            def chain(ins):
                steps[0] += 1
                ins.then_inc(pool_step, 1)
                pool.wait_ge(pool_step, steps[0])

            with nc.allow_non_contiguous_dma(reason="two small vectors"):
                pool.dma_start(w_forget[:, :, :, :].rearrange("p l k h -> p (l k) h"),
                               a["w_in"].rearrange("l (k p) n -> p (l k) n", p=P)[:, :, 6 * MIX:6 * MIX + HEADS]
                               ).then_inc(small_in, 16)
                pool.dma_start(bias_f[0:HEADS, :], a["b_forget"].rearrange("l h -> h l")).then_inc(small_in, 16)
                pool.dma_start(router[:, :, :], a["router_w"][0].rearrange("(k p) e -> p k e", p=P)).then_inc(small_in, 16)
            chain(pool.memset(poolw[:, :, :, :], 0.0))
            for layer in range(DEPTH):
                for g in range(len(WINDOWS)):
                    r0 = 64 * (g % 2)
                    pool.dma_start(poolw[r0:r0 + 64, layer, g // 2, r0:r0 + 64],
                                   a["pool_w"][layer, g]).then_inc(small_in, 16)
            pool.wait_ge(consts_in, 16)
            for layer in range(DEPTH):
                wait_moved(pool, after(layer, "mixT"))
                chain(pool.memset(flat_xn[:, 0:(HEADS + 1) * SEQ], 0.0))
                for h in range(HEADS):
                    chain(pool.tensor_scalar(decay_q[32:32 + HEADS, h, :], ones[32:32 + HEADS, :],
                                             ident[32:32 + HEADS, 32 + h:33 + h], None, ALU.mult))
                pool.memset(decay_k[0:HEADS, :], 1.0).then_inc(decay_set, 1)
                pool.wait_ge(decay_set, layer + 1)
                chain(pool.memset(u_pad[:, :, 0:PAD], 0.0))
                wait_moved(pool, after(layer, "u"))
                for c in range(2):
                    u = u_pad[:, c, :]
                    end = PAD + SEQ

                    def wider(dst, src, shift):
                        lo = 2 * shift - 1
                        chain(pool.tensor_tensor(dst[:, lo:end], src[:, lo:end], src[:, lo - shift:end - shift], ALU.add))

                    wider(run_a, u, 1)
                    wider(run_b, run_a, 2)
                    if c == 1:
                        wider(run_a, run_b, 4)
                        wider(run_b, run_a, 8)
                    for half, src in enumerate((run_a, run_b)):
                        rows = slice(64 * half, 64 * half + 64)
                        chain(pool.tensor_tensor(pool_r[rows, c, :], src[rows, PAD:end], inv_count[rows, c, :], ALU.mult))
                        ins = pool.tensor_tensor(pool_r[rows, c, :], pool_r[rows, c, :], u[rows, PAD:end], ALU.subtract)
                        chain(ins)
                pool.engine_nop().then_inc(pool_ready, 1)

        @block.scalar
        def _(act):
            steps = [0]

            def chain(ins):
                steps[0] += 1
                ins.then_inc(act_step, 1)
                act.wait_ge(act_step, steps[0])

            def move(out_, in_, scale=1.0):
                return act.activation(out_, in_, ACT.Copy, scale=scale)

            def split(layer, c, r=0):
                wait_used(act, layer, c, r)
                act.wait_ge(raw_in[c % RAW], (r + c // RAW + 1) * (16 * PIECE_DMAS))
                move(w_high[:, c % SPLIT, :], raw[:, c % RAW, :]).then_inc(high_ready, 1)

            def rms(n, src, arrived):
                for t in range(TT):
                    arrived(t)
                    chain(act.activation(xn[:, t, :], src[:, t, :], ACT.Square, accum_out=stats[:, 0, 2 * n + t:2 * n + t + 1]))
                pair = slice(2 * n, 2 * n + 2)
                chain(act.activation(stats[:, 1, pair], stats[:, 0, pair], ACT.Ln, bias=eps, scale=1.0 / D))
                act.activation(stats[:, 2, pair], stats[:, 1, pair], ACT.Exp, scale=-0.5).then_inc(rms_ready, 1)

            def pre(layer, q):
                def arrived(t):
                    if layer == 0 and q == 0:
                        act.wait_ge(x_in, 16)
                    else:
                        act.wait_ge(h_ready, TT * (3 * layer + q - 1) + t + 1)
                rms(norm(layer, 2 * q), h_res, arrived)

            def post(layer, q):
                def arrived(t):
                    if q < 2:
                        wait_moved(act, after(layer, ("out", "xo")[q]))
                    elif layer == 0:
                        act.wait_ge(y_act, 1)
                        act.wait_ge(y_dve, 1)
                    else:
                        act.wait_ge(sum_added, 4 * EXPERTS)
                rms(norm(layer, 2 * q + 1), res, arrived)

            def take(layer, stage, i):
                n = tile(layer, stage, i)
                if stage in SPLIT_STAGES:
                    act.wait_ge(tile_full, n + 1)
                    for dst, src, gain, _ in split_tile(layer, stage, i):
                        ins = move(dst, src, gain)
                    ins.then_inc(tile_high, 1)
                elif MOVER[n] == 0:
                    act.wait_ge(tile_full, n + 1)
                    plain_tile(move, layer, stage, i).then_inc(tile_act, 1)

            def memory(layer):
                rms(norm(layer, 0) + 1, mem_n, lambda t: act.wait_ge(mem_in, 16 * (layer + 1)))

            def take_all(layer, stage):
                for i in range(COUNT[stage]):
                    take(layer, stage, i)
                    if stage == "out" and i == COUNT[stage] // 2:
                        memory(layer)
                    if stage in PIECE_STAGES and i % 2 == 1:
                        split(layer, first_piece(layer) + PIECE_TILES.index((stage, i - 1)) + SPLIT)

            def heads(layer):
                for i in range(HEADS + 2):
                    if i < HEADS:
                        n = HEADS * layer + i
                        act.wait_ge(sb_scored, n + 1)
                        z = banks[:, 2 + i % 3, 0:TRI]
                        chain(act.activation(sb_l[:, i % 2, :], z, ACT.Abs))
                        chain(act.activation(sb_l[:, i % 2, :], sb_l[:, i % 2, :], ACT.Exp, scale=-1.0))
                        act.activation(sb_l[:, i % 2, :], sb_l[:, i % 2, :], ACT.Ln, bias=1.0).then_inc(sb_soft, 1)
                        act.wait_ge(fox_masked, n + 1)
                        for t, cols in enumerate((slice(0, P), slice(P, TRI))):
                            ins = act.activation(fox_p[:, i % 2, cols], fox_p[:, i % 2, cols], ACT.Exp,
                                                 bias=fox_nmax[:, i % 2, t:t + 1], accum_out=fox_sum[:, i % 2, t:t + 1])
                        ins.then_inc(fox_exp, 1)
                    if 1 <= i <= HEADS:
                        j, n = i - 1, HEADS * layer + i - 1
                        act.wait_ge(sb_logw, n + 1)
                        act.activation(sb_w[:, j % 2, :], sb_w[:, j % 2, :], ACT.Exp).then_inc(sb_wt, 1)
                        act.wait_ge(fox_turned, n + 1)
                        move(fox_pT[:, j % 2, :], banks[:, 5, 0:TRI]).then_inc(fox_pt, 1)
                    if i >= 2 and i % 2 == 1:
                        pair = (i - 3) // 2
                        act.wait_ge(sb_out, HEADS * layer + 2 * pair + 2)
                        move(mix_high[:, pair, :], banks[:, 7, 0:SEQ]).then_inc(sb_high, 1)
                        act.wait_ge(fox_out, HEADS * layer + 2 * pair + 2)
                        move(mix_high[:, PAIRS + pair, :], banks[:, 6, 0:SEQ]).then_inc(fox_high, 1)

            def xa_heads(layer):
                for i in range(XH + 2):
                    if i < XH:
                        n = XH * layer + i
                        act.wait_ge(xa_max, n + 1)
                        if i >= 2:
                            act.wait_ge(xa_turned, n - 1)
                        for t in range(TT):
                            cols = slice(t * SEQ, t * SEQ + SEQ)
                            ins = act.activation(x_p[:, i % 2, cols], banks[:, i % 2, cols], ACT.Exp,
                                                 bias=x_nmax[:, i % 2, t:t + 1], accum_out=x_sum[:, i % 2, t:t + 1])
                        ins.then_inc(xa_exp, 1)
                    if 1 <= i <= XH:
                        j, n = i - 1, XH * layer + i - 1
                        act.wait_ge(xa_turned, n + 1)
                        move(x_pT[:, j % 2, :], banks[:, 2 + j % 2, :]).then_inc(xa_pt, 1)
                    if i >= 2:
                        j, n = i - 2, XH * layer + i - 2
                        act.wait_ge(xa_out, n + 1)
                        move(mix_high[:, 2 * j:2 * j + 2, :].rearrange("p a b -> p (a b)"),
                             banks[:, 4 + j % 2, :]).then_inc(xa_high, 1)

            def turned(n):
                act.wait_ge(hidden_turned, n + 1)
                move(hT_high[:, :, :].rearrange("p a b -> p (a b)"), banks[:, 6, :]).then_inc(hT_half, 1)

            def step(layer, c, r, n, halves=(0, 1, 2), spread_of=None):
                split(layer, c + SPLIT, r)
                act.wait_ge(mixed, r * RAW + (c + 2 - before_mixer(layer)))
                act.activation(silu_g[:, :, :], banks[:, 4:6, 0:FFC], ACT.Silu).then_inc(silu_ready, 1)
                for k in halves[1:]:
                    split(layer, c + k + SPLIT, r)
                if spread_of is not None:
                    act.wait_ge(spread_full, spread_of + 1)
                    move(spread[:, :, :].rearrange("p a b -> p (a b)"), banks[:, 7, :]).then_inc(spread_ready, 1)
                turned(n)

            def gather(layer, e):
                for i in range(COUNT["ffT"]):
                    act.wait_ge(gathered, e * COUNT["ffT"] + (i + 1))
                    for j in range(2):
                        d = 2 * i + j
                        g = G_FF + KT * layer + d
                        ins = move(x_high[:, d, :], banks[:, 7 - i % 2, j * SEQ:(j + 1) * SEQ], gcols[:, g:g + 1])
                    ins.then_inc(gather_high, 1)

            def mixer(layer, c, r, e, y, more):
                n = e * STEPS + layer * STEPS
                step(layer, c, r, n, (0, 1), e if layer else None)
                with act.Fori(0, (STEPS - 3) // 2) as k:
                    for j in range(2):
                        step(layer, c + 2 + 3 * j, r + k, k * 2 + (n + (1 + j)))
                c = c + 3 * (STEPS - 2) - 1
                step(layer, c, r, n + (STEPS - 2))
                last_step(layer, c + SPLIT, r, n + (STEPS - 1), e, y, more)

            def last_step(layer, c, r, n, e, y, more):
                split(layer, c + SPLIT, r)
                act.wait_ge(mixed, r * RAW + (c + 2 - before_mixer(layer)))
                act.activation(silu_g[:, :, :], banks[:, 4:6, 0:FFC], ACT.Silu).then_inc(silu_ready, 1)
                with more(act):
                    split(layer, c + 1 + SPLIT, r)
                    split(layer, c + 2 + SPLIT, r)
                turned(n)
                if layer:
                    with more(act):
                        gather(layer, e + 1)
                act.wait_ge(mixed, r * RAW + (c + 4 - before_mixer(layer)))
                move(y, banks[:, 0:2, :].rearrange("p a b -> p (a b)")).then_inc(y_act, 1)
                with more(act):
                    split(layer, c + 3 + SPLIT, r)

            act.wait_ge(consts_in, 16)
            for layer in range(DEPTH):
                act.preload_act_table_set("natural_log_exp_and_others")
                pre(layer, 0)
                if layer == 0:
                    act.wait_ge(tile_full, 1)
                    move(gcols[:, :], banks[:, 0, 0:G_ROWS]).then_inc(tile_act, 1)
                    act.wait_ge(tile_act, 1)
                    for c in range(SPLIT):
                        split(0, c)
                take_all(layer, "mixT")
                take_all(layer, "f")
                take_all(layer, "u")
                wait_moved(act, after(layer, "f"))
                act.wait_ge(small_in, SMALL_DMAS * 16)
                fl = forget[0:HEADS, 0, :]
                fa = forget[0:HEADS, 1, :]
                chain(act.activation(fa, fl, ACT.Abs, bias=bias_f[0:HEADS, layer:layer + 1]))
                chain(act.activation(fa, fa, ACT.Exp, scale=-1.0))
                act.activation(fa, fa, ACT.Ln, bias=1.0).then_inc(forget_log, 1)
                take_all(layer, "fqk")
                take_all(layer, "sqk")
                take_all(layer, "v")
                heads(layer)
                take_all(layer, "pool")
                take_all(layer, "out")
                post(layer, 0)
                pre(layer, 1)
                take_all(layer, "memT")
                take_all(layer, "xk")
                take_all(layer, "xv")
                take_all(layer, "xaT")
                take_all(layer, "xq")
                xa_heads(layer)
                take_all(layer, "xo")
                post(layer, 1)
                pre(layer, 2)
                take_all(layer, "ffT")
                c = first_piece(layer) + PIECES
                if layer == 0:
                    mixer(0, c, 0, 0, res[:, 0, :], always)
                else:
                    act.wait_ge(gap_ready, 1)
                    act.activation(egap[:, :], gap[:, :], ACT.Exp).then_inc(gap_exp, 1)
                    gather(layer, 0)
                    with act.Fori(0, EXPERTS // 2) as q:
                        r = q * (2 * MIXER // RAW)
                        mixer(layer, c, r, q * 2, y_sb[:, 0, :], always)
                        mixer(layer, c + MIXER, r, q * 2 + 1, y_sb[:, 0, :], lambda eng: eng.If(q < EXPERTS // 2 - 1))
                post(layer, 2)
            act.wait_ge(h_ready, TT * 3 * DEPTH)
            act.dma_start(out[0].rearrange("(t p) d -> p t d", p=P), h_res[:, :, :]).then_inc(out_done, 16)
            act.wait_ge(out_done, 16)

        @block.vector
        def _(dve):
            steps = [0]

            def chain(ins):
                steps[0] += 1
                ins.then_inc(dve_step, 1)
                dve.wait_ge(dve_step, steps[0])

            def inv_rms(n, t):
                return stats[:, 2, 2 * n + t:2 * n + t + 1]

            def pre(layer, q):
                n = norm(layer, 2 * q)
                dve.wait_ge(rms_ready, n + 1)
                for t in range(TT):
                    dve.tensor_scalar(xn[:, t, :], h_res[:, t, :], inv_rms(n, t), None, ALU.mult).then_inc(xn_ready, 1)

            def post(layer, q):
                n, p = norm(layer, 2 * q + 1), 3 * layer + q
                dve.wait_ge(rms_ready, n + 1)
                dve.wait_ge(gpost_in, 16 * (p + 1))
                for t in range(TT):
                    chain(dve.scalar_tensor_tensor(out=res[:, t, :], in0=res[:, t, :], scalar=inv_rms(n, t),
                                                   in1=gpost, op0=ALU.mult, op1=ALU.mult))
                    dve.tensor_tensor(h_res[:, t, :], h_res[:, t, :], res[:, t, :], ALU.add).then_inc(h_ready, 1)

            def move(out_, in_, scale=1.0):
                return dve.tensor_scalar(out_, in_, scale, None, ALU.mult)

            def low(out_, in_, high, gain=None):
                if gain is None:
                    return dve.tensor_tensor(out_, in_, plain(high), ALU.subtract)
                return dve.scalar_tensor_tensor(out=out_, in0=in_, scalar=gain, in1=plain(high), op0=ALU.mult,
                                                op1=ALU.subtract)

            def split(layer, c, r=0):
                dve.wait_ge(high_ready, r * RAW + (c + 1))
                low(w_low[:, c % SPLIT, :], raw[:, c % RAW, :], w_high[:, c % SPLIT, :]).then_inc(low_ready, 1)

            def take(layer, stage, i):
                n = tile(layer, stage, i)
                if stage in SPLIT_STAGES:
                    dve.wait_ge(tile_high, highs_before(n) + 1)
                    for high, src, gain, dst in split_tile(layer, stage, i):
                        ins = low(dst, src, high, gain)
                    ins.then_inc(tile_dve, 1)
                elif MOVER[n] == 1:
                    dve.wait_ge(tile_full, n + 1)
                    plain_tile(move, layer, stage, i).then_inc(tile_dve, 1)

            def memory(layer):
                n = norm(layer, 0) + 1
                dve.wait_ge(rms_ready, n + 1)
                for t in range(TT):
                    dve.tensor_scalar(mem_n[:, t, :], mem_n[:, t, :], inv_rms(n, t), None, ALU.mult).then_inc(mem_ready, 1)

            def take_all(layer, stage):
                for i in range(COUNT[stage]):
                    take(layer, stage, i)
                    if stage == "out" and i == COUNT[stage] // 2:
                        memory(layer)
                    if stage in PIECE_STAGES and i % 2 == 1:
                        split(layer, first_piece(layer) + PIECE_TILES.index((stage, i - 1)) + SPLIT)

            def decay(layer):
                fl, fa, fc = (forget[0:HEADS, r, :] for r in range(3))
                wait_moved(dve, after(layer, "f"))
                dve.wait_ge(small_in, SMALL_DMAS * 16)
                chain(dve.tensor_scalar(fc, fl, bias_f[0:HEADS, layer:layer + 1], 0.0, ALU.add, ALU.min))
                dve.wait_ge(forget_log, layer + 1)
                chain(dve.tensor_tensor(fl, fc, fa, ALU.subtract))
                chain(dve.tensor_tensor_scan(fc, ones[0:HEADS, :], fl, 0.0, ALU.mult, ALU.add))
                dve.wait_ge(decay_set, layer + 1)
                for h in range(HEADS):
                    dve.tensor_scalar(decay_q[0:HEADS, h, :], fc, ident[0:HEADS, h:h + 1], None, ALU.mult)
                dve.tensor_scalar(decay_k[32:32 + HEADS, :], fc, -1.0, None, ALU.mult).then_inc(decay_ready, 1)

            def heads(layer):
                for i in range(HEADS + 2):
                    if i < HEADS:
                        n = HEADS * layer + i
                        dve.wait_ge(fox_scored, n + 1)
                        if i >= 2:
                            dve.wait_ge(fox_turned, n - 1)
                        for t, cols in enumerate((slice(0, P), slice(P, TRI))):
                            chain(dve.tensor_tensor_reduce(out=fox_p[:, i % 2, cols], in0=banks[:, i % 2, cols],
                                                           in1=causal[:, cols], scale=1.0, scalar=3.0 * LOW, op0=ALU.add,
                                                           op1=ALU.max, accum_out=fox_max[:, i % 2, t:t + 1]))
                        dve.tensor_scalar(fox_nmax[:, i % 2, :], fox_max[:, i % 2, :], -1.0, None,
                                          ALU.mult).then_inc(fox_masked, 1)
                        dve.wait_ge(sb_soft, n + 1)
                        chain(dve.scalar_tensor_tensor(out=sb_keep[:, i % 2, :], in0=banks[:, 2 + i % 3, 0:TRI], scalar=0.0,
                                                       in1=sb_l[:, i % 2, :], op0=ALU.max, op1=ALU.add))
                        dve.tensor_tensor(sb_keep[:, i % 2, :], sb_keep[:, i % 2, :], strict, ALU.mult).then_inc(sb_kept, 1)
                        dve.wait_ge(fox_exp, n + 1)
                        chain(dve.reciprocal(fox_inv[:, i % 2, :], fox_sum[:, i % 2, :]))
                        for t, cols in enumerate((slice(0, P), slice(P, TRI))):
                            ins = dve.tensor_scalar(fox_p[:, i % 2, cols], fox_p[:, i % 2, cols],
                                                    fox_inv[:, i % 2, t:t + 1], None, ALU.mult)
                        ins.then_inc(fox_prob, 1)
                    if 1 <= i <= HEADS:
                        j, n = i - 1, HEADS * layer + i - 1
                        dve.wait_ge(sb_summed, n + 1)
                        if j >= 2:
                            dve.wait_ge(sb_out, n - 1)
                        dve.tensor_tensor(sb_w[:, j % 2, :], banks[:, 2 + j % 3, 0:TRI], low_min, ALU.min).then_inc(sb_logw, 1)
                    if i >= 2 and i % 2 == 1:
                        pair = (i - 3) // 2
                        dve.wait_ge(sb_high, PAIRS * layer + pair + 1)
                        low(mix_low[:, pair, :], banks[:, 7, 0:SEQ], mix_high[:, pair, :]).then_inc(sb_mix, 1)
                        dve.wait_ge(fox_high, PAIRS * layer + pair + 1)
                        low(mix_low[:, PAIRS + pair, :], banks[:, 6, 0:SEQ], mix_high[:, PAIRS + pair, :]).then_inc(fox_mix, 1)

            def xa_heads(layer):
                for i in range(XH + 2):
                    if i < XH:
                        n = XH * layer + i
                        dve.wait_ge(xa_scored, n + 1)
                        chain(dve.tensor_reduce(x_max[:, i % 2, :], banks[:, i % 2, :].rearrange("p (t m) -> p t m", t=TT),
                                                AX_X, ALU.max))
                        dve.tensor_scalar(x_nmax[:, i % 2, :], x_max[:, i % 2, :], -1.0, None, ALU.mult).then_inc(xa_max, 1)
                        dve.wait_ge(xa_exp, n + 1)
                        chain(dve.reciprocal(x_inv[:, i % 2, :], x_sum[:, i % 2, :]))
                        for t in range(TT):
                            cols = slice(t * SEQ, t * SEQ + SEQ)
                            ins = dve.tensor_scalar(x_p[:, i % 2, cols], x_p[:, i % 2, cols], x_inv[:, i % 2, t:t + 1],
                                                    None, ALU.mult)
                        ins.then_inc(xa_prob, 1)
                    if i >= 2:
                        j, n = i - 2, XH * layer + i - 2
                        dve.wait_ge(xa_high, n + 1)
                        both = slice(2 * j, 2 * j + 2)
                        low(mix_low[:, both, :].rearrange("p a b -> p (a b)"), banks[:, 4 + j % 2, :],
                            mix_high[:, both, :].rearrange("p a b -> p (a b)")).then_inc(xa_mix, 1)

            def product(n):
                dve.wait_ge(silu_ready, n + 1)
                dve.tensor_tensor(hidden[:, :, :], silu_g[:, :, :], banks[:, 4:6, SEQ:2 * SEQ], ALU.mult).then_inc(hidden_ready, 1)

            def turned(n):
                dve.wait_ge(hT_half, n + 1)
                low(hT_low[:, :, :].rearrange("p a b -> p (a b)"), banks[:, 6, :],
                    hT_high[:, :, :].rearrange("p a b -> p (a b)")).then_inc(hT_ready, 1)

            def step(layer, c, r, n, halves=(0, 1, 2)):
                split(layer, c + SPLIT, r)
                product(n)
                for k in halves[1:]:
                    split(layer, c + k + SPLIT, r)
                turned(n)

            def gather(layer, e):
                for i in range(COUNT["ffT"]):
                    dve.wait_ge(gather_high, e * COUNT["ffT"] + (i + 1))
                    for j in range(2):
                        d = 2 * i + j
                        g = G_FF + KT * layer + d
                        ins = low(x_low[:, d, :], banks[:, 7 - i % 2, j * SEQ:(j + 1) * SEQ], x_high[:, d, :], gcols[:, g:g + 1])
                    ins.then_inc(gather_low, 1)

            def find_places(e):
                for t in range(TT):
                    dve.tensor_scalar(place[:, t, :], iota, rank_wide[:, t, bass.ds(e, 1)], chosen_wide[:, t, bass.ds(e, 1)],
                                      ALU.is_equal, ALU.mult).then_inc(place_ready, 1)

            def mixer(layer, c, r, e, y, more):
                n = e * STEPS + layer * STEPS
                if layer:
                    dve.wait_ge(place_ready, e * TT + TT)
                    for t in range(TT):
                        dve.tensor_scalar(place_g[:, t, :], place[:, t, :], gate[:, t, bass.ds(e, 1)], None,
                                          ALU.mult).then_inc(place_g_ready, 1)
                    with more(dve):
                        dve.wait_ge(place_g_ready, e * TT + TT)
                        find_places(e + 1)
                step(layer, c, r, n, (0, 1))
                with dve.Fori(0, (STEPS - 3) // 2) as k:
                    for j in range(2):
                        step(layer, c + 2 + 3 * j, r + k, k * 2 + (n + (1 + j)))
                c = c + 3 * (STEPS - 2) - 1
                step(layer, c, r, n + (STEPS - 2))
                c = c + SPLIT
                split(layer, c + SPLIT, r)
                product(n + (STEPS - 1))
                with more(dve):
                    split(layer, c + 1 + SPLIT, r)
                    split(layer, c + 2 + SPLIT, r)
                turned(n + (STEPS - 1))
                if layer:
                    with more(dve):
                        gather(layer, e + 1)
                dve.wait_ge(mixed, r * RAW + (c + 4 - before_mixer(layer)))
                move(y, banks[:, 2:4, :].rearrange("p a b -> p (a b)")).then_inc(y_dve, 1)
                with more(dve):
                    split(layer, c + 3 + SPLIT, r)
                if layer:
                    for j in range(4):
                        t, hh = j // 2, j % 2
                        dve.wait_ge(sum_full, e * 4 + (j + 1))
                        dst = res[:, t, hh * HALF:(hh + 1) * HALF]
                        dve.tensor_tensor(dst, banks[:, SUM_BANKS[j], :], dst, ALU.add).then_inc(sum_added, 1)

            def route():
                dve.wait_ge(logits_full, 1)
                chain(dve.tensor_copy(logits.rearrange("p a b -> p (a b)"), banks[:, 7, 0:TT * 8]))
                for t in range(TT):
                    chain(dve.max(top[:, t, :], logits[:, t, :]))
                    chain(dve.max_index(topi[:, t, :], top[:, t, :], logits[:, t, :]))
                    chain(dve.tensor_copy(topf[:, t, :], topi[:, t, :]))
                    chain(dve.tensor_scalar(first[:, t, :], iota[:, 0:8], topf[:, t, 0:1], None, ALU.is_equal))
                    chain(dve.tensor_scalar(second[:, t, :], iota[:, 0:8], topf[:, t, 1:2], None, ALU.is_equal))
                    dve.tensor_tensor(chosen[:, t, :], first[:, t, :], second[:, t, :], ALU.add).then_inc(chosen_ready, 1)
                dve.tensor_tensor(gap[:, :], top[:, :, 1], top[:, :, 0], ALU.subtract).then_inc(gap_ready, 1)
                dve.wait_ge(gap_exp, 1)
                chain(dve.tensor_scalar(gate2[:, :], egap[:, :], 1.0, None, ALU.add))
                chain(dve.reciprocal(gate1[:, :], gate2[:, :]))
                chain(dve.tensor_tensor(gate2[:, :], egap[:, :], gate1[:, :], ALU.mult))
                for t in range(TT):
                    chain(dve.tensor_scalar(gate[:, t, :], first[:, t, :], gate1[:, t:t + 1], None, ALU.mult))
                    chain(dve.scalar_tensor_tensor(out=gate[:, t, :], in0=second[:, t, :], scalar=gate2[:, t:t + 1],
                                                   in1=gate[:, t, :], op0=ALU.mult, op1=ALU.add))
                dve.wait_ge(rank_full, 1)
                chain(dve.tensor_copy(rank, view(banks[:, 6, :], 0, TT, 8)))
                dve.tensor_copy(count_i[:, :], banks[:, 6, TT * 8:TT * 8 + 8]).then_inc(rank_ready, 1)

            dve.wait_ge(consts_in, 16)
            for layer in range(DEPTH):
                pre(layer, 0)
                if layer == 0:
                    for c in range(SPLIT):
                        split(0, c)
                    dve.wait_ge(tile_act, 1)
                take_all(layer, "mixT")
                take_all(layer, "f")
                take_all(layer, "u")
                take_all(layer, "fqk")
                decay(layer)
                take_all(layer, "sqk")
                take_all(layer, "v")
                heads(layer)
                take_all(layer, "pool")
                take_all(layer, "out")
                post(layer, 0)
                pre(layer, 1)
                take_all(layer, "memT")
                take_all(layer, "xk")
                take_all(layer, "xv")
                take_all(layer, "xaT")
                take_all(layer, "xq")
                xa_heads(layer)
                take_all(layer, "xo")
                post(layer, 1)
                pre(layer, 2)
                take_all(layer, "ffT")
                c = first_piece(layer) + PIECES
                if layer == 0:
                    mixer(0, c, 0, 0, res[:, 1, :], always)
                else:
                    route()
                    chain(dve.memset(res[:, :, :], 0.0))
                    find_places(0)
                    gather(layer, 0)
                    with dve.Fori(0, EXPERTS // 2) as q:
                        r = q * (2 * MIXER // RAW)
                        mixer(layer, c, r, q * 2, y_sb[:, 1, :], always)
                        mixer(layer, c + MIXER, r, q * 2 + 1, y_sb[:, 1, :], lambda eng: eng.If(q < EXPERTS // 2 - 1))
                post(layer, 2)

        @block.tensor
        def _(pe):
            def bank(n):
                if n >= BANKS:
                    m = n - BANKS
                    pe.wait_ge((tile_act, tile_dve)[MOVER[m]], MOVER[:m + 1].count(MOVER[m]))
                return banks[:, n % BANKS, :]

            def product(dst, stay, move, start, stop):
                pe.matmul(dst, stay[0], move[0], start=start, stop=False, skip_group_check=True)
                pe.matmul(dst, stay[0], move[1], start=False, stop=False, skip_group_check=True)
                return pe.matmul(dst, stay[1], move[0], start=False, stop=stop, skip_group_check=True)

            def parts(pair, *at):
                return [t[at] for t in pair]

            x_parts = (x_high[:, :, :], x_low[:, :, :])
            mix_parts = (mix_high[:, :, :], mix_low[:, :, :])
            every = slice(None)

            def turn_stage(layer, stage, src, ready, count):
                pe.wait_ge(ready, count)
                for i in range(COUNT[stage]):
                    dst = bank(tile(layer, stage, i))
                    for j in range(2):
                        for t in range(TT):
                            ins = pe.transpose(dst[:, j * SEQ + t * P:j * SEQ + (t + 1) * P],
                                               src[:, t, (2 * i + j) * P:(2 * i + j + 1) * P], ident)
                    ins.then_inc(tile_full, 1)

            def pieces(layer, stage, tokens=None):
                for i in range(COUNT[stage]):
                    n = tile(layer, stage, i)
                    if i % 2 == 0:
                        c = first_piece(layer) + PIECE_TILES.index((stage, i))
                        pe.wait_ge(high_ready, c + 1)
                        pe.wait_ge(low_ready, c + 1)
                        wt = weights(c % SPLIT, KT, FFC)
                    dst = bank(n)[:, 0:FFC]
                    cols = slice((i % 2) * P, (i % 2 + 1) * P)
                    for k in range(KT):
                        if tokens is None:
                            stay, move = parts(wt, every, k, cols), parts(x_parts, every, k, every)
                        else:
                            stay, move = parts(tokens, every, k, cols), parts(wt, every, k, every)
                        ins = product(dst, stay, move, k == 0, k == KT - 1)
                    ins.then_inc(tile_full, 1)

            def heads(layer):
                wait_moved(pe, after(layer, "v"))
                pe.wait_ge(decay_ready, layer + 1)
                for i in range(HEADS + 2):
                    if i < HEADS:
                        rows, c, n = slice(HD * (i % 2), HD * (i % 2) + HD), i // 2, HEADS * layer + i
                        fq, fk, sq, sk = (qkT[rows, PAIRS * m + c, :] for m in range(4))
                        b = banks[:, i % 2, :]
                        if i >= 2:
                            pe.wait_ge(fox_masked, n - 1)
                        for t, cols, keys in ((0, slice(0, P), P), (1, slice(P, TRI), SEQ)):
                            pe.matmul(b[:, cols], fq[:, t * P:(t + 1) * P], fk[:, 0:keys], start=(t == 0), stop=False,
                                      skip_group_check=True)
                        for t, cols, keys in ((0, slice(0, P), P), (1, slice(P, TRI), SEQ)):
                            ins = pe.matmul(b[:, cols], decay_q[:, i, t * P:(t + 1) * P], decay_k[:, 0:keys],
                                            start=False, stop=True, skip_group_check=True)
                        ins.then_inc(fox_scored, 1)
                        b = banks[:, 2 + i % 3, :]
                        pe.matmul(b[:, 0:SEQ], sk[:, 0:P], sq, start=True, stop=False, skip_group_check=True)
                        pe.matmul(b[:, SEQ:TRI], sk[:, P:SEQ], sq[:, P:SEQ], start=False, stop=False,
                                  skip_group_check=True).then_inc(sb_scored, 1)
                    if 1 <= i <= HEADS:
                        j, n = i - 1, HEADS * layer + i - 1
                        b = banks[:, 2 + j % 3, :]
                        pe.wait_ge(sb_kept, n + 1)
                        keep = sb_keep[:, j % 2, :]
                        pe.matmul(b[:, 0:SEQ], neg_tri, keep[:, 0:SEQ], start=False, stop=False, skip_group_check=True)
                        pe.matmul(b[:, P:SEQ], neg_ones, keep[:, SEQ:TRI], start=False, stop=False, skip_group_check=True)
                        pe.matmul(b[:, SEQ:TRI], neg_tri, keep[:, SEQ:TRI], start=False, stop=True,
                                  skip_group_check=True).then_inc(sb_summed, 1)
                        pe.wait_ge(fox_prob, n + 1)
                        if j >= 1:
                            pe.wait_ge(fox_pt, n)
                        for m in range(3):
                            ins = pe.transpose(banks[:, 5, m * P:(m + 1) * P], fox_p[:, j % 2, m * P:(m + 1) * P], ident)
                        ins.then_inc(fox_turned, 1)
                    if i >= 2:
                        j, n = i - 2, HEADS * layer + i - 2
                        out_rows, pairs = slice(HD * (j % 2), HD * (j % 2) + HD), PAIRS * layer + j // 2
                        for kind, b, wt, ready, moved, done in ((0, 7, sb_w, sb_wt, sb_mix, sb_out),
                                                                (1, 6, fox_pT, fox_pt, fox_mix, fox_out)):
                            pe.wait_ge(ready, n + 1)
                            if j >= 2 and j % 2 == 0:
                                pe.wait_ge(moved, pairs)
                            o = banks[out_rows, b, :]
                            v0, v1 = (vals[:, t, kind * MIX + j * HD:kind * MIX + (j + 1) * HD] for t in range(TT))
                            pe.matmul(o[:, 0:SEQ], v0, wt[:, j % 2, 0:SEQ], start=True, stop=False, skip_group_check=True)
                            pe.matmul(o[:, P:SEQ], v1, wt[:, j % 2, SEQ:TRI], start=False, stop=True,
                                      skip_group_check=True).then_inc(done, 1)
                pe.wait_ge(sb_mix, PAIRS * (layer + 1))
                pe.wait_ge(fox_mix, PAIRS * (layer + 1))

            def xa_heads(layer):
                wait_moved(pe, after(layer, "xq"))
                for i in range(XH + 2):
                    if i < XH:
                        n = XH * layer + i
                        if i >= 2:
                            pe.wait_ge(xa_exp, n - 1)
                        for t in range(TT):
                            for k in range(2):
                                ins = pe.matmul(banks[:, i % 2, t * SEQ:(t + 1) * SEQ], xqT[:, 2 * i + k, t * P:(t + 1) * P],
                                                xkT[:, 2 * i + k, :], start=(t == 0 and k == 0), stop=(k == 1),
                                                skip_group_check=True)
                        ins.then_inc(xa_scored, 1)
                    if 1 <= i <= XH:
                        j, n = i - 1, XH * layer + i - 1
                        pe.wait_ge(xa_prob, n + 1)
                        if j >= 2:
                            pe.wait_ge(xa_pt, n - 1)
                        for m in range(TT):
                            for t in range(TT):
                                ins = pe.transpose(banks[:, 2 + j % 2, m * SEQ + t * P:m * SEQ + (t + 1) * P],
                                                   x_p[:, j % 2, t * SEQ + m * P:t * SEQ + (m + 1) * P], ident)
                        ins.then_inc(xa_turned, 1)
                    if i >= 2:
                        j, n = i - 2, XH * layer + i - 2
                        pe.wait_ge(xa_pt, n + 1)
                        if j >= 2:
                            pe.wait_ge(xa_mix, n - 1)
                        for d in range(2):
                            for m in range(TT):
                                ins = pe.matmul(banks[:, 4 + j % 2, d * SEQ:(d + 1) * SEQ],
                                                xval[:, m, (2 * j + d) * P:(2 * j + d + 1) * P],
                                                x_pT[:, j % 2, m * SEQ:(m + 1) * SEQ],
                                                start=(m == 0), stop=(m == TT - 1))
                        ins.then_inc(xa_out, 1)
                pe.wait_ge(xa_mix, XH * (layer + 1))

            def gather(e):
                pe.wait_ge(place_ready, e * TT + TT)
                for i in range(COUNT["ffT"]):
                    if i >= 2:
                        pe.wait_ge(gather_low, e * COUNT["ffT"] + (i - 1))
                    for j in range(2):
                        d = 2 * i + j
                        for t in range(TT):
                            ins = pe.matmul(banks[:, 7 - i % 2, j * SEQ:(j + 1) * SEQ], xn[:, t, d * P:(d + 1) * P],
                                            place[:, t, :], start=(t == 0), stop=(t == TT - 1))
                    ins.then_inc(gathered, 1)

            def wait_parts(c):
                pe.wait_ge(high_ready, c + 1)
                pe.wait_ge(low_ready, c + 1)

            def gate_or_up(c, at, half, blocks):
                wait_parts(c)
                wt = weights(at, KT, FFC)
                for b in range(blocks):
                    for k in range(KT):
                        ins = product(banks[:, 4 + b, half * FFC:(half + 1) * FFC],
                                      parts(x_parts, every, k, slice(b * P, (b + 1) * P)), parts(wt, every, k, every),
                                      k == 0, k == KT - 1)
                ins.then_inc(mixed, 1)

            def turn_hidden(n, blocks):
                pe.wait_ge(hidden_ready, n + 1)
                for b in range(blocks):
                    for j in range(FPS):
                        ins = pe.transpose(banks[:, 6, j * SEQ + b * P:j * SEQ + (b + 1) * P],
                                           hidden[:, b, j * P:(j + 1) * P], ident)
                ins.then_inc(hidden_turned, 1)

            def down(c, at, n, blocks, begin=False):
                wait_parts(c)
                pe.wait_ge(hT_ready, n + 1)
                wt = weights(at, FPS, D)
                for b in range(blocks):
                    for hh in range(2):
                        for j in range(FPS):
                            ins = product(banks[:, 2 * b + hh, :],
                                          parts((hT_high[:, :, :], hT_low[:, :, :]), every, j, slice(b * P, (b + 1) * P)),
                                          parts(wt, every, j, slice(hh * HALF, (hh + 1) * HALF)),
                                          begin and j == 0, True)
                ins.then_inc(mixed, 1)

            def mixer(c, n, blocks, first, last):
                gate_or_up(c, 0, 0, blocks)
                gate_or_up(c + 1, 1, 1, blocks)
                first()
                turn_hidden(n, blocks)
                gate_or_up(c + 2, 2, 0, blocks)
                gate_or_up(c + 3, 0, 1, blocks)
                down(c + 4, 1, n, blocks, begin=True)
                turn_hidden(n + 1, blocks)
                with pe.Fori(0, STEPS - 2) as i:
                    gate_or_up(i * 3 + (c + 5), 2, 0, blocks)
                    gate_or_up(i * 3 + (c + 6), 0, 1, blocks)
                    down(i * 3 + (c + 7), 1, i + (n + 1), blocks)
                    turn_hidden(i + (n + 2), blocks)
                last()
                down(c + (MIXER - 1), 2, n + (STEPS - 1), blocks)

            def expert(c, e, blocks):
                def turn_places():
                    pe.wait_ge(place_g_ready, e * TT + TT)
                    for m in range(2):
                        for t in range(TT):
                            ins = pe.transpose(banks[:, 7, m * SEQ + t * P:m * SEQ + (t + 1) * P],
                                               place_g[:, t, m * P:(m + 1) * P], ident)
                    ins.then_inc(spread_full, 1)

                def gather_next():
                    with pe.If(e < EXPERTS - 1):
                        pe.wait_ge(spread_ready, e + 1)
                        pe.wait_ge(hT_ready, e * STEPS + 2 * STEPS)
                        gather(e + 1)

                mixer(c, e * STEPS + STEPS, blocks, turn_places, gather_next)
                pe.wait_ge(spread_ready, e + 1)
                pe.wait_ge(y_act, e + 2)
                pe.wait_ge(y_dve, e + 2)
                for j in range(4):
                    t, hh = j // 2, j % 2
                    for m in range(blocks):
                        ins = pe.matmul(banks[:, SUM_BANKS[j], :], spread[:, m, t * P:(t + 1) * P],
                                        y_sb[:, m, hh * HALF:(hh + 1) * HALF], start=(m == 0), stop=(m == blocks - 1))
                    ins.then_inc(sum_full, 1)

            pe.wait_ge(consts_in, 16)
            pe.wait_ge(vectors_in, 5 * 16)
            pe.transpose(bank(0)[:, 0:G_ROWS], grow[0:G_ROWS, :], ident[0:G_ROWS, 0:G_ROWS]).then_inc(tile_full, 1)
            pe.wait_ge(small_in, SMALL_DMAS * 16)
            for layer in range(DEPTH):
                turn_stage(layer, "mixT", xn, xn_ready, TT * (3 * layer + 1))
                wait_moved(pe, after(layer, "mixT"))
                dst = bank(tile(layer, "f"))
                for m, x in enumerate((x_high_f, x_low_f)):
                    for k in range(KT):
                        ins = pe.matmul(dst[0:HEADS, 0:SEQ], w_forget[:, layer, k, :], x[:, k, :],
                                        start=(m == 0 and k == 0), stop=(m == 1 and k == KT - 1))
                ins.then_inc(tile_full, 1)
                pieces(layer, "u")
                pieces(layer, "fqk")
                pieces(layer, "sqk")
                pieces(layer, "v", x_parts)
                heads(layer)
                pe.wait_ge(pool_ready, layer + 1)
                for c in range(COUNT["pool"]):
                    pe.matmul(bank(tile(layer, "pool", c))[:, 0:SEQ], poolw[:, layer, c, :], pool_r[:, c, :],
                              start=True, stop=True).then_inc(tile_full, 1)
                wait_moved(pe, after(layer, "pool"))
                pieces(layer, "out", mix_parts)
                turn_stage(layer, "memT", mem_n, mem_ready, TT * (layer + 1))
                wait_moved(pe, after(layer, "memT"))
                pieces(layer, "xk")
                pieces(layer, "xv", x_parts)
                turn_stage(layer, "xaT", xn, xn_ready, TT * (3 * layer + 2))
                wait_moved(pe, after(layer, "xaT"))
                pieces(layer, "xq")
                xa_heads(layer)
                pieces(layer, "xo", mix_parts)
                turn_stage(layer, "ffT", xn, xn_ready, TT * (3 * layer + 3))
                wait_moved(pe, after(layer, "ffT"))
                c = first_piece(layer) + PIECES
                if layer == 0:
                    mixer(c, 0, 2, lambda: None, lambda: None)
                    pe.wait_ge(y_act, 1)
                    pe.wait_ge(y_dve, 1)
                    continue
                for t in range(TT):
                    for m, x in enumerate((x_high_f, x_low_f)):
                        for k in range(KT):
                            ins = pe.matmul(banks[:, 7, t * 8:t * 8 + 8], x[:, k, t * P:(t + 1) * P], router[:, k, :],
                                            start=(m == 0 and k == 0), stop=(m == 1 and k == KT - 1))
                ins.then_inc(logits_full, 1)
                pe.wait_ge(chosen_ready, TT)
                before, all_rows = strict[:, 0:P], ones[:, 0:P]
                for at, terms in ((0, ((before, 0),)), (8, ((all_rows, 0), (before, 1))),
                                  (16, ((all_rows, 0), (all_rows, 1)))):
                    for m, (mask, t) in enumerate(terms):
                        ins = pe.matmul(banks[:, 6, at:at + 8], mask, chosen[:, t, :],
                                        start=(m == 0), stop=(m == len(terms) - 1))
                ins.then_inc(rank_full, 1)
                pe.wait_ge(rank_ready, 1)
                gather(0)
                pe.wait_ge(gather_low, COUNT["ffT"])
                with pe.Fori(0, EXPERTS) as e:
                    tokens_here = pe.value_load(count_i[0:1, bass.ds(e, 1)], min_val=0, max_val=SEQ)
                    with pe.If(tokens_here < P + 1):
                        expert(e * MIXER + c, e, 1)
                    with pe.Else():
                        expert(e * MIXER + c, e, 2)


_INS = ["x", "mem", "mix_norm_pre", "mix_norm_post", "w_in", "b_forget", "pool_w", "pool_scale", "w_out",
        "xa_norm_pre", "xa_norm_post", "mem_norm", "xa_wq", "xa_wkv", "xa_wo", "ffn_norm_pre", "ffn_norm_post",
        "dense_w_gate", "dense_w_up", "dense_w_down", "router_w", "moe_w_gate", "moe_w_up", "moe_w_down"]


def kernel(**inputs):
    import concourse.bacc as bacc
    from concourse.bass_utils import run_bass_kernel_spmd

    nc = bacc.Bacc("TRN2", target_bir_lowering=False, num_devices=1)
    arrays, aps = {}, {}
    for name in _INS:
        arr = np.ascontiguousarray(inputs[name])
        arrays[f"in_{name}_dram"] = arr
        aps[name] = nc.dram_tensor(f"in_{name}_dram", arr.shape, mybir.dt.from_np(arr.dtype), kind="ExternalInput").ap()
    table = constants()
    arrays["in_constants_dram"] = table
    consts = nc.dram_tensor("in_constants_dram", table.shape, F32, kind="ExternalInput").ap()
    out = nc.dram_tensor("out_0_dram", (1, SEQ, D), F32, kind="ExternalOutput").ap()
    build(nc, aps, out, consts)
    r = run_bass_kernel_spmd(nc, [arrays], core_ids=[0])
    return r.results[0]["out_0_dram"]
```

```python
from contextlib import ExitStack

import numpy as np

import concourse.bass as bass
from concourse import mybir

ALU = mybir.AluOpType
ACT = mybir.ActivationFunctionType
AX_X = mybir.AxisListType.X
F32 = mybir.dt.float32
F32R = mybir.dt.float32r
I32 = mybir.dt.int32
U32 = mybir.dt.uint32

P = 128
D = 1024
SEQ = 256
DEPTH = 2
KT = D // P
TT = SEQ // P
HD = 64
HEADS = 6
MIX = HEADS * HD
PAIRS = HEADS // 2
XH = 4
XHD = D // XH
FF = 2816
FFC = 256
STEPS = FF // FFC
FPS = FFC // P
EXPERTS = 8
WINDOWS = (2, 4, 8, 16)
PAD = WINDOWS[-1]
SMALL_DMAS = 2 + DEPTH * len(WINDOWS)
HALF = 512
BANKS = 8
LOW = -1.0e30
TRI = P + SEQ

RAW = 6
SPLIT = 3
PIECE = KT * FFC
PIECE_DMAS = 2
NORMS = 7
PIECES = 30
MIXER = 3 * STEPS
HALF_BLOCK = P // 2
PAIR_TURNS = 2 * MIXER // RAW

STAGES = [("mixT", 4), ("f", 1), ("u", 2), ("fqk", 6), ("sqk", 6), ("v", 6), ("pool", 2), ("out", 8),
          ("memT", 4), ("xk", 8), ("xv", 8), ("xaT", 4), ("xq", 8), ("xo", 8), ("ffT", 4)]
COUNT = dict(STAGES)
TURNED_BEFORE = {("out", 6): "memT", ("xv", 2): "xaT"}
ORDER = [(name, i) for name, count in STAGES if name not in TURNED_BEFORE.values() for i in range(count)]
for _before, _name in TURNED_BEFORE.items():
    _at = ORDER.index(_before)
    ORDER[_at:_at] = [(_name, i) for i in range(COUNT[_name])]
SPLIT_STAGES = ("mixT", "pool", "memT", "xaT", "ffT")
PIECE_STAGES = ("u", "fqk", "sqk", "v", "out", "xk", "xv", "xq", "xo")
PIECE_TILES = [(name, i) for name in PIECE_STAGES for i in range(0, COUNT[name], 2)]
assert len(PIECE_TILES) == PIECES
PER_LAYER = len(ORDER)


def movers():
    who = [0]
    for _ in range(DEPTH):
        who += [1 if name in SPLIT_STAGES else (i + 1) % 2 for name, i in ORDER]
    return who


MOVER = movers()

C_IDENT, C_TRI, C_NEG, C_ONES = 0, 128, 256, 384
C_STRICT, C_MIN, C_CAUSAL = 640, 1024, 1408
C_IOTA, C_INV, C_EPS, C_TWICE, C_FOLD, C_END = 1792, 2048, 2560, 2561, 2689, 2817

G_MIX, G_XA, G_MEM, G_FF, G_POOL, G_ROWS = 0, 16, 32, 48, 64, 68


GAIN_OF = {"mixT": G_MIX, "xaT": G_XA, "memT": G_MEM, "ffT": G_FF}


def constants():
    c = np.zeros((P, C_END), np.float32)
    i, j = np.arange(P)[:, None], np.arange(P)[None, :]
    c[:, C_IDENT:C_IDENT + P] = i == j
    c[:, C_TRI:C_TRI + P] = -1.0 * (i >= j)
    c[:, C_NEG:C_NEG + P] = -1.0
    c[:, C_ONES:C_ONES + SEQ] = 1.0
    c[:, C_STRICT:C_STRICT + TRI] = 1.0
    for b in (0, SEQ):
        c[:, C_STRICT + b:C_STRICT + b + P] = i < j
        c[:, C_MIN + b:C_MIN + b + P] = np.where(i < j, 0.0, LOW)
        c[:, C_CAUSAL + b:C_CAUSAL + b + P] = np.where(j <= i, 0.0, LOW)
    c[:, C_IOTA:C_IOTA + SEQ] = np.arange(SEQ)
    for g, w in enumerate(WINDOWS):
        col = C_INV + SEQ * (g // 2)
        c[64 * (g % 2):64 * (g % 2) + 64, col:col + SEQ] = 1.0 / np.minimum(np.arange(SEQ) + 1, w)
    c[:, C_EPS] = 1e-6
    c[:, C_TWICE:C_TWICE + P] = i == j % HALF_BLOCK
    c[:, C_FOLD:C_FOLD + P] = i == j + HALF_BLOCK
    return c


def build(nc, a, out, consts_dram):
    with ExitStack() as ctx:
        def sb(name, shape, dt=F32):
            return ctx.enter_context(nc.sbuf_tensor(name, shape, dt))

        def sem(name):
            return ctx.enter_context(nc.semaphore(name))

        banks = ctx.enter_context(nc.psum_tensor("banks", [P, BANKS, HALF], F32))

        raw = sb("raw", [P, RAW, PIECE])
        w_high = sb("w_high", [P, SPLIT, PIECE], F32R)
        w_low = sb("w_low", [P, SPLIT, PIECE], F32R)
        h_res = sb("h_res", [P, TT, D])
        xn = sb("xn", [P, TT, D])
        x_high = sb("x_high", [P, KT, SEQ], F32R)
        x_low = sb("x_low", [P, KT, SEQ], F32R)
        mix_high = sb("mix_high", [P, KT, SEQ], F32R)
        mix_low = sb("mix_low", [P, KT, SEQ], F32R)
        res = sb("res", [P, TT, D])
        cst = sb("cst", [P, C_END])
        phase = sb("phase", [P, 9216])
        hT_high = sb("hT_high", [P, FPS, SEQ], F32R)
        hT_low = sb("hT_low", [P, FPS, SEQ], F32R)
        gcols = sb("gcols", [P, G_ROWS])
        stats = sb("stats", [P, 3, 2 * NORMS * DEPTH])
        small = sb("small", [P, 296])
        count_i = sb("count_i", [P, EXPERTS], I32)
        topi = sb("topi", [P, TT, 8], U32)
        poolw = sb("poolw", [P, DEPTH, 2, P])
        w_forget = sb("w_forget", [P, DEPTH, KT, HEADS])

        ident = cst[:, C_IDENT:C_IDENT + P]
        neg_tri = cst[:, C_TRI:C_TRI + P]
        neg_ones = cst[:, C_NEG:C_NEG + P]
        ones = cst[:, C_ONES:C_ONES + SEQ]
        strict = cst[:, C_STRICT:C_STRICT + TRI]
        low_min = cst[:, C_MIN:C_MIN + TRI]
        causal = cst[:, C_CAUSAL:C_CAUSAL + TRI]
        iota = cst[:, C_IOTA:C_IOTA + SEQ]
        inv_count = cst[:, C_INV:C_INV + 2 * SEQ].rearrange("p (c t) -> p c t", c=2)
        twice = cst[:, C_TWICE:C_TWICE + P]
        fold = cst[:, C_FOLD:C_FOLD + P]
        eps = cst[:, C_EPS:C_EPS + 1]

        def view(t, at, *dims):
            n = int(np.prod(dims))
            flat = t[:, at:at + n]
            if len(dims) == 1:
                return flat
            if len(dims) == 2:
                return flat.rearrange("p (a b) -> p a b", a=dims[0])
            return flat.rearrange("p (a b c) -> p a b c", a=dims[0], b=dims[1])

        def plain(t):
            return t.bitcast(F32)

        x_high_f, x_low_f = plain(x_high[:, :, :]), plain(x_low[:, :, :])

        qkT = view(phase, 0, 12, SEQ)
        vals = view(phase, 3072, TT, 2 * MIX)
        fox_p = view(phase, 4608, 2, TRI)
        fox_pT = view(phase, 5376, 2, TRI)
        sb_l = view(phase, 6144, 2, TRI)
        sb_keep = view(phase, 6912, 2, TRI)
        sb_w = view(phase, 7680, 2, TRI)
        forget = view(phase, 8448, 3, SEQ)
        mem_n = view(phase, 0, TT, D)
        xkT = view(phase, 0, KT, SEQ)
        xval = view(phase, 2048, TT, D)
        xqT = view(phase, 4096, KT, SEQ)
        x_p = view(phase, 6144, 2, TT * SEQ)
        x_pT = view(phase, 7168, 2, TT * SEQ)
        y_sb = view(phase, 0, 2, D)
        silu_g = view(phase, 2048, 2, FFC)
        hidden = view(phase, 2560, 2, FFC)
        place = view(phase, 3072, TT, SEQ)
        place_g = view(phase, 3584, TT, SEQ)
        spread = view(phase, 4096, 2, SEQ)
        low_rows = view(phase, 4608, 2, FFC)
        gpost = phase[:, 8192:9216]
        grow = phase[:, 0:P]
        flat_xn = xn[:, :, :].rearrange("p t d -> p (t d)")
        decay_q = view(flat_xn, 0, HEADS, SEQ)
        decay_k = flat_xn[:, HEADS * SEQ:(HEADS + 1) * SEQ]
        flat_res = res[:, :, :].rearrange("p t d -> p (t d)")
        u_pad = view(flat_res, 0, 2, PAD + SEQ)
        run_a = flat_res[:, 544:816]
        run_b = flat_res[:, 816:1088]
        pool_r = view(flat_res, 1088, 2, SEQ)

        fox_nmax = view(small, 0, 2, 2)
        fox_sum = view(small, 4, 2, 2)
        fox_inv = view(small, 8, 2, 2)
        x_nmax = view(small, 12, 2, 2)
        x_sum = view(small, 16, 2, 2)
        x_inv = view(small, 20, 2, 2)
        x_max = view(small, 24, 2, 2)
        bias_f = view(small, 28, DEPTH)
        logits = view(small, 32, TT, 8)
        top = view(small, 48, TT, 8)
        topf = view(small, 64, TT, 8)
        first = view(small, 80, TT, 8)
        second = view(small, 96, TT, 8)
        chosen = view(small, 112, TT, 8)
        gate = view(small, 144, TT, 8)
        rank = view(small, 160, TT, 8)
        gap = view(small, 192, TT)
        egap = view(small, 194, TT)
        gate1 = view(small, 196, TT)
        gate2 = view(small, 198, TT)
        router = view(small, 208, KT, 8)
        fox_max = view(small, 200, 2, 2)
        halves = view(small, 272, 8)
        neg_halves = view(small, 280, 8)
        half_more = view(small, 288, 8)

        consts_in = sem("consts_in")
        x_in = sem("x_in")
        mem_in = sem("mem_in")
        vectors_in = sem("vectors_in")
        forget_in = sem("forget_in")
        small_in = sem("small_in")
        gpost_in = sem("gpost_in")
        raw_in = [sem(f"raw_in{s}") for s in range(RAW)]
        high_ready = sem("high_ready")
        low_ready = sem("low_ready")
        act_step = sem("act_step")
        dve_step = sem("dve_step")
        pool_step = sem("pool_step")
        tile_full = sem("tile_full")
        tile_high = sem("tile_high")
        tile_act = sem("tile_act")
        tile_dve = sem("tile_dve")
        squared = sem("squared")
        rms_ready = sem("rms_ready")
        mem_ready = sem("mem_ready")
        gained = sem("gained")
        xn_ready = sem("xn_ready")
        h_ready = sem("h_ready")
        forget_log = sem("forget_log")
        decay_set = sem("decay_set")
        decay_ready = sem("decay_ready")
        pool_ready = sem("pool_ready")
        fox_scored, fox_masked, fox_exp, fox_prob, fox_turned, fox_pt, fox_out, fox_high, fox_mix = (
            sem(f"fox_{n}") for n in ("scored", "masked", "exp", "prob", "turned", "pt", "out", "high", "mix"))
        sb_scored, sb_soft, sb_kept, sb_summed, sb_logw, sb_wt, sb_out, sb_high, sb_mix = (
            sem(f"sb_{n}") for n in ("scored", "soft", "kept", "summed", "logw", "wt", "out", "high", "mix"))
        xa_scored, xa_max, xa_exp, xa_prob, xa_turned, xa_pt, xa_out, xa_high, xa_mix = (
            sem(f"xa_{n}") for n in ("scored", "max", "exp", "prob", "turned", "pt", "out", "high", "mix"))
        mixed = sem("mixed")
        silu_ready = sem("silu_ready")
        hidden_ready = sem("hidden_ready")
        hidden_turned = sem("hidden_turned")
        hT_half, hT_ready = sem("hT_half"), sem("hT_ready")
        rows_out = sem("rows_out")
        gate_whole, up_whole = sem("gate_whole"), sem("up_whole")
        place_single = sem("place_single")
        x_masked, x_stacked, h_stacked = sem("x_masked"), sem("x_stacked"), sem("h_stacked")
        y_act, y_dve = sem("y_act"), sem("y_dve")
        logits_full = sem("logits_full")
        gap_ready, gap_exp = sem("gap_ready"), sem("gap_exp")
        chosen_ready = sem("chosen_ready")
        rank_full, rank_ready = sem("rank_full"), sem("rank_ready")
        place_ready, place_g_ready = sem("place_ready"), sem("place_g_ready")
        gathered, gather_high, gather_low = sem("gathered"), sem("gather_high"), sem("gather_low")
        spread_full, spread_ready = sem("spread_full"), sem("spread_ready")
        sum_full, sum_added = sem("sum_full"), sem("sum_added")
        out_done = sem("out_done")

        def tile(layer, stage, i=0):
            return 1 + PER_LAYER * layer + ORDER.index((stage, i))

        def after(layer, stage):
            return tile(layer, stage, COUNT[stage] - 1) + 1

        def wait_moved(eng, n):
            for who, moved in enumerate((tile_act, tile_dve)):
                count = MOVER[:n].count(who)
                if count:
                    eng.wait_ge(moved, count)

        def highs_before(n):
            names = [None] + DEPTH * [name for name, _ in ORDER]
            return sum(name in SPLIT_STAGES for name in names[:n])

        def first_piece(layer):
            return layer * (PIECES + MIXER)

        def before_mixer(layer):
            return PIECES * (layer + 1)

        def wait_used(eng, layer, c, r):
            start = first_piece(layer)
            p = c - start - SPLIT
            if p < 0:
                if layer:
                    eng.wait_ge(mixed, layer * MIXER + p + 1)
                return
            if p < PIECES:
                stage, i = PIECE_TILES[p]
                eng.wait_ge(tile_full, tile(layer, stage, i + 1) + 1)
            if p >= PIECES or not isinstance(r, int) or r:
                eng.wait_ge(mixed, r * RAW + (c - SPLIT - before_mixer(layer) + 1))

        def weights(at, *dims):
            return view(w_high[:, at, :], 0, *dims), view(w_low[:, at, :], 0, *dims)

        def norm(layer, j):
            return NORMS * layer + (j + 1 if j else 0)

        def split_tile(layer, stage, i):
            src = banks[:, tile(layer, stage, i) % BANKS, :]
            if stage == "pool":
                g, d = G_POOL + 2 * layer + i, 2 * PAIRS + i
                return [(mix_high[:, d, :], src[:, 0:SEQ], gcols[:, g:g + 1], mix_low[:, d, :])]
            parts = []
            for j in range(2):
                d = 2 * i + j
                g = GAIN_OF[stage] + KT * layer + d
                high, low = (mix_high, mix_low) if stage == "xaT" else (x_high, x_low)
                parts.append((high[:, d, :], src[:, j * SEQ:(j + 1) * SEQ], gcols[:, g:g + 1], low[:, d, :]))
            return parts

        def plain_tile(move, layer, stage, i):
            src = banks[:, tile(layer, stage, i) % BANKS, 0:SEQ]
            cols = slice(i // 2 * FFC, (i // 2 + 1) * FFC)
            if stage == "f":
                return move(forget[0:HEADS, 0, :], src[0:HEADS, :])
            if stage == "u":
                return move(u_pad[:, i, PAD:], src)
            if stage in ("fqk", "sqk"):
                return move(qkT[:, (0 if stage == "fqk" else 2 * PAIRS) + i, :], src, HD ** -0.5 if i < PAIRS else 1.0)
            if stage == "xk":
                return move(xkT[:, i, :], src)
            if stage == "xq":
                return move(xqT[:, i, :], src, XHD ** -0.5)
            dst = {"v": vals, "xv": xval, "out": res, "xo": res}[stage]
            return move(dst[:, i % 2, cols], src)

        def pick(eng, blocks, do):
            if isinstance(blocks, int):
                return do(blocks)
            with eng.If(blocks):
                do(1)
            with eng.Else():
                do(2)

        def of_tokens(eng, e):
            return eng.value_load(count_i[0:1, bass.ds(e, 1)], min_val=0, max_val=SEQ) < P + 1

        def first_blocks(eng):
            eng.wait_ge(rank_ready, 1)
            return of_tokens(eng, 0)

        def halves_of_output(dst, blocks):
            if blocks == 1:
                return [(dst[:, 0, j * HALF:(j + 1) * HALF], banks[:, j, :]) for j in range(2)]
            return [(dst[:, j, :], banks[:, 2 * j:2 * j + 2, :].rearrange("p a b -> p (a b)")) for j in range(2)]

        turned_bank = view(banks[:, 6, :], 0, FPS, SEQ)

        def w(name, layer):
            return a[name][layer].rearrange("(k p) n -> p k n", p=P)

        block = ctx.enter_context(nc.Block())

        @block.sync
        def _(sp):
            sp.dma_start(h_res[:, :, :], a["x"][0].rearrange("(t p) d -> p t d", p=P)).then_inc(x_in, 16)
            sp.dma_start(cst[:, :], consts_dram).then_inc(consts_in, 16)
            for i, name in enumerate(("mix_norm_pre", "xa_norm_pre", "mem_norm", "ffn_norm_pre")):
                sp.dma_start(grow[16 * i:16 * i + 16, :],
                             a[name].rearrange("l (k p) -> (l k) p", p=P)).then_inc(vectors_in, 16)
            sp.dma_start(grow[G_POOL:G_ROWS, :],
                         a["pool_scale"].rearrange("l (k p) -> (l k) p", p=P)).then_inc(vectors_in, 16)

            def load_gpost(layer, q):
                if q == 0:
                    sp.wait_ge(sb_mix, PAIRS * (layer + 1))
                    sp.wait_ge(fox_mix, PAIRS * (layer + 1))
                else:
                    sp.wait_ge(h_ready, TT * (3 * layer + q))
                name = ("mix_norm_post", "xa_norm_post", "ffn_norm_post")[q]
                sp.dma_start(gpost, a[name][layer:layer + 1, :].to_broadcast([P, D])).then_inc(gpost_in, 16)

            def load(c, r, parts):
                if c >= RAW:
                    sp.wait_ge(low_ready, r * RAW + (c - RAW + 1))
                for dst, src in parts:
                    sp.dma_start(dst, src).then_inc(raw_in[c % RAW], 16)

            def columns(c, src):
                dst = view(raw[:, c % RAW, :], 0, KT, FFC)
                half = KT // 2
                return [(dst[:, k:k + half, :], src[:, k:k + half, :]) for k in (0, half)]

            def unit(layer, p):
                c = first_piece(layer) + p
                stage, i = PIECE_TILES[p]
                at = i // 2 * FFC
                name, at = {"u": ("w_in", 6 * MIX + HEADS), "fqk": ("w_in", 3 * MIX + at), "sqk": ("w_in", at),
                            "v": ("w_in", 2 * MIX + at), "out": ("w_out", at), "xk": ("xa_wkv", at),
                            "xv": ("xa_wkv", D + at), "xq": ("xa_wq", at), "xo": ("xa_wo", at)}[stage]
                if stage != "v" or i == 0:
                    return load(c, 0, columns(c, w(name, layer)[:, :, at:at + FFC]))
                if i == 4:
                    return load(c, 0, columns(c, w(name, layer)[:, :, 5 * MIX + P:6 * MIX]))
                dst = view(raw[:, c % RAW, :], 0, KT, FFC)
                load(c, 0, [(dst[:, :, 0:P], w(name, layer)[:, :, at:at + P]),
                            (dst[:, :, P:FFC], w(name, layer)[:, :, 5 * MIX:5 * MIX + P])])

            def gate_up(ws, c, r, at):
                for j in range(2):
                    load(c + j, r, columns(c + j, ws[j].rearrange("(k p) n -> p k n", p=P)[:, :, bass.ds(at, FFC)]))

            def down(ws, c, r, at):
                dst = view(raw[:, c % RAW, :], 0, FPS, D)
                src = ws[2][bass.ds(at, FFC), :].rearrange("(t p) n -> p t n", p=P)
                load(c, r, [(dst[:, t, :], src[:, t, :]) for t in range(FPS)])

            def mixer(ws, c, r, following):
                with sp.Fori(0, (STEPS - 1) // 2) as n:
                    for j in range(2):
                        gate_up(ws, c + 2 + 3 * j, r + n, n * (2 * FFC) + (j + 1) * FFC)
                        down(ws, c + 4 + 3 * j, r + n, n * (2 * FFC) + j * FFC)
                c = c + MIXER - 1
                if following:
                    gate_up(following, c, r, 0)
                    c = c + 2
                down(ws, c, r, (STEPS - 1) * FFC)

            def of_expert(e):
                return [a[m][0][bass.ds(e, 1)].rearrange("a d f -> (a d) f")
                        for m in ("moe_w_gate", "moe_w_up", "moe_w_down")]

            for layer in range(DEPTH):
                for p in range(PIECES):
                    if p == 14:
                        load_gpost(layer, 0)
                        sp.dma_start(mem_n[:, :, :], a["mem"][0].rearrange("(t p) d -> p t d", p=P)).then_inc(mem_in, 16)
                    if p == 26:
                        load_gpost(layer, 1)
                    unit(layer, p)
                c = first_piece(layer) + PIECES
                if layer == 0:
                    dense = [a[m][0] for m in ("dense_w_gate", "dense_w_up", "dense_w_down")]
                    gate_up(dense, c, 0, 0)
                    mixer(dense, c, 0, None)
                else:
                    gate_up(of_expert(0), c, 0, 0)
                    with sp.Fori(0, EXPERTS // 2 - 1) as q:
                        for j in range(2):
                            mixer(of_expert(q * 2 + j), c + MIXER * j, q * PAIR_TURNS, of_expert(q * 2 + (j + 1)))
                    for j in range(2):
                        e = EXPERTS - 2 + j
                        mixer(of_expert(e), c + MIXER * j, (EXPERTS // 2 - 1) * PAIR_TURNS,
                              of_expert(e + 1) if j == 0 else None)
                load_gpost(layer, 2)
            sp.wait_ge(out_done, TT * 16)

        @block.gpsimd
        def _(pool):
            steps = [0]

            def chain(ins):
                steps[0] += 1
                ins.then_inc(pool_step, 1)
                pool.wait_ge(pool_step, steps[0])

            with nc.allow_non_contiguous_dma(reason="small strided weights"):
                pool.dma_start(w_forget[:, :, :, :].rearrange("p l k h -> p (l k) h"),
                               a["w_in"].rearrange("l (k p) n -> p (l k) n", p=P)[:, :, 6 * MIX:6 * MIX + HEADS]
                               ).then_inc(forget_in, 16)
                pool.dma_start(bias_f[0:HEADS, :], a["b_forget"].rearrange("l h -> h l")).then_inc(small_in, 16)
                pool.dma_start(router[:, :, :], a["router_w"][0].rearrange("(k p) e -> p k e", p=P)).then_inc(small_in, 16)
            chain(pool.memset(poolw[:, :, :, :], 0.0))
            for layer in range(DEPTH):
                for g in range(len(WINDOWS)):
                    r0 = 64 * (g % 2)
                    pool.dma_start(poolw[r0:r0 + 64, layer, g // 2, r0:r0 + 64],
                                   a["pool_w"][layer, g]).then_inc(small_in, 16)
            pool.wait_ge(consts_in, 16)
            for layer in range(DEPTH):
                wait_moved(pool, after(layer, "mixT"))
                chain(pool.memset(flat_xn[:, 0:(HEADS + 1) * SEQ], 0.0))
                for h in range(HEADS):
                    chain(pool.tensor_scalar(decay_q[32:32 + HEADS, h, :], ones[32:32 + HEADS, :],
                                             ident[32:32 + HEADS, 32 + h:33 + h], None, ALU.mult))
                pool.memset(decay_k[0:HEADS, :], 1.0).then_inc(decay_set, 1)
                pool.wait_ge(decay_set, layer + 1)
                chain(pool.memset(u_pad[:, :, 0:PAD], 0.0))
                wait_moved(pool, after(layer, "u"))
                for c in range(2):
                    u = u_pad[:, c, :]
                    end = PAD + SEQ

                    def wider(dst, src, shift):
                        lo = 2 * shift - 1
                        chain(pool.tensor_tensor(dst[:, lo:end], src[:, lo:end], src[:, lo - shift:end - shift], ALU.add))

                    wider(run_a, u, 1)
                    wider(run_b, run_a, 2)
                    if c == 1:
                        wider(run_a, run_b, 4)
                        wider(run_b, run_a, 8)
                    for half, src in enumerate((run_a, run_b)):
                        rows = slice(64 * half, 64 * half + 64)
                        chain(pool.tensor_tensor(pool_r[rows, c, :], src[rows, PAD:end], inv_count[rows, c, :], ALU.mult))
                        ins = pool.tensor_tensor(pool_r[rows, c, :], pool_r[rows, c, :], u[rows, PAD:end], ALU.subtract)
                        chain(ins)
                pool.engine_nop().then_inc(pool_ready, 1)

        @block.scalar
        def _(act):
            steps = [0]

            def chain(ins):
                steps[0] += 1
                ins.then_inc(act_step, 1)
                act.wait_ge(act_step, steps[0])

            def move(out_, in_, scale=1.0):
                return act.activation(out_, in_, ACT.Copy, scale=scale)

            def split(layer, c, r=0):
                wait_used(act, layer, c, r)
                act.wait_ge(raw_in[c % RAW], (r + c // RAW + 1) * (16 * PIECE_DMAS))
                move(w_high[:, c % SPLIT, :], raw[:, c % RAW, :]).then_inc(high_ready, 1)

            def rms(n, src, arrived):
                for t in range(TT):
                    arrived(t)
                    act.activation(xn[:, t, :], src[:, t, :], ACT.Square,
                                   accum_out=stats[:, 0, 2 * n + t:2 * n + t + 1]).then_inc(squared, 1)
                act.wait_ge(squared, TT * (n + 1))
                if n == 0:
                    act.wait_ge(consts_in, 16)
                pair = slice(2 * n, 2 * n + 2)
                chain(act.activation(stats[:, 1, pair], stats[:, 0, pair], ACT.Ln, bias=eps, scale=1.0 / D))
                act.activation(stats[:, 2, pair], stats[:, 1, pair], ACT.Exp, scale=-0.5).then_inc(rms_ready, 1)

            def pre(layer, q):
                def arrived(t):
                    if layer == 0 and q == 0:
                        act.wait_ge(x_in, 16)
                    else:
                        act.wait_ge(h_ready, TT * (3 * layer + q - 1) + t + 1)
                rms(norm(layer, 2 * q), h_res, arrived)

            def post(layer, q):
                def arrived(t):
                    if q < 2:
                        wait_moved(act, after(layer, ("out", "xo")[q]))
                    elif layer == 0:
                        act.wait_ge(y_act, 1)
                        act.wait_ge(y_dve, 1)
                    else:
                        act.wait_ge(sum_added, 1 + 4 * EXPERTS)
                rms(norm(layer, 2 * q + 1), res, arrived)

            def take(layer, stage, i):
                n = tile(layer, stage, i)
                if stage in SPLIT_STAGES:
                    act.wait_ge(tile_full, n + 1)
                    for dst, src, gain, _ in split_tile(layer, stage, i):
                        ins = move(dst, src, gain)
                    ins.then_inc(tile_high, 1)
                elif MOVER[n] == 0:
                    act.wait_ge(tile_full, n + 1)
                    plain_tile(move, layer, stage, i).then_inc(tile_act, 1)

            def memory(layer):
                rms(norm(layer, 0) + 1, mem_n, lambda t: act.wait_ge(mem_in, 16 * (layer + 1)))

            def take_all(layer, stage, start=0, stop=BANKS, last_split=True):
                for i in range(start, min(stop, COUNT[stage])):
                    if (stage, i) in TURNED_BEFORE:
                        take_all(layer, TURNED_BEFORE[stage, i])
                    take(layer, stage, i)
                    if (stage, i) == ("out", 3):
                        memory(layer)
                    if stage in PIECE_STAGES and i % 2 == 1 and (i < COUNT[stage] - 1 or last_split):
                        split_behind(layer, stage, i - 1)

            def split_behind(layer, stage, i=None):
                i = COUNT[stage] - 2 if i is None else i
                split(layer, first_piece(layer) + PIECE_TILES.index((stage, i)) + SPLIT)

            def heads(layer):
                for i in range(HEADS + 2):
                    if i < HEADS:
                        n = HEADS * layer + i
                        act.wait_ge(sb_scored, n + 1)
                        z = banks[:, 2 + i % 3, 0:TRI]
                        chain(act.activation(sb_l[:, i % 2, :], z, ACT.Abs))
                        chain(act.activation(sb_l[:, i % 2, :], sb_l[:, i % 2, :], ACT.Exp, scale=-1.0))
                        act.activation(sb_l[:, i % 2, :], sb_l[:, i % 2, :], ACT.Ln, bias=1.0).then_inc(sb_soft, 1)
                        act.wait_ge(fox_masked, n + 1)
                        for t, cols in enumerate((slice(0, P), slice(P, TRI))):
                            ins = act.activation(fox_p[:, i % 2, cols], fox_p[:, i % 2, cols], ACT.Exp,
                                                 bias=fox_nmax[:, i % 2, t:t + 1], accum_out=fox_sum[:, i % 2, t:t + 1])
                        ins.then_inc(fox_exp, 1)
                    if 1 <= i <= HEADS:
                        j, n = i - 1, HEADS * layer + i - 1
                        act.wait_ge(sb_logw, n + 1)
                        act.activation(sb_w[:, j % 2, :], sb_w[:, j % 2, :], ACT.Exp).then_inc(sb_wt, 1)
                        act.wait_ge(fox_turned, n + 1)
                        move(fox_pT[:, j % 2, :], banks[:, 5, 0:TRI]).then_inc(fox_pt, 1)
                    if i >= 2 and i % 2 == 1:
                        pair = (i - 3) // 2
                        act.wait_ge(sb_out, HEADS * layer + 2 * pair + 2)
                        move(mix_high[:, pair, :], banks[:, 7, 0:SEQ]).then_inc(sb_high, 1)
                        act.wait_ge(fox_out, HEADS * layer + 2 * pair + 2)
                        move(mix_high[:, PAIRS + pair, :], banks[:, 6, 0:SEQ]).then_inc(fox_high, 1)

            def xa_heads(layer):
                for i in range(XH + 2):
                    if i < XH:
                        n = XH * layer + i
                        act.wait_ge(xa_max, n + 1)
                        if i >= 2:
                            act.wait_ge(xa_turned, n - 1)
                        for t in range(TT):
                            cols = slice(t * SEQ, t * SEQ + SEQ)
                            ins = act.activation(x_p[:, i % 2, cols], banks[:, i % 2, cols], ACT.Exp,
                                                 bias=x_nmax[:, i % 2, t:t + 1], accum_out=x_sum[:, i % 2, t:t + 1])
                        ins.then_inc(xa_exp, 1)
                    if 1 <= i <= XH:
                        j, n = i - 1, XH * layer + i - 1
                        act.wait_ge(xa_turned, n + 1)
                        move(x_pT[:, j % 2, :], banks[:, 2 + j % 2, :]).then_inc(xa_pt, 1)
                    if i >= 2:
                        j, n = i - 2, XH * layer + i - 2
                        act.wait_ge(xa_out, n + 1)
                        move(mix_high[:, 2 * j:2 * j + 2, :].rearrange("p a b -> p (a b)"),
                             banks[:, 4 + j % 2, :]).then_inc(xa_high, 1)

            def turned(n, blocks):
                act.wait_ge(hidden_turned, n + 1)
                move(hT_high[:, :, 0:blocks * P], turned_bank[:, :, 0:blocks * P]).then_inc(hT_half, 1)

            def take_rows(layer, c, r, j, blocks):
                act.wait_ge(mixed, r * RAW + (c + 1 + j - before_mixer(layer)))
                move(low_rows[:, j, :], banks[:, 4 + j, (blocks - 1) * FFC:blocks * FFC]).then_inc(rows_out, 1)

            def silu(n, layer, blocks):
                if layer:
                    act.wait_ge(gate_whole, n - (STEPS - 1))
                act.activation(silu_g.rearrange("p b f -> p (b f)")[:, 0:blocks * FFC], banks[:, 4, 0:blocks * FFC],
                               ACT.Silu).then_inc(silu_ready, 1)

            def step(layer, c, r, n, blocks, ahead=(0, 1, 2), y=None, y_blocks=None, between=None):
                for j in range(2):
                    if layer:
                        pick(act, blocks, lambda b: take_rows(layer, c, r, j, b))
                    if j == 0:
                        split(layer, c + SPLIT, r)
                pick(act, blocks, lambda b: silu(n, layer, b))
                if 1 in ahead:
                    split(layer, c + 1 + SPLIT, r)
                if y is not None:
                    pick(act, y_blocks, lambda b: take_output(layer, c + 2, r, y, b))
                pick(act, blocks, lambda b: turned(n, b))
                if between:
                    between()
                if 2 in ahead:
                    split(layer, c + 2 + SPLIT, r)

            def take_output(layer, c, r, y, blocks):
                act.wait_ge(mixed, r * RAW + (c + 1 - before_mixer(layer)))
                move(*halves_of_output(y, blocks)[0]).then_inc(y_act, 1)

            def gather(layer, e, into, blocks):
                for i in range(KT // 2):
                    act.wait_ge(gathered, e * (KT // 2) + (i + 1))
                    for j in range(2):
                        d = 2 * i + j
                        g = G_FF + KT * layer + d
                        ins = move(into[:, d, 0:blocks * P], banks[:, 7 - i % 2, j * SEQ:j * SEQ + blocks * P],
                                   gcols[:, g:g + 1])
                    ins.then_inc(gather_high, 1)

            def mixer(layer, c, r, e, y, into, last):
                n = e * STEPS + layer * STEPS
                own = of_tokens(act, e) if layer else 2
                following = of_tokens(act, e + 1) if layer and not last else None

                def places():
                    act.wait_ge(spread_full, e + 1)
                    move(spread[:, :, :].rearrange("p a b -> p (a b)"), banks[:, 7, :]).then_inc(spread_ready, 1)

                def steps(blocks):
                    step(layer, c + 2, r, n + 1, blocks, between=places if layer else None)
                    if layer and not last:
                        pick(act, following, lambda b: gather(layer, e + 1, into, b))
                    with act.Fori(0, (STEPS - 3) // 2) as k:
                        for j in range(2):
                            step(layer, c + 5 + 3 * j, r + k, k * 2 + (n + (2 + j)), blocks)
                    step(layer, c + MIXER - 4, r, n + (STEPS - 1), blocks, (0,) if last and layer else (0, 1, 2))

                pick(act, own, steps)
                if not last:
                    step(layer, c + MIXER - 1, r, n + STEPS, following, y=y, y_blocks=own)
                    return
                act.preload_act_table_set("natural_log_exp_and_others")
                pick(act, own, lambda b: take_output(layer, c + MIXER - 1, r, y, b))

            act.preload_act_table_set("natural_log_exp_and_others")
            for layer in range(DEPTH):
                pre(layer, 0)
                if layer:
                    split(layer - 1, first_piece(layer) - 1 + SPLIT)
                if layer == 0:
                    act.wait_ge(tile_full, 1)
                    move(gcols[:, :], banks[:, 0, 0:G_ROWS]).then_inc(tile_act, 1)
                    act.wait_ge(tile_act, 1)
                take_all(layer, "mixT")
                if layer == 0:
                    for c in range(SPLIT):
                        split(0, c)
                take_all(layer, "f")
                take_all(layer, "u")
                wait_moved(act, after(layer, "f"))
                act.wait_ge(small_in, SMALL_DMAS * 16)
                fl = forget[0:HEADS, 0, :]
                fa = forget[0:HEADS, 1, :]
                chain(act.activation(fa, fl, ACT.Abs, bias=bias_f[0:HEADS, layer:layer + 1]))
                chain(act.activation(fa, fa, ACT.Exp, scale=-1.0))
                act.activation(fa, fa, ACT.Ln, bias=1.0).then_inc(forget_log, 1)
                take_all(layer, "fqk")
                take_all(layer, "sqk")
                take_all(layer, "v")
                heads(layer)
                take_all(layer, "pool")
                take_all(layer, "out", last_split=False)
                post(layer, 0)
                split_behind(layer, "out")
                take_all(layer, "xk", 0, 2)
                pre(layer, 1)
                take_all(layer, "xk", 2)
                take_all(layer, "xv")
                take_all(layer, "xq")
                xa_heads(layer)
                take_all(layer, "xo", last_split=False)
                post(layer, 1)
                split_behind(layer, "xo")
                pre(layer, 2)
                take_all(layer, "ffT")
                c = first_piece(layer) + PIECES
                if layer == 0:
                    step(0, c, 0, 0, 2, (0, 1))
                    mixer(0, c, 0, 0, res, None, True)
                else:
                    act.wait_ge(gap_ready, 1)
                    act.activation(egap[:, :], gap[:, :], ACT.Exp).then_inc(gap_exp, 1)
                    own = first_blocks(act)
                    pick(act, own, lambda b: gather(layer, 0, x_high, b))
                    step(layer, c, 0, STEPS, own, (0, 1))

                    def pair(q, last):
                        for j, into in enumerate((mix_high, x_high)):
                            mixer(layer, c + MIXER * j, q * PAIR_TURNS, q * 2 + j, y_sb, into, last and j == 1)

                    with act.Fori(0, EXPERTS // 2 - 1) as q:
                        pair(q, False)
                    pair(EXPERTS // 2 - 1, True)
                post(layer, 2)
            for t in range(TT):
                act.wait_ge(h_ready, TT * (3 * DEPTH - 1) + t + 1)
                act.dma_start(out[0, t * P:(t + 1) * P, :], h_res[:, t, :]).then_inc(out_done, 16)
            act.wait_ge(out_done, TT * 16)

        @block.vector
        def _(dve):
            steps = [0]

            def chain(ins):
                steps[0] += 1
                ins.then_inc(dve_step, 1)
                dve.wait_ge(dve_step, steps[0])

            def inv_rms(n, t):
                return stats[:, 2, 2 * n + t:2 * n + t + 1]

            def pre(layer, q):
                n = norm(layer, 2 * q)
                dve.wait_ge(rms_ready, n + 1)
                for t in range(TT):
                    dve.tensor_scalar(xn[:, t, :], h_res[:, t, :], inv_rms(n, t), None, ALU.mult).then_inc(xn_ready, 1)

            def post(layer, q):
                n, p = norm(layer, 2 * q + 1), 3 * layer + q
                dve.wait_ge(gpost_in, 16 * (p + 1))
                for t in range(TT):
                    dve.wait_ge(squared, TT * n + t + 1)
                    dve.tensor_tensor(res[:, t, :], res[:, t, :], gpost, ALU.mult).then_inc(gained, 1)
                dve.wait_ge(gained, TT * (p + 1))
                dve.wait_ge(rms_ready, n + 1)
                for t in range(TT):
                    dve.scalar_tensor_tensor(out=h_res[:, t, :], in0=res[:, t, :], scalar=inv_rms(n, t),
                                             in1=h_res[:, t, :], op0=ALU.mult, op1=ALU.add).then_inc(h_ready, 1)

            def move(out_, in_, scale=1.0):
                return dve.tensor_scalar(out_, in_, scale, None, ALU.mult)

            def low(out_, in_, high, gain=None):
                if gain is None:
                    return dve.tensor_tensor(out_, in_, plain(high), ALU.subtract)
                return dve.scalar_tensor_tensor(out=out_, in0=in_, scalar=gain, in1=plain(high), op0=ALU.mult,
                                                op1=ALU.subtract)

            def split(layer, c, r=0):
                dve.wait_ge(high_ready, r * RAW + (c + 1))
                low(w_low[:, c % SPLIT, :], raw[:, c % RAW, :], w_high[:, c % SPLIT, :]).then_inc(low_ready, 1)

            def take(layer, stage, i):
                n = tile(layer, stage, i)
                if stage in SPLIT_STAGES:
                    dve.wait_ge(tile_high, highs_before(n) + 1)
                    for high, src, gain, dst in split_tile(layer, stage, i):
                        ins = low(dst, src, high, gain)
                    ins.then_inc(tile_dve, 1)
                elif MOVER[n] == 1:
                    dve.wait_ge(tile_full, n + 1)
                    plain_tile(move, layer, stage, i).then_inc(tile_dve, 1)

            def memory(layer):
                n = norm(layer, 0) + 1
                dve.wait_ge(rms_ready, n + 1)
                for t in range(TT):
                    dve.tensor_scalar(mem_n[:, t, :], mem_n[:, t, :], inv_rms(n, t), None, ALU.mult).then_inc(mem_ready, 1)

            def take_all(layer, stage, start=0, stop=BANKS, last_split=True):
                for i in range(start, min(stop, COUNT[stage])):
                    if (stage, i) in TURNED_BEFORE:
                        take_all(layer, TURNED_BEFORE[stage, i])
                    take(layer, stage, i)
                    if (stage, i) == ("out", 3):
                        memory(layer)
                    if stage in PIECE_STAGES and i % 2 == 1 and (i < COUNT[stage] - 1 or last_split):
                        split_behind(layer, stage, i - 1)

            def split_behind(layer, stage, i=None):
                i = COUNT[stage] - 2 if i is None else i
                split(layer, first_piece(layer) + PIECE_TILES.index((stage, i)) + SPLIT)

            def decay(layer):
                fl, fa, fc = (forget[0:HEADS, r, :] for r in range(3))
                wait_moved(dve, after(layer, "f"))
                dve.wait_ge(small_in, SMALL_DMAS * 16)
                chain(dve.tensor_scalar(fc, fl, bias_f[0:HEADS, layer:layer + 1], 0.0, ALU.add, ALU.min))
                dve.wait_ge(forget_log, layer + 1)
                chain(dve.tensor_tensor(fl, fc, fa, ALU.subtract))
                chain(dve.tensor_tensor_scan(fc, ones[0:HEADS, :], fl, 0.0, ALU.mult, ALU.add))
                dve.wait_ge(decay_set, layer + 1)
                for h in range(HEADS):
                    dve.tensor_scalar(decay_q[0:HEADS, h, :], fc, ident[0:HEADS, h:h + 1], None, ALU.mult)
                dve.tensor_scalar(decay_k[32:32 + HEADS, :], fc, -1.0, None, ALU.mult).then_inc(decay_ready, 1)

            def heads(layer):
                for i in range(HEADS + 2):
                    if i < HEADS:
                        n = HEADS * layer + i
                        dve.wait_ge(fox_scored, n + 1)
                        if i >= 2:
                            dve.wait_ge(fox_turned, n - 1)
                        for t, cols in enumerate((slice(0, P), slice(P, TRI))):
                            chain(dve.tensor_tensor_reduce(out=fox_p[:, i % 2, cols], in0=banks[:, i % 2, cols],
                                                           in1=causal[:, cols], scale=1.0, scalar=3.0 * LOW, op0=ALU.add,
                                                           op1=ALU.max, accum_out=fox_max[:, i % 2, t:t + 1]))
                        dve.tensor_scalar(fox_nmax[:, i % 2, :], fox_max[:, i % 2, :], -1.0, None,
                                          ALU.mult).then_inc(fox_masked, 1)
                        dve.wait_ge(sb_soft, n + 1)
                        chain(dve.scalar_tensor_tensor(out=sb_keep[:, i % 2, :], in0=banks[:, 2 + i % 3, 0:TRI], scalar=0.0,
                                                       in1=sb_l[:, i % 2, :], op0=ALU.max, op1=ALU.add))
                        dve.tensor_tensor(sb_keep[:, i % 2, :], sb_keep[:, i % 2, :], strict, ALU.mult).then_inc(sb_kept, 1)
                        dve.wait_ge(fox_exp, n + 1)
                        chain(dve.reciprocal(fox_inv[:, i % 2, :], fox_sum[:, i % 2, :]))
                        for t, cols in enumerate((slice(0, P), slice(P, TRI))):
                            ins = dve.tensor_scalar(fox_p[:, i % 2, cols], fox_p[:, i % 2, cols],
                                                    fox_inv[:, i % 2, t:t + 1], None, ALU.mult)
                        ins.then_inc(fox_prob, 1)
                    if 1 <= i <= HEADS:
                        j, n = i - 1, HEADS * layer + i - 1
                        dve.wait_ge(sb_summed, n + 1)
                        if j >= 2:
                            dve.wait_ge(sb_out, n - 1)
                        dve.tensor_tensor(sb_w[:, j % 2, :], banks[:, 2 + j % 3, 0:TRI], low_min, ALU.min).then_inc(sb_logw, 1)
                    if i >= 2 and i % 2 == 1:
                        pair = (i - 3) // 2
                        dve.wait_ge(sb_high, PAIRS * layer + pair + 1)
                        low(mix_low[:, pair, :], banks[:, 7, 0:SEQ], mix_high[:, pair, :]).then_inc(sb_mix, 1)
                        dve.wait_ge(fox_high, PAIRS * layer + pair + 1)
                        low(mix_low[:, PAIRS + pair, :], banks[:, 6, 0:SEQ], mix_high[:, PAIRS + pair, :]).then_inc(fox_mix, 1)

            def xa_heads(layer):
                for i in range(XH + 2):
                    if i < XH:
                        n = XH * layer + i
                        dve.wait_ge(xa_scored, n + 1)
                        chain(dve.tensor_reduce(x_max[:, i % 2, :], banks[:, i % 2, :].rearrange("p (t m) -> p t m", t=TT),
                                                AX_X, ALU.max))
                        dve.tensor_scalar(x_nmax[:, i % 2, :], x_max[:, i % 2, :], -1.0, None, ALU.mult).then_inc(xa_max, 1)
                        dve.wait_ge(xa_exp, n + 1)
                        chain(dve.reciprocal(x_inv[:, i % 2, :], x_sum[:, i % 2, :]))
                        for t in range(TT):
                            cols = slice(t * SEQ, t * SEQ + SEQ)
                            ins = dve.tensor_scalar(x_p[:, i % 2, cols], x_p[:, i % 2, cols], x_inv[:, i % 2, t:t + 1],
                                                    None, ALU.mult)
                        ins.then_inc(xa_prob, 1)
                    if i >= 2:
                        j, n = i - 2, XH * layer + i - 2
                        dve.wait_ge(xa_high, n + 1)
                        both = slice(2 * j, 2 * j + 2)
                        low(mix_low[:, both, :].rearrange("p a b -> p (a b)"), banks[:, 4 + j % 2, :],
                            mix_high[:, both, :].rearrange("p a b -> p (a b)")).then_inc(xa_mix, 1)

            def product(layer, c, r, n, blocks):
                dve.wait_ge(silu_ready, n + 1)
                if layer:
                    dve.wait_ge(up_whole, n - (STEPS - 1))
                else:
                    dve.wait_ge(mixed, r * RAW + (c + 2 - before_mixer(layer)))
                cols = slice(0, blocks * FFC)
                dve.tensor_tensor(hidden.rearrange("p b f -> p (b f)")[:, cols],
                                  silu_g.rearrange("p b f -> p (b f)")[:, cols],
                                  banks[:, 5, cols], ALU.mult).then_inc(hidden_ready, 1)

            def turned(layer, n, e, blocks):
                dve.wait_ge(hT_half, n + 1)
                if layer:
                    at = slice(blocks * P - HALF_BLOCK, blocks * P)
                    second = hT_high[:, :, at]
                    dve.scalar_tensor_tensor(out=second, in0=plain(second), scalar=neg_halves[:, bass.ds(e, 1)],
                                             in1=turned_bank[:, :, at], op0=ALU.mult,
                                             op1=ALU.add).then_inc(h_stacked, 1)
                    dve.wait_ge(h_stacked, n - (STEPS - 1))
                low(*(t[:, :, 0:blocks * P] for t in (hT_low, turned_bank, hT_high))).then_inc(hT_ready, 1)

            def step(layer, c, r, n, e, blocks, ahead=(0, 1, 2), y=None, y_blocks=None, between=None):
                split(layer, c + SPLIT, r)
                pick(dve, blocks, lambda b: product(layer, c, r, n, b))
                if between:
                    between()
                if y is not None:
                    pick(dve, y_blocks, lambda b: take_output(layer, c + 2, r, y, b))
                if 1 in ahead:
                    split(layer, c + 1 + SPLIT, r)
                pick(dve, blocks, lambda b: turned(layer, n, e, b))
                if 2 in ahead:
                    split(layer, c + 2 + SPLIT, r)

            def take_output(layer, c, r, y, blocks):
                dve.wait_ge(mixed, r * RAW + (c + 1 - before_mixer(layer)))
                move(*halves_of_output(y, blocks)[1]).then_inc(y_dve, 1)

            def gather(layer, e, high, into, blocks):
                for i in range(KT // 2):
                    dve.wait_ge(gather_high, e * (KT // 2) + (i + 1))
                    at = slice(blocks * P - HALF_BLOCK, blocks * P)
                    second = high[:, 2 * i:2 * i + 2, at]
                    src = view(banks[:, 7 - i % 2, :], 0, 2, SEQ)[:, :, at]
                    dve.tensor_scalar(second, plain(second), halves[:, bass.ds(e, 1)], None, ALU.mult).then_inc(x_masked, 1)
                    dve.wait_ge(x_masked, e * (KT // 2) + (i + 1))
                    for j in range(2):
                        g = G_FF + KT * layer + 2 * i + j
                        low(second[:, j, :], src[:, j, :], second[:, j, :], gcols[:, g:g + 1]).then_inc(x_stacked, 1)
                    dve.wait_ge(x_stacked, e * KT + (2 * i + 2))
                    for j in range(2):
                        d = 2 * i + j
                        g = G_FF + KT * layer + d
                        ins = low(into[:, d, 0:blocks * P], banks[:, 7 - i % 2, j * SEQ:j * SEQ + blocks * P],
                                  high[:, d, 0:blocks * P], gcols[:, g:g + 1])
                    ins.then_inc(gather_low, 1)

            def find_places(e, blocks):
                for t in range(TT):
                    dve.tensor_scalar(place[:, t, :], iota, rank[:, t, bass.ds(e, 1)], chosen[:, t, bass.ds(e, 1)],
                                      ALU.is_equal, ALU.mult).then_inc(place_single, 1)
                    dve.wait_ge(place_single, e * TT + (t + 1))
                    end = blocks * P
                    second = place[:, t, end - HALF_BLOCK:end]
                    dve.scalar_tensor_tensor(out=second, in0=place[:, t, end - P:end - HALF_BLOCK], scalar=halves[:, bass.ds(e, 1)],
                                             in1=second, op0=ALU.mult, op1=ALU.add).then_inc(place_ready, 1)

            def mixer(layer, c, r, e, y, into, last):
                n = e * STEPS + layer * STEPS
                own = of_tokens(dve, e) if layer else 2
                following = of_tokens(dve, e + 1) if layer and not last else None

                def places():
                    dve.wait_ge(place_ready, e * TT + TT)
                    for t in range(TT):
                        dve.tensor_scalar(place_g[:, t, :], place[:, t, :], gate[:, t, bass.ds(e, 1)], None,
                                          ALU.mult).then_inc(place_g_ready, 1)

                    def next_places(blocks):
                        dve.wait_ge(place_g_ready, e * TT + TT)
                        find_places(e + 1, blocks)

                    if not last:
                        pick(dve, following, next_places)

                def steps(blocks):
                    step(layer, c + 2, r, n + 1, e, blocks, between=places if layer else None)
                    if layer and not last:
                        pick(dve, following, lambda b: gather(layer, e + 1, *into, b))
                    with dve.Fori(0, (STEPS - 3) // 2) as k:
                        for j in range(2):
                            step(layer, c + 5 + 3 * j, r + k, k * 2 + (n + (2 + j)), e, blocks)
                    step(layer, c + MIXER - 4, r, n + (STEPS - 1), e, blocks, (0,) if last and layer else (0, 1, 2))

                pick(dve, own, steps)
                if not last:
                    step(layer, c + MIXER - 1, r, n + STEPS, e + 1, following, y=y, y_blocks=own)
                else:
                    pick(dve, own, lambda b: take_output(layer, c + MIXER - 1, r, y, b))
                if layer:
                    for j in range(4):
                        t, hh = j // 2, j % 2
                        dve.wait_ge(sum_full, e * 4 + (j + 1))
                        dst = res[:, t, hh * HALF:(hh + 1) * HALF]
                        dve.tensor_tensor(dst, banks[:, j, :], dst, ALU.add).then_inc(sum_added, 1)

            def route():
                dve.wait_ge(logits_full, 1)
                chain(dve.tensor_copy(logits.rearrange("p a b -> p (a b)"), banks[:, 7, 0:TT * 8]))
                for t in range(TT):
                    chain(dve.max(top[:, t, :], logits[:, t, :]))
                    chain(dve.max_index(topi[:, t, :], top[:, t, :], logits[:, t, :]))
                    chain(dve.tensor_copy(topf[:, t, :], topi[:, t, :]))
                    chain(dve.tensor_scalar(first[:, t, :], iota[:, 0:8], topf[:, t, 0:1], None, ALU.is_equal))
                    chain(dve.tensor_scalar(second[:, t, :], iota[:, 0:8], topf[:, t, 1:2], None, ALU.is_equal))
                    dve.tensor_tensor(chosen[:, t, :], first[:, t, :], second[:, t, :], ALU.add).then_inc(chosen_ready, 1)
                dve.tensor_tensor(gap[:, :], top[:, :, 1], top[:, :, 0], ALU.subtract).then_inc(gap_ready, 1)
                dve.wait_ge(gap_exp, 1)
                chain(dve.tensor_scalar(gate2[:, :], egap[:, :], 1.0, None, ALU.add))
                chain(dve.reciprocal(gate1[:, :], gate2[:, :]))
                chain(dve.tensor_tensor(gate2[:, :], egap[:, :], gate1[:, :], ALU.mult))
                for t in range(TT):
                    chain(dve.tensor_scalar(gate[:, t, :], first[:, t, :], gate1[:, t:t + 1], None, ALU.mult))
                    chain(dve.scalar_tensor_tensor(out=gate[:, t, :], in0=second[:, t, :], scalar=gate2[:, t:t + 1],
                                                   in1=gate[:, t, :], op0=ALU.mult, op1=ALU.add))
                dve.wait_ge(rank_full, 1)
                chain(dve.tensor_copy(rank, view(banks[:, 6, :], 0, TT, 8)))
                counts = banks[:, 6, TT * 8:TT * 8 + 8]
                chain(dve.tensor_scalar(halves, counts, HALF_BLOCK + 0.5, None, ALU.is_lt))
                chain(dve.tensor_scalar(half_more, counts, P + 0.5, None, ALU.is_gt))
                chain(dve.tensor_tensor(halves, halves, half_more, ALU.add))
                chain(dve.tensor_scalar(half_more, counts, P + HALF_BLOCK + 0.5, None, ALU.is_lt))
                chain(dve.tensor_tensor(halves, halves, half_more, ALU.mult))
                chain(dve.tensor_scalar(neg_halves, halves, -1.0, None, ALU.mult))
                dve.tensor_copy(count_i[:, :], counts).then_inc(rank_ready, 1)

            dve.wait_ge(consts_in, 16)
            for layer in range(DEPTH):
                pre(layer, 0)
                if layer:
                    split(layer - 1, first_piece(layer) - 1 + SPLIT)
                if layer == 0:
                    dve.wait_ge(tile_act, 1)
                take_all(layer, "mixT")
                if layer == 0:
                    for c in range(SPLIT):
                        split(0, c)
                take_all(layer, "f")
                take_all(layer, "u")
                take_all(layer, "fqk")
                decay(layer)
                take_all(layer, "sqk")
                take_all(layer, "v")
                heads(layer)
                take_all(layer, "pool")
                take_all(layer, "out", last_split=False)
                post(layer, 0)
                split_behind(layer, "out")
                take_all(layer, "xk", 0, 2)
                pre(layer, 1)
                take_all(layer, "xk", 2)
                take_all(layer, "xv")
                take_all(layer, "xq")
                xa_heads(layer)
                take_all(layer, "xo", last_split=False)
                post(layer, 1)
                pre(layer, 2)
                split_behind(layer, "xo")
                take_all(layer, "ffT")
                c = first_piece(layer) + PIECES
                if layer == 0:
                    step(0, c, 0, 0, 0, 2, (0, 1))
                    mixer(0, c, 0, 0, res, None, True)
                else:
                    route()
                    dve.memset(res[:, :, :], 0.0).then_inc(sum_added, 1)
                    dve.wait_ge(sum_added, 1)
                    own = first_blocks(dve)
                    pick(dve, own, lambda b: find_places(0, b))
                    pick(dve, own, lambda b: gather(layer, 0, x_high, x_low, b))
                    step(layer, c, 0, STEPS, 0, own, (0, 1))

                    def pair(q, last):
                        for j, into in enumerate(((mix_high, mix_low), (x_high, x_low))):
                            mixer(layer, c + MIXER * j, q * PAIR_TURNS, q * 2 + j, y_sb, into, last and j == 1)

                    with dve.Fori(0, EXPERTS // 2 - 1) as q:
                        pair(q, False)
                    pair(EXPERTS // 2 - 1, True)
                post(layer, 2)

        @block.tensor
        def _(pe):
            def bank(n):
                if n >= BANKS:
                    m = n - BANKS
                    pe.wait_ge((tile_act, tile_dve)[MOVER[m]], MOVER[:m + 1].count(MOVER[m]))
                return banks[:, n % BANKS, :]

            def wait_turned(layer, stage, k):
                if k % 2 == 0:
                    pe.wait_ge(tile_dve, MOVER[:tile(layer, stage, k // 2) + 1].count(1))

            def product(dst, stay, move, start, stop, stacked=False):
                if stacked:
                    pe.matmul(dst, stay[0], move[0], start=start, stop=False, skip_group_check=True)
                    return pe.matmul(dst, stay[0], move[1], start=False, stop=stop, skip_group_check=True)
                pe.matmul(dst, stay[0], move[0], start=start, stop=False, skip_group_check=True)
                pe.matmul(dst, stay[0], move[1], start=False, stop=False, skip_group_check=True)
                return pe.matmul(dst, stay[1], move[0], start=False, stop=stop, skip_group_check=True)

            def parts(pair, *at):
                return [t[at] for t in pair]

            x_parts = (x_high[:, :, :], x_low[:, :, :])
            mix_parts = (mix_high[:, :, :], mix_low[:, :, :])
            every = slice(None)

            def turn_stage(layer, stage, src, ready, count):
                pe.wait_ge(ready, count)
                for i in range(COUNT[stage]):
                    dst = bank(tile(layer, stage, i))
                    for j in range(2):
                        for t in range(TT):
                            ins = pe.transpose(dst[:, j * SEQ + t * P:j * SEQ + (t + 1) * P],
                                               src[:, t, (2 * i + j) * P:(2 * i + j + 1) * P], ident)
                    ins.then_inc(tile_full, 1)

            def pieces(layer, stage, tokens=None, x=x_parts):
                for i in range(COUNT[stage]):
                    if (stage, i) == ("out", 6):
                        turn_stage(layer, "memT", mem_n, mem_ready, TT * (layer + 1))
                    if (stage, i) == ("xv", 2):
                        turn_stage(layer, "xaT", xn, xn_ready, TT * (3 * layer + 2))
                    n = tile(layer, stage, i)
                    if i % 2 == 0:
                        c = first_piece(layer) + PIECE_TILES.index((stage, i))
                        pe.wait_ge(high_ready, c + 1)
                        pe.wait_ge(low_ready, c + 1)
                        wt = weights(c % SPLIT, KT, FFC)
                    dst = bank(n)[:, 0:FFC]
                    cols = slice((i % 2) * P, (i % 2 + 1) * P)
                    for k in range(KT):
                        if tokens is None:
                            stay, move = parts(wt, every, k, cols), parts(x, every, k, every)
                        else:
                            stay, move = parts(tokens, every, k, cols), parts(wt, every, k, every)
                        ins = product(dst, stay, move, k == 0, k == KT - 1)
                    ins.then_inc(tile_full, 1)

            def heads(layer):
                wait_moved(pe, after(layer, "v"))
                pe.wait_ge(decay_ready, layer + 1)
                for i in range(HEADS + 2):
                    if i < HEADS:
                        rows, c, n = slice(HD * (i % 2), HD * (i % 2) + HD), i // 2, HEADS * layer + i
                        fq, fk, sq, sk = (qkT[rows, PAIRS * m + c, :] for m in range(4))
                        b = banks[:, i % 2, :]
                        if i >= 2:
                            pe.wait_ge(fox_masked, n - 1)
                        for t, cols, keys in ((0, slice(0, P), P), (1, slice(P, TRI), SEQ)):
                            pe.matmul(b[:, cols], fq[:, t * P:(t + 1) * P], fk[:, 0:keys], start=(t == 0), stop=False,
                                      skip_group_check=True)
                        for t, cols, keys in ((0, slice(0, P), P), (1, slice(P, TRI), SEQ)):
                            ins = pe.matmul(b[:, cols], decay_q[:, i, t * P:(t + 1) * P], decay_k[:, 0:keys],
                                            start=False, stop=True, skip_group_check=True)
                        ins.then_inc(fox_scored, 1)
                        b = banks[:, 2 + i % 3, :]
                        pe.matmul(b[:, 0:SEQ], sk[:, 0:P], sq, start=True, stop=False, skip_group_check=True)
                        pe.matmul(b[:, SEQ:TRI], sk[:, P:SEQ], sq[:, P:SEQ], start=False, stop=False,
                                  skip_group_check=True).then_inc(sb_scored, 1)
                    if 1 <= i <= HEADS:
                        j, n = i - 1, HEADS * layer + i - 1
                        b = banks[:, 2 + j % 3, :]
                        pe.wait_ge(sb_kept, n + 1)
                        keep = sb_keep[:, j % 2, :]
                        pe.matmul(b[:, 0:SEQ], neg_tri, keep[:, 0:SEQ], start=False, stop=False, skip_group_check=True)
                        pe.matmul(b[:, P:SEQ], neg_ones, keep[:, SEQ:TRI], start=False, stop=False, skip_group_check=True)
                        pe.matmul(b[:, SEQ:TRI], neg_tri, keep[:, SEQ:TRI], start=False, stop=True,
                                  skip_group_check=True).then_inc(sb_summed, 1)
                        pe.wait_ge(fox_prob, n + 1)
                        if j >= 1:
                            pe.wait_ge(fox_pt, n)
                        for m in range(3):
                            ins = pe.transpose(banks[:, 5, m * P:(m + 1) * P], fox_p[:, j % 2, m * P:(m + 1) * P], ident)
                        ins.then_inc(fox_turned, 1)
                    if i >= 2:
                        j, n = i - 2, HEADS * layer + i - 2
                        out_rows, pairs = slice(HD * (j % 2), HD * (j % 2) + HD), PAIRS * layer + j // 2
                        for kind, b, wt, ready, moved, done in ((0, 7, sb_w, sb_wt, sb_mix, sb_out),
                                                                (1, 6, fox_pT, fox_pt, fox_mix, fox_out)):
                            pe.wait_ge(ready, n + 1)
                            if j >= 2 and j % 2 == 0:
                                pe.wait_ge(moved, pairs)
                            o = banks[out_rows, b, :]
                            v0, v1 = (vals[:, t, kind * MIX + j * HD:kind * MIX + (j + 1) * HD] for t in range(TT))
                            pe.matmul(o[:, 0:SEQ], v0, wt[:, j % 2, 0:SEQ], start=True, stop=False, skip_group_check=True)
                            pe.matmul(o[:, P:SEQ], v1, wt[:, j % 2, SEQ:TRI], start=False, stop=True,
                                      skip_group_check=True).then_inc(done, 1)
                pe.wait_ge(sb_mix, PAIRS * (layer + 1))
                pe.wait_ge(fox_mix, PAIRS * (layer + 1))

            def xa_heads(layer):
                wait_moved(pe, after(layer, "xq"))
                for i in range(XH + 2):
                    if i < XH:
                        n = XH * layer + i
                        if i >= 2:
                            pe.wait_ge(xa_exp, n - 1)
                        for t in range(TT):
                            for k in range(2):
                                ins = pe.matmul(banks[:, i % 2, t * SEQ:(t + 1) * SEQ], xqT[:, 2 * i + k, t * P:(t + 1) * P],
                                                xkT[:, 2 * i + k, :], start=(t == 0 and k == 0), stop=(k == 1),
                                                skip_group_check=True)
                        ins.then_inc(xa_scored, 1)
                    if 1 <= i <= XH:
                        j, n = i - 1, XH * layer + i - 1
                        pe.wait_ge(xa_prob, n + 1)
                        if j >= 2:
                            pe.wait_ge(xa_pt, n - 1)
                        for m in range(TT):
                            for t in range(TT):
                                ins = pe.transpose(banks[:, 2 + j % 2, m * SEQ + t * P:m * SEQ + (t + 1) * P],
                                                   x_p[:, j % 2, t * SEQ + m * P:t * SEQ + (m + 1) * P], ident)
                        ins.then_inc(xa_turned, 1)
                    if i >= 2:
                        j, n = i - 2, XH * layer + i - 2
                        pe.wait_ge(xa_pt, n + 1)
                        if j >= 2:
                            pe.wait_ge(xa_mix, n - 1)
                        for d in range(2):
                            for m in range(TT):
                                ins = pe.matmul(banks[:, 4 + j % 2, d * SEQ:(d + 1) * SEQ],
                                                xval[:, m, (2 * j + d) * P:(2 * j + d + 1) * P],
                                                x_pT[:, j % 2, m * SEQ:(m + 1) * SEQ],
                                                start=(m == 0), stop=(m == TT - 1))
                        ins.then_inc(xa_out, 1)
                pe.wait_ge(xa_mix, XH * (layer + 1))

            def gather(e, blocks, steps):
                for i in range(KT // 2):
                    if i == 1 and steps is not None:
                        pe.wait_ge(hT_ready, steps)
                    if i >= 2:
                        pe.wait_ge(gather_low, e * (KT // 2) + (i - 1))
                    for j in range(2):
                        d = 2 * i + j
                        for t in range(TT):
                            ins = pe.matmul(banks[:, 7 - i % 2, j * SEQ:j * SEQ + blocks * P], xn[:, t, d * P:(d + 1) * P],
                                            place[:, t, 0:blocks * P], start=(t == 0), stop=(t == TT - 1))
                    ins.then_inc(gathered, 1)

            def wait_parts(c):
                pe.wait_ge(high_ready, c + 1)
                pe.wait_ge(low_ready, c + 1)


            def gate_or_up(c, at, half, lay, x=x_parts, turned=None):
                wait_parts(c)
                wt = weights(at, KT, FFC)
                for b in range(lay[0]):
                    for k in range(KT):
                        if turned is not None and b == 0:
                            wait_turned(turned, "ffT", k)
                        ins = product(banks[:, 4 + half, b * FFC:(b + 1) * FFC],
                                      parts(x, every, k, slice(b * P, (b + 1) * P)), parts(wt, every, k, every),
                                      k == 0, k == KT - 1, lay == (b + 1, True))
                ins.then_inc(mixed, 1)

            def whole(n, half, lay):
                done = (gate_whole, up_whole)[half]
                if not lay[1]:
                    return pe.nop().then_inc(done, 1)
                pe.wait_ge(rows_out, (n - STEPS) * 2 + (half + 1))
                pe.matmul(banks[:, 4 + half, (lay[0] - 1) * FFC:lay[0] * FFC], fold, low_rows[:, half, :], start=False, stop=True,
                          skip_group_check=True).then_inc(done, 1)

            def turn_hidden(n, lay):
                pe.wait_ge(hidden_ready, n + 1)
                for b in range(lay[0]):
                    for j in range(FPS):
                        if lay == (b + 1, True):
                            ins = pe.matmul(banks[:, 6, j * SEQ + b * P:j * SEQ + (b + 1) * P],
                                            hidden[:, b, j * P:(j + 1) * P], twice,
                                            start=True, stop=True)
                            continue
                        ins = pe.transpose(banks[:, 6, j * SEQ + b * P:j * SEQ + (b + 1) * P],
                                           hidden[:, b, j * P:(j + 1) * P], ident)
                ins.then_inc(hidden_turned, 1)

            def down(c, at, n, lay, begin=False):
                wait_parts(c)
                pe.wait_ge(hT_ready, n + 1)
                wt = weights(at, FPS, D)
                for b in range(lay[0]):
                    for hh in range(2):
                        for j in range(FPS):
                            ins = product(banks[:, 2 * b + hh, :],
                                          parts((hT_high[:, :, :], hT_low[:, :, :]), every, j, slice(b * P, (b + 1) * P)),
                                          parts(wt, every, j, slice(hh * HALF, (hh + 1) * HALF)),
                                          begin and j == 0, True, lay == (b + 1, True))
                ins.then_inc(mixed, 1)

            def step(c, at, n, lay, x, routed, begin=False, added=None):
                gate_or_up(c, at, 0, lay, x)
                gate_or_up(c + 1, (at + 1) % SPLIT, 1, lay, x)
                if routed:
                    whole(n, 0, lay)
                    if not lay[1]:
                        whole(n, 1, lay)
                if added is not None:
                    pe.wait_ge(sum_added, added)
                down(c + 2, (at + 2) % SPLIT, n - 1, lay, begin)
                if routed and lay[1]:
                    whole(n, 1, lay)
                turn_hidden(n, lay)

            def later_steps(c, n, lay, x, routed):
                with pe.Fori(0, STEPS - 2) as i:
                    step(i * 3 + (c + 5), 2, i + (n + 2), lay, x, routed)

            def by_tokens(tokens, do):
                with pe.If(tokens < P + 1):
                    with pe.If(tokens < HALF_BLOCK + 1):
                        do((1, True))
                    with pe.Else():
                        do((1, False))
                with pe.Else():
                    with pe.If(tokens < P + HALF_BLOCK + 1):
                        do((2, True))
                    with pe.Else():
                        do((2, False))

            def tokens_of(e):
                return pe.value_load(count_i[0:1, bass.ds(e, 1)], min_val=0, max_val=SEQ)

            def first_step(c, at, n, lay, x, routed):
                gate_or_up(c, at, 0, lay, x, None if routed else 0)
                gate_or_up(c + 1, (at + 1) % SPLIT, 1, lay, x)
                if routed:
                    whole(n, 0, lay)
                    whole(n, 1, lay)

            def expert(c, e, x, next_x, last):
                n = e * STEPS + STEPS
                end = c + (MIXER - 1)
                tokens = tokens_of(e)
                tokens_next = None if last else tokens_of(e + 1)

                def gather_next(blocks):
                    pe.wait_ge(spread_ready, e + 1)
                    pe.wait_ge(place_ready, (e + 1) * TT + TT)
                    gather(e + 1, blocks, n + 2)

                def all_steps(lay):
                    step(c + 2, 2, n + 1, lay, x, True, begin=True, added=e * 4 + 1)
                    pe.wait_ge(place_g_ready, e * TT + TT)
                    for m in range(2):
                        for t in range(TT):
                            ins = pe.transpose(banks[:, 7, m * SEQ + t * P:m * SEQ + (t + 1) * P],
                                               place_g[:, t, m * P:(m + 1) * P], ident)
                    ins.then_inc(spread_full, 1)
                    if not last:
                        with pe.If(tokens_next < P + 1):
                            gather_next(1)
                        with pe.Else():
                            gather_next(2)
                    later_steps(c, n, lay, x, True)

                def first_of_next(lay):
                    pe.wait_ge(gather_low, (e + 2) * (KT // 2))
                    first_step(end, 2, n + STEPS, lay, next_x, True)

                def share(blocks):
                    pe.wait_ge(spread_ready, e + 1)
                    pe.wait_ge(y_act, e + 2)
                    pe.wait_ge(y_dve, e + 2)
                    for j in range(4):
                        t, hh = j // 2, j % 2
                        for m in range(blocks):
                            ins = pe.matmul(banks[:, j, :], spread[:, m, t * P:(t + 1) * P],
                                            y_sb[:, m, hh * HALF:(hh + 1) * HALF], start=(m == 0), stop=(m == blocks - 1))
                        ins.then_inc(sum_full, 1)

                by_tokens(tokens, all_steps)
                if not last:
                    by_tokens(tokens_next, first_of_next)
                by_tokens(tokens, lambda lay: down(end if last else end + 2, 2 if last else 1, n + (STEPS - 1), lay))
                if not last:
                    by_tokens(tokens_next, lambda lay: turn_hidden(n + STEPS, lay))
                with pe.If(tokens < P + 1):
                    share(1)
                with pe.Else():
                    share(2)

            pe.wait_ge(consts_in, 16)
            pe.wait_ge(vectors_in, 5 * 16)
            pe.transpose(bank(0)[:, 0:G_ROWS], grow[0:G_ROWS, :], ident[0:G_ROWS, 0:G_ROWS]).then_inc(tile_full, 1)
            for layer in range(DEPTH):
                turn_stage(layer, "mixT", xn, xn_ready, TT * (3 * layer + 1))
                dst = bank(tile(layer, "f"))
                if layer == 0:
                    pe.wait_ge(forget_in, 16)
                for k in range(KT):
                    wait_turned(layer, "mixT", k)
                    for m, x in enumerate((x_high_f, x_low_f)):
                        ins = pe.matmul(dst[0:HEADS, 0:SEQ], w_forget[:, layer, k, :], x[:, k, :],
                                        start=(m == 0 and k == 0), stop=(m == 1 and k == KT - 1))
                ins.then_inc(tile_full, 1)
                pieces(layer, "u")
                pieces(layer, "fqk")
                pieces(layer, "sqk")
                pieces(layer, "v", x_parts)
                heads(layer)
                pe.wait_ge(pool_ready, layer + 1)
                if layer == 0:
                    pe.wait_ge(small_in, SMALL_DMAS * 16)
                for c in range(COUNT["pool"]):
                    pe.matmul(bank(tile(layer, "pool", c))[:, 0:SEQ], poolw[:, layer, c, :], pool_r[:, c, :],
                              start=True, stop=True).then_inc(tile_full, 1)
                wait_moved(pe, after(layer, "pool"))
                pieces(layer, "out", mix_parts)
                wait_moved(pe, after(layer, "memT"))
                pieces(layer, "xk")
                pieces(layer, "xv", x_parts)
                wait_moved(pe, after(layer, "xaT"))
                pieces(layer, "xq", x=mix_parts)
                xa_heads(layer)
                pieces(layer, "xo", mix_parts)
                turn_stage(layer, "ffT", xn, xn_ready, TT * (3 * layer + 3))
                c = first_piece(layer) + PIECES
                if layer == 0:
                    both = (2, False)
                    first_step(c, 0, 0, both, x_parts, False)
                    turn_hidden(0, both)
                    step(c + 2, 2, 1, both, x_parts, False, begin=True)
                    later_steps(c, 0, both, x_parts, False)
                    down(c + MIXER - 1, 2, STEPS - 1, both)
                    pe.wait_ge(y_act, 1)
                    pe.wait_ge(y_dve, 1)
                    continue
                wait_moved(pe, after(layer, "ffT"))
                for t in range(TT):
                    for m, x in enumerate((x_high_f, x_low_f)):
                        for k in range(KT):
                            ins = pe.matmul(banks[:, 7, t * 8:t * 8 + 8], x[:, k, t * P:(t + 1) * P], router[:, k, :],
                                            start=(m == 0 and k == 0), stop=(m == 1 and k == KT - 1))
                ins.then_inc(logits_full, 1)
                pe.wait_ge(chosen_ready, TT)
                before, all_rows = strict[:, 0:P], ones[:, 0:P]
                for at, terms in ((0, ((before, 0),)), (8, ((all_rows, 0), (before, 1))),
                                  (16, ((all_rows, 0), (all_rows, 1)))):
                    for m, (mask, t) in enumerate(terms):
                        ins = pe.matmul(banks[:, 6, at:at + 8], mask, chosen[:, t, :],
                                        start=(m == 0), stop=(m == len(terms) - 1))
                ins.then_inc(rank_full, 1)
                pe.wait_ge(rank_ready, 1)
                pe.wait_ge(place_ready, TT)
                gather(0, 2, None)
                pe.wait_ge(gather_low, KT // 2)

                def start(lay):
                    first_step(c, 0, STEPS, lay, x_parts, True)
                    turn_hidden(STEPS, lay)

                by_tokens(tokens_of(0), start)

                def pair(q, last):
                    for j, (x, next_x) in enumerate(((x_parts, mix_parts), (mix_parts, x_parts))):
                        expert(q * (2 * MIXER) + (c + MIXER * j), q * 2 + j, x, next_x, last and j == 1)

                with pe.Fori(0, EXPERTS // 2 - 1) as q:
                    pair(q, False)
                pair(EXPERTS // 2 - 1, True)


_INS = ["x", "mem", "mix_norm_pre", "mix_norm_post", "w_in", "b_forget", "pool_w", "pool_scale", "w_out",
        "xa_norm_pre", "xa_norm_post", "mem_norm", "xa_wq", "xa_wkv", "xa_wo", "ffn_norm_pre", "ffn_norm_post",
        "dense_w_gate", "dense_w_up", "dense_w_down", "router_w", "moe_w_gate", "moe_w_up", "moe_w_down"]


def kernel(**inputs):
    import concourse.bacc as bacc
    from concourse.bass_utils import run_bass_kernel_spmd

    nc = bacc.Bacc("TRN2", target_bir_lowering=False, num_devices=1)
    arrays, aps = {}, {}
    for name in _INS:
        arr = np.ascontiguousarray(inputs[name])
        arrays[f"in_{name}_dram"] = arr
        aps[name] = nc.dram_tensor(f"in_{name}_dram", arr.shape, mybir.dt.from_np(arr.dtype), kind="ExternalInput").ap()
    table = constants()
    arrays["in_constants_dram"] = table
    consts = nc.dram_tensor("in_constants_dram", table.shape, F32, kind="ExternalInput").ap()
    out = nc.dram_tensor("out_0_dram", (1, SEQ, D), F32, kind="ExternalOutput").ap()
    build(nc, aps, out, consts)
    r = run_bass_kernel_spmd(nc, [arrays], core_ids=[0])
    return r.results[0]["out_0_dram"]
```
